# Optimizing a Trainium2 kernel written in Bass

```python
import jax, jax.numpy as jnp
from jax import lax
import numpy as np
import math

D_MODEL = 1024
BATCH = 1
SEQ = 512
DEPTH = 1

GLA_HEADS = 4
GLA_KEY_DIM = D_MODEL // 2
GLA_VALUE_DIM = D_MODEL
GLA_HEAD_K = GLA_KEY_DIM // GLA_HEADS
GLA_HEAD_V = GLA_VALUE_DIM // GLA_HEADS
GATE_RANK = 16
GATE_NORMALIZER = 16.0
CHUNK = 64
POOL_GROUPS = 4
POOL_WIDTH = D_MODEL // 2
POOL_GROUP_W = POOL_WIDTH // POOL_GROUPS
POOL_OUT_GROUP_W = D_MODEL // POOL_GROUPS
POOL_WINDOWS = (2, 4, 8, 16)
N_BRANCHES = 2
D_FF = -(-8 * D_MODEL // (3 * 256)) * 256
IN_WIDTH = 2 * GLA_KEY_DIM + 2 * GLA_VALUE_DIM + 2 * GATE_RANK + POOL_WIDTH + N_BRANCHES * D_MODEL
EPS = 1e-6


def rmsnorm(x, g):
    xf = x.astype(jnp.float32)
    y = xf * lax.rsqrt(jnp.mean(xf * xf, axis=-1, keepdims=True) + EPS)
    return (y * g.astype(jnp.float32)).astype(x.dtype)

def gla_chunked(q, k, v, log_a, include_diag):
    bsz, heads, length, dk = q.shape
    dv = v.shape[-1]
    n = length // CHUNK
    q = q.reshape(bsz, heads, n, CHUNK, dk).astype(jnp.float32)
    k = k.reshape(bsz, heads, n, CHUNK, dk).astype(jnp.float32)
    v = v.reshape(bsz, heads, n, CHUNK, dv).astype(jnp.float32)
    b = jnp.cumsum(log_a.reshape(bsz, heads, n, CHUNK, dk).astype(jnp.float32), axis=3)
    b_last = b[:, :, :, -1:, :]
    q_e = q * jnp.exp(b)
    k_e = k * jnp.exp(-b)
    k_d = k * jnp.exp(b_last - b)
    mask = jnp.tril(jnp.ones((CHUNK, CHUNK), dtype=bool), 0 if include_diag else -1)
    scores = jnp.einsum('bhncd,bhnsd->bhncs', q_e, k_e)
    scores = jnp.where(mask, scores, 0.0)
    o_intra = jnp.einsum('bhncs,bhnse->bhnce', scores, v)
    kv = jnp.einsum('bhnsd,bhnse->bhnde', k_d, v)
    decay = jnp.exp(b_last[:, :, :, 0, :])

    def step(state, inp):
        kv_n, dec_n = inp
        return dec_n[..., None] * state + kv_n, state

    s0 = jnp.zeros((bsz, heads, dk, dv), jnp.float32)
    _, s_in = lax.scan(step, s0, (jnp.moveaxis(kv, 2, 0), jnp.moveaxis(decay, 2, 0)))
    s_in = jnp.moveaxis(s_in, 0, 2)
    o_inter = jnp.einsum('bhncd,bhnde->bhnce', q_e, s_in)
    return (o_intra + o_inter).reshape(bsz, heads, length, dv)

def to_heads(t, heads):
    bsz, length, width = t.shape
    return t.reshape(bsz, length, heads, width // heads).transpose(0, 2, 1, 3)

def multiscale_pool(u):
    bsz, length, _ = u.shape
    ug = u.reshape(bsz, length, POOL_GROUPS, POOL_GROUP_W).astype(jnp.float32)
    cs = jnp.concatenate([jnp.zeros((bsz, 1, POOL_GROUPS, POOL_GROUP_W), jnp.float32),
                          jnp.cumsum(ug, axis=1)], axis=1)
    pos = jnp.arange(length)[:, None]
    win = jnp.array(POOL_WINDOWS, dtype=jnp.int32)[None, :]
    lo = jnp.clip(pos - win // 2, 0, length)
    hi = jnp.clip(pos + win - win // 2, 0, length)
    gi = jnp.arange(POOL_GROUPS)[None, :]
    window_sum = cs[:, hi, gi] - cs[:, lo, gi]
    count = (hi - lo).astype(jnp.float32)[None, :, :, None]
    return window_sum / count - ug

def first_inputs(seed: int = 0) -> dict:
    key = jax.random.key(seed)
    ks = jax.random.split(key, 16)

    def nrm(k, shape, scale):
        return jax.random.normal(k, shape, jnp.float32) * scale

    return {
        'x': nrm(ks[0], (BATCH, SEQ, D_MODEL), 1.0),
        'norm_mix': 1.0 + nrm(ks[1], (DEPTH, D_MODEL), 0.05),
        'w_in': nrm(ks[2], (DEPTH, D_MODEL, IN_WIDTH), D_MODEL ** -0.5),
        'w_decay_up_fwd': nrm(ks[3], (DEPTH, GATE_RANK, GLA_KEY_DIM), GATE_RANK ** -0.5),
        'b_decay_fwd': nrm(ks[4], (DEPTH, GLA_KEY_DIM), 0.1),
        'w_decay_up_bwd': nrm(ks[5], (DEPTH, GATE_RANK, GLA_KEY_DIM), GATE_RANK ** -0.5),
        'b_decay_bwd': nrm(ks[6], (DEPTH, GLA_KEY_DIM), 0.1),
        'gla_norm': 1.0 + nrm(ks[7], (DEPTH, GLA_VALUE_DIM), 0.05),
        'w_branch_gla': nrm(ks[8], (DEPTH, GLA_VALUE_DIM, D_MODEL), GLA_VALUE_DIM ** -0.5),
        'w_pool_group': nrm(ks[9], (DEPTH, POOL_GROUPS, POOL_GROUP_W, POOL_OUT_GROUP_W), POOL_GROUP_W ** -0.5),
        'pool_scale': 1.0 + nrm(ks[10], (DEPTH, D_MODEL), 0.05),
        'w_out': nrm(ks[11], (DEPTH, D_MODEL, D_MODEL), D_MODEL ** -0.5),
        'norm_ffn': 1.0 + nrm(ks[12], (DEPTH, D_MODEL), 0.05),
        'w_ffn_in': nrm(ks[13], (DEPTH, D_MODEL, 2 * D_FF), D_MODEL ** -0.5),
        'w_ffn_out': nrm(ks[14], (DEPTH, D_FF, D_MODEL), D_FF ** -0.5),
        'norm_final': 1.0 + nrm(ks[15], (D_MODEL,), 0.05),
    }

def first_block(x, norm_mix, w_in, w_decay_up_fwd, b_decay_fwd, w_decay_up_bwd, b_decay_bwd,
              gla_norm, w_branch_gla, w_pool_group, pool_scale, w_out, norm_ffn,
              w_ffn_in, w_ffn_out, norm_final):
    bsz, length, _ = x.shape
    split_sizes = [GLA_KEY_DIM, GLA_KEY_DIM, GLA_VALUE_DIM, GLA_VALUE_DIM, GATE_RANK, GATE_RANK,
                   POOL_WIDTH, D_MODEL, D_MODEL]
    split_points = [int(p) for p in np.cumsum(split_sizes)[:-1]]
    for l in range(DEPTH):
        h = rmsnorm(x, norm_mix[l])
        proj = h @ w_in[l]
        q, k, v, r, lr_f, lr_b, u, g_a, g_b = jnp.split(proj, split_points, axis=-1)

        log_a_f = jax.nn.log_sigmoid((lr_f @ w_decay_up_fwd[l] + b_decay_fwd[l]).astype(jnp.float32)) / GATE_NORMALIZER
        log_a_b = jax.nn.log_sigmoid((lr_b @ w_decay_up_bwd[l] + b_decay_bwd[l]).astype(jnp.float32)) / GATE_NORMALIZER
        qh = to_heads(q, GLA_HEADS) * (GLA_HEAD_K ** -0.5)
        kh = to_heads(k, GLA_HEADS)
        vh = to_heads(v, GLA_HEADS)
        af = to_heads(log_a_f, GLA_HEADS)
        ab = to_heads(log_a_b, GLA_HEADS)
        o_fwd = gla_chunked(qh, kh, vh, af, include_diag=True)
        o_bwd = jnp.flip(gla_chunked(jnp.flip(qh, 2), jnp.flip(kh, 2), jnp.flip(vh, 2), jnp.flip(ab, 2),
                                     include_diag=False), 2)
        o = o_fwd + o_bwd
        o = o * lax.rsqrt(jnp.mean(o * o, axis=-1, keepdims=True) + EPS)
        o = o.transpose(0, 2, 1, 3).reshape(bsz, length, GLA_VALUE_DIM) * gla_norm[l].astype(jnp.float32)
        o = (o * jax.nn.silu(r.astype(jnp.float32))).astype(x.dtype)
        y_a = o @ w_branch_gla[l]

        pooled = multiscale_pool(u)
        y_b = jnp.einsum('blgc,gcd->blgd', pooled, w_pool_group[l]).reshape(bsz, length, D_MODEL)
        y_b = (y_b * pool_scale[l]).astype(x.dtype)

        merged = jax.nn.sigmoid(g_a) * y_a + jax.nn.sigmoid(g_b) * y_b
        x = x + merged @ w_out[l]

        h2 = rmsnorm(x, norm_ffn[l])
        gate, up = jnp.split(h2 @ w_ffn_in[l], 2, axis=-1)
        x = x + (jax.nn.silu(gate) * up) @ w_ffn_out[l]
    return rmsnorm(x, norm_final)


ATTN_HEADS = 8
ATTN_HEAD_DIM = 64
ATTN_WIDTH = ATTN_HEADS * ATTN_HEAD_DIM
DILATED_PATTERNS = ((128, 1), (512, 4), (2048, 16))
ATTN_BLOCK = 128
N_BUCKETS = 32
MAX_DISTANCE = 2048
NEG_INF = -1e30
HGRN_HEADS = 8
HGRN_KEY_DIM = 128
HGRN_VAL_DIM = 128
HGRN_FDIM = HGRN_HEADS * HGRN_KEY_DIM
HGRN_WIDTH = HGRN_HEADS * HGRN_VAL_DIM
HGRN_CHUNK = 64
IN_WIDTH_2 = 4 * ATTN_WIDTH + 2 * HGRN_FDIM + 2 * HGRN_WIDTH + 2 * D_MODEL


def rmsnorm_2(x, g):
    xf = x.astype(jnp.float32)
    y = xf * lax.rsqrt(jnp.mean(xf * xf, axis=-1, keepdims=True) + EPS)
    return (y * g.astype(jnp.float32)).astype(x.dtype)

def t5_bucket(dist):
    max_exact = N_BUCKETS // 2
    n = dist.astype(jnp.float32)
    large = max_exact + (jnp.log(jnp.maximum(n, 1.0) / max_exact)
                         / math.log(MAX_DISTANCE / max_exact)
                         * (N_BUCKETS - max_exact)).astype(jnp.int32)
    large = jnp.minimum(large, N_BUCKETS - 1)
    return jnp.where(dist < max_exact, dist, large)

def dilated_pattern(q, k, v, rel_bias, window, dilation):
    B, S, H, E = q.shape
    L = S // dilation
    span = window // dilation
    nb = -(-L // ATTN_BLOCK)
    Lp = nb * ATTN_BLOCK

    def to_sub(t):
        t = t.reshape(B, L, dilation, H, E).transpose(0, 2, 3, 1, 4)
        return jnp.pad(t, ((0, 0), (0, 0), (0, 0), (0, Lp - L), (0, 0)))

    def kv_blocks(t):
        tp = jnp.pad(to_sub(t), ((0, 0), (0, 0), (0, 0), (ATTN_BLOCK, 0), (0, 0)))
        prev = tp[:, :, :, :Lp].reshape(B, dilation, H, nb, ATTN_BLOCK, E)
        cur = tp[:, :, :, ATTN_BLOCK:].reshape(B, dilation, H, nb, ATTN_BLOCK, E)
        return jnp.concatenate([prev, cur], axis=4)

    qs = to_sub(q).reshape(B, dilation, H, nb, ATTN_BLOCK, E)
    ks, vs = kv_blocks(k), kv_blocks(v)

    qi = jnp.arange(ATTN_BLOCK)[:, None]
    kj = jnp.arange(2 * ATTN_BLOCK)[None, :]
    delta = qi + ATTN_BLOCK - kj
    band = (delta >= 0) & (delta <= span)
    key_pos = jnp.arange(nb)[:, None, None] * ATTN_BLOCK + kj[None] - ATTN_BLOCK
    mask = band[None] & (key_pos >= 0)
    bucket = t5_bucket(jnp.clip(delta, 0, None) * dilation)
    bias = rel_bias.astype(jnp.float32)[bucket].transpose(2, 0, 1)

    s = jnp.einsum('bdhnqe,bdhnke->bdhnqk', qs, ks) * (E ** -0.5) + bias[None, None, :, None]
    s = jnp.where(mask, s, NEG_INF)
    m = jnp.max(s, axis=-1, keepdims=True)
    p = jnp.exp(s - m)
    den = jnp.sum(p, axis=-1, keepdims=True)
    o = jnp.einsum('bdhnqk,bdhnke->bdhnqe', p, vs) / den
    lse = (m + jnp.log(den))[..., 0]

    o = o.reshape(B, dilation, H, Lp, E)[:, :, :, :L].transpose(0, 3, 1, 2, 4).reshape(B, S, H, E)
    lse = lse.reshape(B, dilation, H, Lp)[..., :L].transpose(0, 3, 1, 2).reshape(B, S, H)
    return o, lse

def dilated_attention(q, k, v, rel_bias):
    outs, lses = [], []
    for window, dilation in DILATED_PATTERNS:
        o, lse = dilated_pattern(q, k, v, rel_bias, window, dilation)
        outs.append(o)
        lses.append(lse)
    w = jax.nn.softmax(jnp.stack(lses, 0), axis=0)
    return jnp.einsum('gbsh,gbshe->bshe', w, jnp.stack(outs, 0))

def hgrn2_recurrence(q, f_raw, i, lb):
    B, S, H, DK = q.shape
    DV = i.shape[-1]
    C = HGRN_CHUNK
    nc = S // C
    f = lb + (1.0 - lb) * jax.nn.sigmoid(f_raw)
    g = jnp.log(f)
    k = 1.0 - f

    def chunks(t):
        return t.reshape(B, nc, C, H, t.shape[-1]).transpose(1, 0, 3, 2, 4)

    causal = jnp.tril(jnp.ones((C, C), dtype=bool))

    def step(state, inp):
        qc, kc, vc, gc = inp
        b = jnp.cumsum(gc, axis=2)
        o_inter = jnp.einsum('bhtk,bhkv->bhtv', qc * jnp.exp(b), state)
        diff = b[:, :, :, None, :] - b[:, :, None, :, :]
        decay = jnp.exp(jnp.where(causal[:, :, None], diff, -jnp.inf))
        a = jnp.einsum('bhtk,bhsk,bhtsk->bhts', qc, kc, decay)
        o_intra = jnp.einsum('bhts,bhsv->bhtv', a, vc)
        b_last = b[:, :, -1:, :]
        new_state = (jnp.exp(b_last[:, :, 0, :])[..., None] * state
                     + jnp.einsum('bhsk,bhsv->bhkv', kc * jnp.exp(b_last - b), vc))
        return new_state, o_inter + o_intra

    s0 = jnp.zeros((B, H, DK, DV), jnp.float32)
    _, o = lax.scan(step, s0, (chunks(q), chunks(k), chunks(i), chunks(g)))
    return o.transpose(1, 0, 3, 2, 4).reshape(B, S, H, DV)

def second_inputs(seed: int = 0) -> dict:
    key = jax.random.key(seed)
    ks = jax.random.split(key, 13)
    D = D_MODEL
    nrm = lambda k, shape, fan_in: jax.random.normal(k, shape, jnp.float32) * fan_in ** -0.5
    return {
        "x": jax.random.normal(ks[0], (BATCH, SEQ, D), jnp.float32),
        "c": jax.random.normal(ks[1], (BATCH, D), jnp.float32),
        "w_ada": nrm(ks[2], (DEPTH, D, 3 * D), D),
        "b_ada": 0.02 * jax.random.normal(ks[3], (DEPTH, 3 * D), jnp.float32),
        "norm_g": 1.0 + 0.05 * jax.random.normal(ks[4], (DEPTH, D), jnp.float32),
        "w_in": nrm(ks[5], (DEPTH, D, IN_WIDTH_2), D),
        "hgrn_onorm_g": 1.0 + 0.05 * jax.random.normal(ks[6], (DEPTH, HGRN_VAL_DIM), jnp.float32),
        "w_branch_a": nrm(ks[7], (DEPTH, ATTN_WIDTH, D), ATTN_WIDTH),
        "w_branch_b": nrm(ks[8], (DEPTH, HGRN_WIDTH, D), HGRN_WIDTH),
        "w_out": nrm(ks[9], (DEPTH, D, D), D),
        "rel_bias": 0.5 * jax.random.normal(ks[10], (N_BUCKETS, ATTN_HEADS), jnp.float32),
        "hgrn_lb": 0.5 * jax.random.normal(ks[11], (DEPTH + 1, HGRN_FDIM), jnp.float32),
        "final_g": 1.0 + 0.05 * jax.random.normal(ks[12], (D,), jnp.float32),
    }

def second_block(x, c, w_ada, b_ada, norm_g, w_in, hgrn_onorm_g, w_branch_a, w_branch_b,
              w_out, rel_bias, hgrn_lb, final_g):
    B, S, D = x.shape
    sizes = [ATTN_WIDTH] * 4 + [HGRN_FDIM, HGRN_FDIM, HGRN_WIDTH, HGRN_WIDTH, D_MODEL, D_MODEL]
    cuts = [int(v) for v in np.cumsum(sizes)[:-1]]
    lower_bounds = jnp.cumsum(jax.nn.softmax(hgrn_lb.astype(jnp.float32), axis=0), axis=0)
    for l in range(DEPTH):
        mod = jax.nn.silu(c) @ w_ada[l] + b_ada[l]
        shift, scale, gate = jnp.split(mod, 3, axis=-1)
        h = rmsnorm_2(x, norm_g[l]) * (1.0 + scale[:, None]) + shift[:, None]
        proj = h @ w_in[l]
        q_a, k_a, v_a, z_a, q_b, f_b, i_b, z_b, g_a, g_b = jnp.split(proj, cuts, axis=-1)

        heads_a = lambda t: t.astype(jnp.float32).reshape(B, S, ATTN_HEADS, ATTN_HEAD_DIM)
        o_a = dilated_attention(heads_a(q_a), heads_a(k_a), heads_a(v_a), rel_bias)
        o_a = o_a.reshape(B, S, ATTN_WIDTH).astype(x.dtype) * jax.nn.silu(z_a)

        heads_b = lambda t, e: t.astype(jnp.float32).reshape(B, S, HGRN_HEADS, e)
        lb = lower_bounds[l].reshape(HGRN_HEADS, HGRN_KEY_DIM)
        o_b = hgrn2_recurrence(jax.nn.silu(heads_b(q_b, HGRN_KEY_DIM)), heads_b(f_b, HGRN_KEY_DIM),
                               heads_b(i_b, HGRN_VAL_DIM), lb)
        o_b = rmsnorm_2(o_b, hgrn_onorm_g[l]).reshape(B, S, HGRN_WIDTH).astype(x.dtype) * jax.nn.silu(z_b)

        y = jax.nn.sigmoid(g_a) * (o_a @ w_branch_a[l]) + jax.nn.sigmoid(g_b) * (o_b @ w_branch_b[l])
        x = x + gate[:, None] * (y @ w_out[l])
    return rmsnorm_2(x, final_g)


def setup_inputs(seed=0):
    out = dict(first_inputs(seed))
    for name, value in second_inputs(seed + 1).items():
        if name != "x":
            out[name + "_2"] = value
    return out


def reference(
    x, norm_mix, w_in, w_decay_up_fwd, b_decay_fwd, w_decay_up_bwd, b_decay_bwd, gla_norm,
    w_branch_gla, w_pool_group, pool_scale, w_out, norm_ffn, w_ffn_in, w_ffn_out, norm_final,
    c_2, w_ada_2, b_ada_2, norm_g_2, w_in_2, hgrn_onorm_g_2, w_branch_a_2, w_branch_b_2,
    w_out_2, rel_bias_2, hgrn_lb_2, final_g_2,
):
    x = first_block(
        x, norm_mix, w_in, w_decay_up_fwd, b_decay_fwd, w_decay_up_bwd, b_decay_bwd, gla_norm,
        w_branch_gla, w_pool_group, pool_scale, w_out, norm_ffn, w_ffn_in, w_ffn_out,
        norm_final,
    )
    return second_block(
        x, c_2, w_ada_2, b_ada_2, norm_g_2, w_in_2, hgrn_onorm_g_2, w_branch_a_2, w_branch_b_2,
        w_out_2, rel_bias_2, hgrn_lb_2, final_g_2,
    )


_drawn_inputs = setup_inputs


def setup_inputs(seed=0):
    import zlib

    import numpy as np

    out = dict(_drawn_inputs(seed))
    spreads = {}
    factors = {'b_decay_fwd': 5.754,
     'b_decay_bwd': 5.541,
     'gla_norm': 3.584,
     'b_ada_2': 3.353,
     'norm_g_2': 2.896,
     'hgrn_onorm_g_2': 4.064,
     'hgrn_lb_2': 5.58}
    for name, (base, spread) in spreads.items():
        noise = np.random.default_rng([zlib.crc32(name.encode()), seed]).standard_normal(out[name].shape)
        drawn = base * np.exp(spread * noise) if base else spread * noise
        out[name] = __import__('jax').numpy.asarray(drawn.astype(out[name].dtype))
    for name, factor in factors.items():
        out[name] = (out[name] * factor).astype(out[name].dtype)
    return out
```

```python
import concourse.bass as bass
from concourse import mybir
from contextlib import ExitStack
import numpy as np

P = 128
DM = 1024
L = 512
KT = DM // P
TT = L // P
GLA_HEADS, DK, DV, CHUNK = 4, 128, 256, 64
NCH = L // CHUNK
RANK = 16
POOL_WINDOWS = (2, 4, 8, 16)
NG = len(POOL_WINDOWS)
PAD = 8
D_FF = 2816
FT = D_FF // P
A_HEADS, AE = 8, 64
AW = A_HEADS * AE
H_HEADS = 8
N_BUCKETS, MAX_DISTANCE = 32, 2048
PATTERNS = ((128, 1), (512, 4), (2048, 16))
NEG_INF = -1e30
EPS = 1e-6
LEVELS = 7
BW = 640

C_Q, C_K, C_V, C_R = 0, 512, 1024, 2048
C_LR = 3072
C_U = C_LR + 2 * RANK
C_GA = C_U + 512
C_GB = C_GA + DM
D_QA, D_KA, D_VA, D_ZA = 0, 512, 1024, 1536
D_QB, D_FB, D_IB, D_ZB = 2048, 3072, 4096, 5120
D_GA, D_GB = 6144, 7168

R_NM, R_GN, R_PS, R_NF, R_BF, R_BB, R_NG2, R_ADA = 0, 8, 16, 24, 32, 36, 40, 48
R_LB0, R_LB1, R_NFIN, R_C, R_ON, R_FG = 72, 80, 88, 96, 104, 105

U_LR, U_HEAD, U_C, U_POOL, U_BR, U_OUT = 0, 1, 17, 23, 24, 28
U_FIN, U_FOUT, U_ATT, U_HG, U_G2 = 32, 54, 70, 78, 94
U_BA, U_BB, U_OUT2, U_END = 102, 104, 108, 112


def first_tile(u):
    if u == 0:
        return 0
    if u <= U_POOL:
        return 2 * u - 1
    if u <= U_FOUT:
        return 53 + 2 * (u - U_BR)
    if u <= U_ATT:
        return 113 + (u - U_FOUT)
    if u <= U_BA:
        return 129 + 2 * (u - U_ATT)
    if u == U_BA + 1:
        return 197
    return 201 + 2 * (u - U_BB)


def shape_constants():
    f = np.float32
    ident = np.eye(P, dtype=f)
    s, t = np.arange(P)[:, None], np.arange(P)[None, :]
    masks = [(s // CHUNK == t // CHUNK) & (s <= t), (s // CHUNK == t // CHUNK) & (s > t)]
    for lev in range(LEVELS):
        half = 1 << lev
        masks.append((s // (2 * half) == t // (2 * half)) & (s % (2 * half) < half) & (t % (2 * half) >= half))
    masks.append(s == t)
    masks = np.ascontiguousarray(np.stack(masks, 1).astype(f))
    edge = np.zeros((NG, 2 * PAD), f)
    for g, w in enumerate(POOL_WINDOWS):
        for c in range(PAD):
            for side, pos in ((0, c), (1, L - PAD + c)):
                lo, hi = max(pos - w // 2, 0), min(pos + w - w // 2, L)
                edge[g, side * PAD + c] = 1.0 / (hi - lo)
    dist = np.arange(BW) - (P - 1)
    n = np.maximum(dist, 0).astype(f)
    exact = N_BUCKETS // 2
    large = exact + (np.log(np.maximum(n, f(1)) / f(exact)) / f(np.log(MAX_DISTANCE / exact))
                     * f(N_BUCKETS - exact)).astype(np.int32)
    bucket = np.where(dist < exact, np.maximum(dist, 0), np.minimum(large, N_BUCKETS - 1))
    count = np.zeros(BW, np.int64)
    for window, dil in PATTERNS:
        count += (dist >= 0) & (dist <= window) & (dist % dil == 0)
    hot = np.zeros((N_BUCKETS + 1, BW), f)
    hot[bucket, np.arange(BW)] = count > 0
    hot[N_BUCKETS] = np.where(count > 0, np.log(np.maximum(count, 1)), NEG_INF)
    return {"ident": ident, "masks": masks, "edge": edge, "hot": hot}


def build(nc, inp, out):
    f32, f32r, u8 = mybir.dt.float32, mybir.dt.float32r, mybir.dt.uint8
    ALU, ACT = mybir.AluOpType, mybir.ActivationFunctionType
    ds = bass.ds
    KB = 1024
    BASE = (nc.sbuf_base + 31) // 32 * 32

    def at(name, kb, shape, dt=f32):
        return nc.alloc_sbuf_tensor_at(name, shape, dt, offset=BASE + int(kb * KB))

    raw = at("raw", 0, [P, 2, 16 * P])
    whi = at("whi", 16, [P, 2, 16 * P], f32r)
    wlo = at("wlo", 32, [P, 2, 16 * P], f32r)
    hhi = at("hhi", 48, [P, KT, L], f32r)
    hlo = at("hlo", 64, [P, KT, L], f32r)
    xres = at("xres", 80, [P, KT, L])
    sig_ga = at("sig_ga", 80, [P, KT, L])
    S0 = 96
    ident = at("ident", S0, [P, P])
    ones = at("ones", S0 + .5, [P, P])
    vcol = at("vcol", S0 + 1, [P, P])
    masks = at("masks", S0 + 1.5, [P, LEVELS + 3, P], u8)
    mod = at("mod", S0 + 2.75, [P, 24])
    lbt = at("lbt", S0 + 3, [P, 6, 8])
    small = at("small", S0 + 3.25, [P, 32])
    edge = at("edge", S0 + 3.5, [P, NG, 2 * PAD])
    amax = at("amax", S0 + 3.75, [P, 2, TT])
    aden = at("aden", S0 + 4, [P, 2, TT])
    dec = at("dec", S0 + 4.25, [P, 2, NCH])
    relb = at("relb", S0 + 4.5, [P, A_HEADS])
    tick = at("tick", S0 + 5, [1, 8])
    A0 = 101.5
    eps_col = small[:, 0:1]
    silu_c = small[:, 8:16]
    g2_col = small[:, 16:24]

    xnat = at("xnat", A0 + 16, [P, TT, DM])
    vrow = at("vrow", A0 + 32, [P, P])
    hot = at("hot", A0 + 34, [N_BUCKETS + 1, BW])
    brow = at("brow", A0 + 37, [A_HEADS, BW])
    mask_src = at("mask_src", A0 + 88, [P, LEVELS + 3, P])
    wup = at("wup", A0 + 40, [2 * RANK, 2, L])
    nsq = at("nsq", A0, [P, 2, L])
    nacc = at("nacc", A0 + 4, [P, L])
    nrs = at("nrs", A0 + 6, [P, L])
    nht = at("nht", A0 + 8, [P, 2, L])
    b_all = at("b_all", A0, [P, 8, L])
    o_all = at("o_all", A0 + 16, [P, KT, L])
    lrT = at("lrT", A0 + 44, [2 * RANK, L])
    gq, gk = at("gq", A0 + 32, [P, L]), at("gk", A0 + 34, [P, L])
    lt = at("lt", A0 + 46, [P, 2, 2, L])
    gv = at("gv", A0 + 36, [P, TT, DV])
    gr = at("gr", A0 + 54, [P, 2, L])
    qe, ke = at("qe", A0 + 58, [P, 2, L]), at("ke", A0 + 62, [P, 2, L])
    kd = at("kd", A0 + 66, [P, 2, L])
    ex = at("ex", A0 + 70, [P, 3, L])
    kdT = at("kdT", A0 + 76, [P, 2, TT, P])
    ga_sc = at("ga_sc", A0 + 80, [P, TT, P])
    st = at("st", A0 + 82, [P, 2, NCH - 1, DV])
    rst = at("rst", A0 + 96, [P, L])
    gbm = at("gbm", A0, [P, KT, L])
    phi = at("phi", A0 + 64, [P, NG, L], f32r)
    plo = at("plo", A0 + 72, [P, NG, L], f32r)
    ptmp = at("ptmp", A0 + 58, [P, L + 2 * PAD])
    ptmp2 = at("ptmp2", A0 + 60.5, [P, L + 2 * PAD])
    upad = at("upad", A0 + 40, [P, NG, L + 2 * PAD])
    mhi = at("mhi", A0 + 32, [P, KT, L], f32r)
    mlo = at("mlo", A0 + 80, [P, KT, L], f32r)
    ahi = at("ahi", A0, [P, FT, L], f32r)
    alo = at("alo", A0 + 44, [P, FT, L], f32r)
    fsg = at("fsg", A0 + 88, [P, 2, L])
    faa = at("faa", A0 + 92, [P, 2, L])
    ada = at("ada", A0 + 96, [P, 2, KT, P])
    oa = at("oa", A0, [P, AW // P, L])
    ob = at("ob", A0 + 8, [P, KT, L])
    sga = at("sga", A0 + 24, [P, KT, L])
    sgb = at("sgb", A0 + 40, [P, KT, L])
    aq, ak = at("aq", A0 + 56, [P, L]), at("ak", A0 + 58, [P, L])
    av, az = at("av", A0 + 60, [P, L]), at("az", A0 + 62, [P, L])
    avt = at("avt", A0 + 64, [P, TT, P])
    abias = at("abias", A0 + 66, [P, 2, L])
    apr = at("apr", A0 + 70, [P, 2, TT, L])
    apt = at("apt", A0 + 86, [P, TT, L])
    hq, hf = at("hq", A0 + 56, [P, L]), at("hf", A0 + 58, [P, L])
    hi_, hz = at("hi_", A0 + 60, [P, L]), at("hz", A0 + 62, [P, L])
    hk, hb = at("hk", A0 + 64, [P, L]), at("hb", A0 + 66, [P, L])
    hw = at("hw", A0 + 68, [P, LEVELS, L])
    hqe, hkd = at("hqe", A0 + 82, [P, L]), at("hkd", A0 + 84, [P, L])
    hkT = at("hkT", A0 + 86, [P, TT, P])
    hit = at("hit", A0 + 88, [P, TT, P])
    hsc = at("hsc", A0 + 90, [P, TT, P])
    hst = at("hst", A0 + 92, [P, TT - 1, P])
    hsq, hrs = at("hsq", A0 + 94, [P, L]), at("hrs", A0 + 96, [P, L])
    hrst = at("hrst", A0 + 98, [P, L])
    oahi = at("oahi", A0 + 88, [P, AW // P, L], f32r)
    oalo = at("oalo", A0 + 96, [P, AW // P, L], f32r)
    nhi = at("nhi", A0 + 56, [P, KT, L], f32r)
    nlo = at("nlo", A0 + 72, [P, KT, L], f32r)
    yT = at("yT", A0 + 16, [P, KT, L])
    ynat = at("ynat", A0 + 32, [P, TT, DM])

    x_dram = nc.dram_tensor("x_scratch", (P, KT * L), f32, kind="Internal").ap()
    bias_dram = nc.dram_tensor("bias_scratch", (A_HEADS, BW), f32, kind="Internal").ap()

    ctx = ExitStack()
    with ctx:
        acc = [ctx.enter_context(nc.psum_tensor(f"acc{b}", [P, L], f32)) for b in range(4)]
        M = [ctx.enter_context(nc.psum_tensor(f"mid{b}", [P, L], f32)) for b in range(4)]
        def sem(name):
            return ctx.enter_context(nc.semaphore(name))

        s_acc_free = [sem(f"acc_free{b}") for b in range(4)]
        s_unit_in = [sem(f"unit_in{b}") for b in range(2)]
        s_ada_in = [sem(f"ada_in{b}") for b in range(2)]
        s_a_out = sem("a_out")
        s_a_tr = sem("a_tr")
        s_acc_full = sem("acc_full")
        s_ada_mm = sem("ada_mm")
        s_ada_used = sem("ada_used")
        s_aexp = sem("aexp")
        s_amax = sem("amax")
        s_aprob = sem("aprob")
        s_apt = sem("apt")
        s_apv = sem("apv")
        s_arec = sem("arec")
        s_av_tr = sem("av_tr")
        s_avt = sem("avt")
        s_az_sig = sem("az_sig")
        s_b_ready = sem("b_ready")
        s_bias_in = sem("bias_in")
        s_bias_mm = sem("bias_mm")
        s_bias_out = sem("bias_out")
        s_bias_row = sem("bias_row")
        s_bias_src = sem("bias_src")
        s_csig = sem("csig")
        s_der = sem("der")
        s_edge_in = sem("edge_in")
        s_eps = sem("eps")
        s_f_hi = sem("f_hi")
        s_f_lo = sem("f_lo")
        s_f_sig = sem("f_sig")
        s_gdec = sem("gdec")
        s_gdf = sem("gdf")
        s_gex = sem("gex")
        s_gfin = sem("gfin")
        s_gln = sem("gln")
        s_gmask = sem("gmask")
        s_go = sem("go")
        s_grs = sem("grs")
        s_gsc = sem("gsc")
        s_gsq = sem("gsq")
        s_gst = sem("gst")
        s_gsum = sem("gsum")
        s_gt = sem("gt")
        s_h_b = sem("h_b")
        s_h_cp = sem("h_cp")
        s_h_df = sem("h_df")
        s_h_dl = sem("h_dl")
        s_h_ex = sem("h_ex")
        s_h_fg = sem("h_fg")
        s_h_itr = sem("h_itr")
        s_h_ktr = sem("h_ktr")
        s_h_kv = sem("h_kv")
        s_h_lex = sem("h_lex")
        s_h_ln = sem("h_ln")
        s_h_mask = sem("h_mask")
        s_h_o = sem("h_o")
        s_h_op = sem("h_op")
        s_h_out = sem("h_out")
        s_h_rl = sem("h_rl")
        s_h_rs = sem("h_rs")
        s_h_score = sem("h_score")
        s_h_sq = sem("h_sq")
        s_h_st = sem("h_st")
        s_h_sum = sem("h_sum")
        s_h_t = sem("h_t")
        s_h_w = sem("h_w")
        s_h_wl = sem("h_wl")
        s_hq_sig = sem("hq_sig")
        s_hrst = sem("hrst")
        s_hz_sig = sem("hz_sig")
        s_id_in = sem("id_in")
        s_kdT = sem("kdT")
        s_kd_tr = sem("kd_tr")
        s_kv = sem("kv")
        s_la = sem("la")
        s_la_abs = sem("la_abs")
        s_la_exp = sem("la_exp")
        s_la_ln = sem("la_ln")
        s_la_min = sem("la_min")
        s_lb = sem("lb")
        s_lb_d = sem("lb_d")
        s_lb_e = sem("lb_e")
        s_lb_m = sem("lb_m")
        s_lb_s = sem("lb_s")
        s_logit = sem("logit")
        s_mask_src = sem("mask_src")
        s_masks = sem("masks")
        s_merge2 = sem("merge2")
        s_merge_hi = sem("merge_hi")
        s_merge_lo = sem("merge_lo")
        s_merged = sem("merged")
        s_mod = sem("mod")
        s_n_hi = sem("n_hi")
        s_n_lo = sem("n_lo")
        s_norm_acc = sem("norm_acc")
        s_norm_hi = sem("norm_hi")
        s_norm_ht = sem("norm_ht")
        s_norm_ln = sem("norm_ln")
        s_norm_lo = sem("norm_lo")
        s_norm_rs = sem("norm_rs")
        s_norm_sq = sem("norm_sq")
        s_norm_sum = sem("norm_sum")
        s_o_hi = sem("o_hi")
        s_o_lo = sem("o_lo")
        s_oa_hi = sem("oa_hi")
        s_oa_lo = sem("oa_lo")
        s_ob_hi = sem("ob_hi")
        s_ob_lo = sem("ob_lo")
        s_ones = sem("ones")
        s_p_hi = sem("p_hi")
        s_p_lo = sem("p_lo")
        s_pool_add = sem("pool_add")
        s_pool_edge = sem("pool_edge")
        s_pool_mid = sem("pool_mid")
        s_pool_side = sem("pool_side")
        s_pooled = sem("pooled")
        s_r_sig = sem("r_sig")
        s_rows_in = sem("rows_in")
        s_rst = sem("rst")
        s_score = sem("score")
        s_silu_c = sem("silu_c")
        s_unit_hi = sem("unit_hi")
        s_unit_lo = sem("unit_lo")
        s_up_mm = sem("up_mm")
        s_upad_zero = sem("upad_zero")
        s_vcol = sem("vcol")
        s_vcol_mm = sem("vcol_mm")
        s_vrow_zero = sem("vrow_zero")
        s_wup_in = sem("wup_in")
        s_xT = sem("xT")
        s_xT_out = sem("xT_out")
        s_x_back = sem("x_back")
        s_x_in = sem("x_in")
        s_x_mid = sem("x_mid")
        s_x_out = sem("x_out")
        s_yT = sem("yT")
        s_y_nat = sem("y_nat")
        s_y_out = sem("y_out")
        s_y_tr = sem("y_tr")

        def later(n):
            return not isinstance(n, int) or n > 0

        def norm_base(n, what):
            if what in ("ht", "hi", "lo"):
                return KT * {0: 0, 1: 1, 3: 2}[n]
            return n * {"sq": KT, "acc": KT - 1}.get(what, 1)

        def cols(t, k):
            return t[:, ds(k, 1), :].rearrange("p a n -> p (a n)") if not isinstance(k, int) else t[:, k, :]

        def col(t, k):
            return t[:, ds(k, 1)] if not isinstance(k, int) else t[:, k:k + 1]

        def vtile(v):
            return v.rearrange("p (a b) -> p a b", b=P)

        def used_before(u, lin=None):
            if isinstance(u, int) and lin is None:
                return first_tile(u - 1) if u >= 2 else 0
            return lin

        def split_hi(act, u, slot, n=16 * P, lin=None):
            act.wait_ge(s_unit_in[slot], unit_count(u, slot))
            if later(used_before(u, lin)):
                act.wait_ge(s_acc_full, used_before(u, lin))
            nc.scalar.activation(whi[:, slot, 0:n], raw[:, slot, 0:n], ACT.Copy).then_inc(s_unit_hi, 1)

        def split_lo(pool, u, slot, n=16 * P):
            pool.wait_ge(s_unit_hi, u + 1)
            nc.gpsimd.tensor_tensor(wlo[:, slot, 0:n], raw[:, slot, 0:n], whi[:, slot, 0:n].bitcast(f32),
                                    ALU.subtract).then_inc(s_unit_lo, 1)

        def unit_count(u, slot):
            return 32 * (u // 2 + 1) if isinstance(u, int) else (u - slot) * 16 + 32

        def raw_free(sp, u):
            if later(u - 1):
                sp.wait_ge(s_unit_lo, u - 1)

        def pe_tile(bank, slot, j, nk, ncol, xh, xl):
            for k in range(nk):
                h = whi[:, slot, k * ncol + j * P:k * ncol + (j + 1) * P]
                lo = wlo[:, slot, k * ncol + j * P:k * ncol + (j + 1) * P]
                nc.tensor.matmul(acc[bank][:, :], h, xh[:, k, :], start=(k == 0), stop=False)
                nc.tensor.matmul(acc[bank][:, :], h, xl[:, k, :], start=False, stop=False)
                last = nc.tensor.matmul(acc[bank][:, :], lo, xh[:, k, :], start=False, stop=(k == nk - 1))
            last.then_inc(s_acc_full, 1)

        def pe_values(bank, slot, pair, xh, xl):
            for t in (2 * pair, 2 * pair + 1):
                o = acc[bank][:, (t % 2) * DV:(t % 2 + 1) * DV]
                for k in range(KT):
                    h, lo = whi[:, slot, k * DV:(k + 1) * DV], wlo[:, slot, k * DV:(k + 1) * DV]
                    xs = slice(t * P, (t + 1) * P)
                    nc.tensor.matmul(o, xh[:, k, xs], h, start=(k == 0), stop=False)
                    nc.tensor.matmul(o, xh[:, k, xs], lo, start=False, stop=False)
                    last = nc.tensor.matmul(o, xl[:, k, xs], h, start=False, stop=(k == KT - 1))
            last.then_inc(s_acc_full, 1)

        def kview(w, c0, n):
            return w.rearrange("(k p) n -> p k n", p=P)[:, :, ds(c0, n)]

        def rawk(slot, nk, ncol, j0=0, n=None):
            return raw[:, slot, 0:nk * ncol].rearrange("p (k n) -> p k n", k=nk)[:, :, j0:j0 + (n or ncol)]

        def TL(u0, c, per=0, i=0):
            t = first_tile(u0) + c
            if isinstance(i, int):
                t += per * i
                return t % 4, t + 1, t // 4
            return t % 4, t + 1 + i * per, t // 4 + i * (per // 4)

        def moved(u0, c, per=0, i=0):
            b, _, free = TL(u0, c, per, i)
            return s_acc_free[b], free + 1

        w_in, w_in2 = inp["w_in"][0], inp["w_in_2"][0]
        w_fin, w_fout = inp["w_ffn_in"][0], inp["w_ffn_out"][0]

        block = ctx.enter_context(nc.Block())

        @block.sync
        def _(sp):
            def load(u, slot, src, nk=KT, ncol=2 * P):
                raw_free(sp, u)
                sp.dma_start(rawk(slot, nk, ncol), src).then_inc(s_unit_in[slot], 32)

            def load_pair(u, slot, w, ca, cb):
                raw_free(sp, u)
                sp.dma_start(rawk(slot, KT, 2 * P, 0, P), kview(w, ca, P)).then_inc(s_unit_in[slot], 16)
                sp.dma_start(rawk(slot, KT, 2 * P, P, P), kview(w, cb, P)).then_inc(s_unit_in[slot], 16)

            xn = inp["x"][0].rearrange("(t p) d -> t p d", p=P)
            sp.dma_start(ident[:, :], inp["ident"]).then_inc(s_id_in, 16)
            for t in range(TT):
                sp.dma_start(xnat[:, t, :], xn[t]).then_inc(s_x_in, 16)
            load(0, 0, kview(w_in, C_LR, P), ncol=P)

            def head_loads(h, u):
                load_pair(u, 1, w_in, C_Q + h * DK, C_K + h * DK)
                load(u + 1, 0, kview(w_in, C_GA + h * 256, 256))
                load(u + 2, 1, kview(w_in, C_V + h * DV, 256))
                load(u + 3, 0, kview(w_in, C_R + h * DV, 256))

            sp.wait_ge(s_bias_row, 2)
            sp.dma_start(bias_dram, brow[:, :]).then_inc(s_bias_out, 16)
            head_loads(0, 1)
            sp.wait_ge(s_norm_ht, KT)
            sp.dma_start(x_dram, xres[:, :, :].rearrange("p k t -> p (k t)")).then_inc(s_x_out, 16)
            with sp.Fori(1, GLA_HEADS) as h:
                head_loads(h, h * 4 + 1)
            for j in range(2):
                load(U_C + j, (U_C + j) % 2, kview(w_in, C_U + j * 256, 256))
            for j in range(4):
                load(U_C + 2 + j, (U_C + j) % 2, kview(w_in, C_GB + j * 256, 256))
            load(U_POOL, U_POOL % 2, inp["w_pool_group"][0].rearrange("g p n -> p g n"), nk=NG)
            for j in range(4):
                load(U_BR + j, j % 2, kview(inp["w_branch_gla"][0], j * 256, 256))
            for j in range(4):
                load(U_OUT + j, j % 2, kview(inp["w_out"][0], j * 256, 256))
                if j == 1:
                    sp.wait_ge(s_merge_hi, KT)
                    sp.wait_ge(s_merge_lo, KT)
                    sp.wait_ge(s_x_out, 16)
                    sp.dma_start(xres[:, :, :].rearrange("p k t -> p (k t)"), x_dram).then_inc(s_x_back, 16)

            def ada_load(n, slot):
                if later(n - 1):
                    sp.wait_ge(s_ada_used, n - 1)
                sp.dma_start(ada[:, slot, :, :], kview(inp["w_ada_2"][0], n * P, P)).then_inc(s_ada_in[slot], 16)

            b, _, free = TL(U_OUT, KT - 1)
            sp.wait_ge(s_acc_free[b], free + 1)
            ada_load(0, 0)
            ada_load(1, 1)
            with sp.Fori(0, FT // 2) as i:
                for j in range(2):
                    load_pair(U_FIN + j + i * 2, j, w_fin, i * 256 + j * P, i * 256 + j * P + D_FF)
                    ada_load(i * 2 + j + 2, j)
            with sp.Fori(0, 4) as i:
                for j in range(4):
                    u, half = U_FOUT + j + i * 4, FT // 2
                    raw_free(sp, u)
                    src = w_fout[(j % 2) * half * P:(j % 2 + 1) * half * P, :]
                    sp.dma_start(rawk(j % 2, half, P), kview(src, i * 256 + (j // 2) * P, P))\
                        .then_inc(s_unit_in[j % 2], 32)

            def bias_load(i):
                if later(i):
                    sp.wait_ge(s_logit, i * 8)
                sp.wait_ge(s_bias_out, 16)
                sp.dma_start(abias[:, :, :], bass.AP(tensor=bias_dram.tensor, offset=i * (2 * BW),
                                                     ap=[[1, P], [BW, 2], [1, L]])).then_inc(s_bias_in, 32)

            def att_loads(i):
                load_pair(U_ATT + i * 2, 0, w_in2, D_QA + i * P, D_KA + i * P)
                load_pair(U_ATT + 1 + i * 2, 1, w_in2, D_VA + i * P, D_ZA + i * P)

            att_loads(0)
            sp.wait_ge(s_norm_lo, norm_base(3, "lo") + KT)
            bias_load(0)
            with sp.Fori(1, A_HEADS // 2) as i:
                att_loads(i)
                bias_load(i)
            with sp.Fori(0, H_HEADS) as h:
                load_pair(U_HG + h * 2, 0, w_in2, D_QB + h * P, D_FB + h * P)
                load_pair(U_HG + 1 + h * 2, 1, w_in2, D_IB + h * P, D_ZB + h * P)
            for j in range(8):
                load(U_G2 + j, j % 2, kview(w_in2, D_GA + j * 256, 256))
            for j in range(2):
                load(U_BA + j, j % 2, kview(inp["w_branch_a_2"][0], j * L, L), nk=AW // P, ncol=L)
            for j in range(4):
                load(U_BB + j, j % 2, kview(inp["w_branch_b_2"][0], j * 256, 256))
            for j in range(4):
                load(U_OUT2 + j, j % 2, kview(inp["w_out_2"][0], j * 256, 256))
            for t in range(TT):
                sp.wait_ge(s_y_nat, 2 * (t + 1))
                sp.dma_start(out[0, t * P:(t + 1) * P, :], ynat[:, t, :]).then_inc(s_y_out, 16)
            sp.wait_ge(s_y_out, 16 * TT)

        @block.scalar
        def _(act):
            A = nc.scalar.activation
            act.wait_ge(s_vrow_zero, 3)
            rows = [("norm_mix", R_NM), ("gla_norm", R_GN), ("pool_scale", R_PS), ("norm_ffn", R_NF),
                    ("b_decay_fwd", R_BF), ("b_decay_bwd", R_BB), ("norm_g_2", R_NG2), ("b_ada_2", R_ADA),
                    ("norm_final", R_NFIN), ("c_2", R_C), ("hgrn_onorm_g_2", R_ON), ("final_g_2", R_FG)]
            for name, r in rows:
                v = inp[name] if len(inp[name].shape) == 1 else inp[name][0]
                n = v.shape[0] // P
                act.dma_start(vrow[r:r + n, :], v.rearrange("(r p) -> r p", p=P)).then_inc(s_rows_in, 16)
            act.dma_start(vrow[R_LB0:R_LB0 + 16, :], inp["hgrn_lb_2"].rearrange("l (r p) -> (l r) p", p=P))\
               .then_inc(s_rows_in, 16)
            act.dma_start(relb[0:N_BUCKETS, :], inp["rel_bias_2"]).then_inc(s_bias_src, 16)
            act.dma_start(hot[:, :], inp["hot"]).then_inc(s_bias_src, 16)
            act.dma_start(mask_src[:, :, :], inp["masks"]).then_inc(s_mask_src, 16)
            e = inp["edge"]
            act.dma_start(edge[:, :, :].rearrange("p g c -> p (g c)"),
                          bass.AP(tensor=e.tensor, offset=0, ap=[[0, P], [1, NG * 2 * PAD]])).then_inc(s_edge_in, 16)
            act.dma_start(wup[0:RANK, 0, :], inp["w_decay_up_fwd"][0]).then_inc(s_wup_in, 16)
            act.dma_start(wup[RANK:2 * RANK, 1, :], inp["w_decay_up_bwd"][0]).then_inc(s_wup_in, 16)

            def added(u0, c):
                b, _, free = TL(u0, c)
                return s_acc_free[b], free + 1

            def norm(n, src_ready):
                for k in range(KT):
                    act.wait_ge(*src_ready(k))
                    if k > 1:
                        act.wait_ge(s_norm_acc, norm_base(n, "acc") + k - 1)
                    A(nsq[:, k % 2, :], xres[:, k, :], ACT.Square).then_inc(s_norm_sq, 1)
                act.wait_ge(s_norm_sum, norm_base(n, "sum") + 1)
                A(nrs[:, :], M[3][:, :], ACT.Ln, bias=eps_col, scale=1.0 / DM).then_inc(s_norm_ln, 1)
                act.wait_ge(s_norm_ln, norm_base(n, "ln") + 1)
                A(nrs[:, :], nrs[:, :], ACT.Exp, scale=-0.5).then_inc(s_norm_rs, 1)

            def norm_hi(n, shift=False):
                for k in range(KT):
                    act.wait_ge(s_norm_ht, norm_base(n, "ht") + k + 1)
                    if shift:
                        A(hhi[:, k, :], nht[:, k % 2, :], ACT.Identity, bias=mod[:, k:k + 1])\
                            .then_inc(s_norm_hi, 1)
                    else:
                        A(hhi[:, k, :], nht[:, k % 2, :], ACT.Copy).then_inc(s_norm_hi, 1)

            act.wait_ge(s_eps, 1)
            act.wait_ge(s_vcol_mm, 1)
            A(vcol[:, :], M[0][:, 0:P], ACT.Copy).then_inc(s_vcol, 1)
            act.wait_ge(s_bias_mm, 2)
            A(brow[:, 0:L], M[1][0:A_HEADS, :], ACT.Copy).then_inc(s_bias_row, 1)
            A(brow[:, L:BW], M[2][0:A_HEADS, 0:BW - L], ACT.Copy).then_inc(s_bias_row, 1)
            act.wait_ge(s_vcol, 1)
            A(small[:, 24:32], vcol[:, R_C:R_C + KT], ACT.Sigmoid).then_inc(s_csig, 1)
            act.wait_ge(s_lb_d, 2)
            A(lbt[:, 3:5, :], lbt[:, 3:5, :], ACT.Exp).then_inc(s_lb_e, 1)

            split_hi(act, 0, 0, KT * P)
            for k in range(KT):
                act.wait_ge(s_xT, k + 1)
                A(xres[:, k, :], M[k % 4][:, :], ACT.Copy).then_inc(s_xT_out, 1)
            norm(0, lambda k: (s_xT_out, k + 1))
            norm_hi(0)

            split_hi(act, 1, 1)
            b, full, _ = TL(U_LR, 0)
            act.wait_ge(s_acc_full, full)
            A(lrT[:, :], acc[b][0:2 * RANK, :], ACT.Copy).then_inc(s_acc_free[b], 1)
            for i in range(8):
                act.wait_ge(s_up_mm, i + 1)
                if i > 1:
                    act.wait_ge(s_la, i - 1)
                t = lt[:, 0, i % 2, :]
                A(t, M[i % 4][:, :], ACT.Abs, bias=vcol[:, R_BF + i:R_BF + i + 1]).then_inc(s_la_abs, 1)
                act.wait_ge(s_la_abs, i + 1)
                A(t, t, ACT.Exp, scale=-1.0).then_inc(s_la_exp, 1)
                act.wait_ge(s_la_exp, i + 1)
                A(t, t, ACT.Ln, bias=1.0).then_inc(s_la_ln, 1)

            def head_evict_qk(h):
                for c, dst, sc in ((0, gq, DK ** -0.5), (1, gk, 1.0)):
                    b, full, _ = TL(U_HEAD, c, 8, h)
                    act.wait_ge(s_acc_full, full)
                    if later(h):
                        act.wait_ge(s_der, h * 6)
                    A(dst[:, :], acc[b][:, :], ACT.Copy, scale=sc).then_inc(s_acc_free[b], 1)

            def head_evict_ga(h):
                for c in range(2):
                    b, full, _ = TL(U_HEAD, 2 + c, 8, h)
                    act.wait_ge(s_acc_full, full)
                    act.wait_ge(s_x_out, 16)
                    A(cols(sig_ga, h * 2 + c), acc[b][:, :], ACT.Sigmoid).then_inc(s_acc_free[b], 1)

            def head_evict_v(h):
                for c in range(2):
                    b, full, _ = TL(U_HEAD, 4 + c, 8, h)
                    act.wait_ge(s_acc_full, full)
                    A(gv[:, 2 * c:2 * c + 2, :].rearrange("p t v -> p (t v)"), acc[b][:, :], ACT.Copy)\
                        .then_inc(s_acc_free[b], 1)

            def head_evict_r(h):
                for c in range(2):
                    b, full, _ = TL(U_HEAD, 6 + c, 8, h)
                    act.wait_ge(s_acc_full, full)
                    if later(h):
                        act.wait_ge(s_gfin, h * 2 + 1)
                    A(gr[:, c, :], acc[b][:, :], ACT.Sigmoid).then_inc(s_r_sig, 1)

            def derive(h):
                for d in range(2):
                    b = cols(b_all, h + 4 * d)
                    last = b.rearrange("p (n c) -> p n c", c=CHUNK)[:, :, CHUNK - 1 if d == 0 else 0]
                    act.wait_ge(s_b_ready, 8)
                    if later(h * 6 + 3 * d):
                        act.wait_ge(s_der, h * 6 + 3 * d)
                    A(ex[:, 0, :], b, ACT.Exp, scale=1.0 / 16).then_inc(s_gex, 1)
                    A(ex[:, 1, :], b, ACT.Exp, scale=-1.0 / 16).then_inc(s_gex, 1)
                    A(dec[:, d, :], last, ACT.Exp, scale=1.0 / 16).then_inc(s_gdec, 1)
                    act.wait_ge(s_gdf, h * 2 + d + 1)
                    A(ex[:, 2, :], ex[:, 2, :], ACT.Exp, scale=1.0 / 16).then_inc(s_gex, 1)

            def gla_kdT(g):
                for d in range(2):
                    act.wait_ge(s_kd_tr, g * 2 + d + 1)
                    A(kdT[:, d, :, :].rearrange("p t k -> p (t k)"), M[d][:, :], ACT.Copy).then_inc(s_kdT, 1)

            def gla_squares(g):
                for j in range(2):
                    act.wait_ge(s_go, g * 2 + j + 1)
                    A(ex[:, j, :], M[j][:, :], ACT.Square).then_inc(s_gsq, 1)

            def gla_rs(g):
                act.wait_ge(s_gsum, g + 1)
                A(ex[:, 2, :], M[2][:, :], ACT.Ln, bias=eps_col, scale=1.0 / DV).then_inc(s_gln, 1)
                act.wait_ge(s_gln, g + 1)
                A(ex[:, 2, :], ex[:, 2, :], ACT.Exp, scale=-0.5).then_inc(s_grs, 1)

            def head_split(h, j):
                v = U_HEAD + 1 + j
                split_hi(act, v + h * 4, v % 2, lin=first_tile(v - 1) + h * 8)

            head_split(0, 0)
            head_evict_qk(0)
            head_split(0, 1)
            head_evict_ga(0)
            head_split(0, 2)
            head_evict_v(0)
            head_split(0, 3)
            head_evict_r(0)
            derive(0)
            with act.Fori(1, GLA_HEADS) as h:
                g = h - 1
                head_split(h, 0)
                head_evict_qk(h)
                gla_kdT(g)
                head_split(h, 1)
                head_evict_ga(h)
                head_split(h, 2)
                gla_squares(g)
                head_evict_v(h)
                head_split(h, 3)
                gla_rs(g)
                head_evict_r(h)
                derive(h)

            g = GLA_HEADS - 1
            for j in range(2):
                split_hi(act, U_C + j + 1, (U_C + j + 1) % 2)
                for c in range(2):
                    b, full, _ = TL(U_C, 2 * j + c)
                    act.wait_ge(s_acc_full, full)
                    act.wait_ge(s_upad_zero, 1)
                    A(upad[:, 2 * j + c, PAD:PAD + L], acc[b][:, :], ACT.Copy).then_inc(s_acc_free[b], 1)
                if j == 0:
                    gla_kdT(g)
            for j in range(4):
                split_hi(act, U_C + 3 + j, (U_C + 3 + j) % 2, 4 * 2 * P if j == 3 else 16 * P)
                if j == 0:
                    gla_squares(g)
                if j == 1:
                    gla_rs(g)
                for c in range(2):
                    b, full, _ = TL(U_C, 4 + 2 * j + c)
                    act.wait_ge(s_acc_full, full)
                    act.wait_ge(s_der, 6 * GLA_HEADS)
                    A(gbm[:, 2 * j + c, :], acc[b][:, :], ACT.Sigmoid).then_inc(s_acc_free[b], 1)
            for g in range(NG):
                act.wait_ge(s_pooled, g + 1)
                A(phi[:, g, :], upad[:, g, PAD:PAD + L], ACT.Copy).then_inc(s_p_hi, 1)
            split_hi(act, U_BR, U_BR % 2)
            act.wait_ge(s_acc_full, first_tile(U_POOL))
            for k in range(KT):
                act.wait_ge(s_gfin, 2 * GLA_HEADS + 1)
                A(hhi[:, k, :], o_all[:, k, :], ACT.Copy).then_inc(s_o_hi, 1)
            for j in range(4):
                split_hi(act, U_BR + j + 1, (U_BR + j + 1) % 2)
                for c in range(2):
                    k = 2 * j + c
                    act.wait_ge(s_merged, k + 1)
                    A(mhi[:, k, :], sig_ga[:, k, :], ACT.Copy).then_inc(s_merge_hi, 1)
            for j in range(4):
                split_hi(act, U_OUT + j + 1, (U_OUT + j + 1) % 2)

            norm(1, lambda k: added(U_OUT, k))
            norm_hi(1)
            with act.Fori(0, FT // 2) as i:
                for j in range(2):
                    v = U_FIN + 1 + j
                    split_hi(act, v + i * 2, v % 2, lin=first_tile(v - 1) + i * 4)
                    b, full, _ = TL(U_FIN, 2 * j, 4, i)
                    act.wait_ge(s_acc_full, full)
                    A(fsg[:, j, :], acc[b][:, :], ACT.Sigmoid).then_inc(s_f_sig, 1)
                    bu, _, free = TL(U_FIN, 2 * j + 1, 4, i)
                    act.wait_ge(s_acc_free[bu], free + 1)
                    A(cols(ahi, i * 2 + j), faa[:, j, :], ACT.Copy).then_inc(s_f_hi, 1)
            with act.Fori(0, 4) as i:
                for j in range(4):
                    v = U_FOUT + 1 + j
                    split_hi(act, v + i * 4, v % 2, lin=first_tile(v - 1) + i * 4)

            norm(2, lambda k: added(U_FOUT, 2 * k + 1))
            norm(3, lambda k: (s_x_mid, k + 1))
            act.wait_ge(s_mod, 2)
            norm_hi(3, shift=True)

            def att_split(i, j):
                v = U_ATT + 1 + j
                split_hi(act, v + i * 2, v % 2, lin=first_tile(v - 1) + i * 4)

            def att_copy(i, c, dst, scale=1.0):
                b, full, _ = TL(U_ATT, c, 4, i)
                act.wait_ge(s_acc_full, full)
                A(dst[:, :], acc[b][:, :], ACT.Copy, scale=scale).then_inc(s_acc_free[b], 1)

            def att_evict0(i, first=False):
                if later(i):
                    act.wait_ge(s_score, i * 8)
                att_copy(i, 0, aq, AE ** -0.5)
                att_copy(i, 1, ak)

            def att_evict1(i):
                if later(i):
                    act.wait_ge(s_av_tr, i)
                att_copy(i, 2, av)
                b, full, _ = TL(U_ATT, 3, 4, i)
                act.wait_ge(s_acc_full, full)
                if later(i):
                    act.wait_ge(s_a_out, i + 1)
                A(az[:, :], acc[b][:, :], ACT.Sigmoid).then_inc(s_az_sig, 1)

            def att_vt(g):
                act.wait_ge(s_av_tr, g + 1)
                A(avt[:, :, :].rearrange("p t v -> p (t v)"), M[3][:, :], ACT.Copy).then_inc(s_avt, 1)

            def att_exp(g, a):
                for q in range(TT):
                    n = (q + 1) * P
                    act.wait_ge(s_amax, g * 8 + a * 4 + q + 1)
                    A(apr[:, a, q, 0:n], apr[:, a, q, 0:n], ACT.Exp, bias=amax[:, a, q:q + 1],
                      accum_out=aden[:, a, q:q + 1]).then_inc(s_aexp, 1)

            def att_pt(g, a):
                act.wait_ge(s_apv, g * 2 + a + 1)
                for q in range(TT):
                    act.wait_ge(s_a_tr, g * 8 + a * 4 + q + 1)
                    A(apt[:, 0:q + 1, q * P:(q + 1) * P], M[q % 3][:, 0:(q + 1) * P].rearrange("p (j c) -> p j c", c=P),
                      ACT.Copy).then_inc(s_apt, 1)

            att_split(0, 0)
            att_evict0(0)
            att_split(0, 1)
            att_evict1(0)

            def att_iteration(i, units):
                g = i - 1
                if units:
                    att_split(i, 0)
                att_vt(g)
                att_exp(g, 0)
                att_pt(g, 0)
                if units:
                    att_evict0(i)
                    att_split(i, 1)
                att_exp(g, 1)
                att_pt(g, 1)
                if units:
                    att_evict1(i)

            with act.Fori(1, A_HEADS // 2) as i:
                att_iteration(i, True)
            att_iteration(A_HEADS // 2, False)

            def hg_split(h, j):
                v = U_HG + 1 + j
                split_hi(act, v + h * 2, v % 2, lin=first_tile(v - 1) + h * 4)

            def hg_evict0(h):
                if later(h):
                    act.wait_ge(s_h_w, h * 7)
                if later(h):
                    act.wait_ge(s_h_score, h * 8 - 7)
                for c, dst in ((0, hq), (1, hf)):
                    b, full, _ = TL(U_HG, c, 4, h)
                    act.wait_ge(s_acc_full, full)
                    if c == 1:
                        if later(h):
                            act.wait_ge(s_h_b, h)
                    A(dst[:, :], acc[b][:, :], ACT.Sigmoid).then_inc(s_hq_sig if c == 0 else s_acc_free[b], 1)

            def hg_evict1(h):
                b, full, _ = TL(U_HG, 2, 4, h)
                act.wait_ge(s_acc_full, full)
                A(hi_[:, :], acc[b][:, :], ACT.Copy).then_inc(s_acc_free[b], 1)
                b, full, _ = TL(U_HG, 3, 4, h)
                act.wait_ge(s_acc_full, full)
                if later(h):
                    act.wait_ge(s_h_out, h + 1)
                A(hz[:, :], acc[b][:, :], ACT.Sigmoid).then_inc(s_hz_sig, 1)

            def hg_factors(g):
                act.wait_ge(s_h_fg, g * 2 + 2)
                A(hf[:, :], hf[:, :], ACT.Ln).then_inc(s_h_ln, 1)
                act.wait_ge(s_h_b, g + 1)
                A(hqe[:, :], hb[:, :], ACT.Exp).then_inc(s_h_ex, 1)
                A(dec[:, 0, 0:TT], hb[:, :].rearrange("p (n c) -> p n c", c=P)[:, :, P - 1], ACT.Exp)\
                    .then_inc(s_h_ex, 1)
                act.wait_ge(s_h_df, g * 8 + 1)
                A(hkd[:, :], hkd[:, :], ACT.Exp).then_inc(s_h_ex, 1)
                for lev in range(LEVELS):
                    act.wait_ge(s_h_df, g * 8 + 2 + lev)
                    A(hw[:, lev, :], hw[:, lev, :], ACT.Exp).then_inc(s_h_lex, 1)

            def hg_copies(g):
                act.wait_ge(s_h_itr, g + 1)
                A(hit[:, :, :].rearrange("p t v -> p (t v)"), M[0][:, :], ACT.Copy).then_inc(s_h_cp, 1)
                act.wait_ge(s_h_ktr, g + 1)
                A(hkT[:, :, :].rearrange("p t k -> p (t k)"), M[1][:, :], ACT.Copy).then_inc(s_h_cp, 1)

            def hg_square(g):
                act.wait_ge(s_h_o, g + 1)
                A(hsq[:, :], M[2][:, :], ACT.Square).then_inc(s_h_sq, 1)

            def hg_rs(g):
                act.wait_ge(s_h_sum, g + 1)
                A(hrs[:, :], M[3][:, :], ACT.Ln, bias=eps_col, scale=1.0 / P).then_inc(s_h_rl, 1)
                act.wait_ge(s_h_rl, g + 1)
                A(hrs[:, :], hrs[:, :], ACT.Exp, scale=-0.5).then_inc(s_h_rs, 1)

            act.wait_ge(s_a_out, A_HEADS // 2 + 1)
            hg_split(0, 0)
            hg_evict0(0)
            hg_split(0, 1)
            hg_evict1(0)

            def hg_iteration(h, units):
                g = h - 1
                hg_factors(g)
                if units:
                    hg_split(h, 0)
                hg_copies(g)
                if units:
                    hg_evict0(h)
                    hg_split(h, 1)
                hg_square(g)
                hg_rs(g)
                if units:
                    hg_evict1(h)

            with act.Fori(1, H_HEADS) as h:
                hg_iteration(h, True)
            hg_iteration(H_HEADS, False)

            for j in range(8):
                split_hi(act, U_G2 + j + 1, (j + 1) % 2)
                for c in range(2):
                    k = 2 * j + c
                    b, full, _ = TL(U_G2, k)
                    act.wait_ge(s_acc_full, full)
                    A((sga if j < 4 else sgb)[:, k % KT, :], acc[b][:, :], ACT.Sigmoid).then_inc(s_acc_free[b], 1)
            act.wait_ge(s_h_out, H_HEADS + 1)
            for k in range(AW // P):
                A(oahi[:, k, :], oa[:, k, :], ACT.Copy).then_inc(s_oa_hi, 1)
            for k in range(KT):
                A(hhi[:, k, :], ob[:, k, :], ACT.Copy).then_inc(s_ob_hi, 1)
            for u in range(U_BA, U_OUT2):
                split_hi(act, u + 1, (u + 1) % 2)
                if u >= U_BB:
                    for c in range(2):
                        k = 2 * (u - U_BB) + c
                        act.wait_ge(s_merge2, k + 1)
                        A(nhi[:, k, :], sgb[:, k, :], ACT.Copy).then_inc(s_n_hi, 1)
            for u in range(U_OUT2, U_END - 1):
                split_hi(act, u + 1, (u + 1) % 2)
            norm(4, lambda k: added(U_OUT2, k))
            for t in range(TT):
                for c in range(2):
                    act.wait_ge(s_y_tr, 2 * t + c + 1)
                    A(ynat[:, t, c * L:(c + 1) * L], M[(2 * t + c) % 4][:, :], ACT.Copy).then_inc(s_y_nat, 1)

        @block.vector
        def _(dve):
            V = nc.vector

            def hold():
                V.memset(tick[:, 0:1], 0.0)

            for n, started in enumerate((s_gfin, s_a_out, s_apv, s_h_out, s_h_rs)):
                V.memset(tick[:, n + 1:n + 2], 0.0).then_inc(started, 1)
            V.memset(ones[:, :], 1.0).then_inc(s_ones, 1)
            V.memset(eps_col, EPS).then_inc(s_eps, 1)
            V.memset(rst[:, :], 1.0).then_inc(s_rst, 1)
            dve.wait_ge(s_rst, 1)
            V.memset(rst[:, :].rearrange("p (n c) -> p n c", c=CHUNK)[:, :, 0], 0.0).then_inc(s_rst, 1)

            dve.wait_ge(s_vcol, 1)
            lb0, lb1 = vcol[:, R_LB0:R_LB0 + 8], vcol[:, R_LB1:R_LB1 + 8]
            V.tensor_tensor(lbt[:, 2, :], lb0, lb1, ALU.max).then_inc(s_lb_m, 1)
            dve.wait_ge(s_lb_m, 1)
            V.tensor_tensor(lbt[:, 3, :], lb0, lbt[:, 2, :], ALU.subtract).then_inc(s_lb_d, 1)
            V.tensor_tensor(lbt[:, 4, :], lb1, lbt[:, 2, :], ALU.subtract).then_inc(s_lb_d, 1)
            dve.wait_ge(s_csig, 1)
            V.tensor_tensor(silu_c, vcol[:, R_C:R_C + KT], small[:, 24:32], ALU.mult).then_inc(s_silu_c, 1)
            dve.wait_ge(s_lb_e, 1)
            V.tensor_tensor(lbt[:, 5, :], lbt[:, 3, :], lbt[:, 4, :], ALU.add).then_inc(s_lb_s, 1)
            dve.wait_ge(s_lb_s, 1)
            V.reciprocal(lbt[:, 5, :], lbt[:, 5, :]).then_inc(s_lb_s, 1)
            dve.wait_ge(s_lb_s, 2)
            V.tensor_tensor(lbt[:, 0, :], lbt[:, 3, :], lbt[:, 5, :], ALU.mult).then_inc(s_lb, 1)
            dve.wait_ge(s_lb, 1)
            V.tensor_scalar(lbt[:, 1, :], lbt[:, 0, :], -1.0, 1.0, ALU.mult, ALU.add).then_inc(s_lb, 1)

            def norm_sum(n):
                for k in range(1, KT):
                    dve.wait_ge(s_norm_sq, norm_base(n, "sq") + k + 1)
                    if k > 1:
                        dve.wait_ge(s_norm_acc, norm_base(n, "acc") + k - 1)
                    V.tensor_tensor(nacc[:, :], nsq[:, 0, :] if k == 1 else nacc[:, :], nsq[:, k % 2, :], ALU.add)\
                        .then_inc(s_norm_acc, 1)
                dve.wait_ge(s_norm_rs, norm_base(n, "rs") + 1)

            def norm_split(n, g, shift=False):
                def low(k):
                    dve.wait_ge(s_norm_hi, norm_base(n, "hi") + k + 1)
                    h = hhi[:, k, :].bitcast(f32)
                    if shift:
                        V.scalar_tensor_tensor(hlo[:, k, :], nht[:, k % 2, :], mod[:, k:k + 1], h, ALU.add,
                                               ALU.subtract).then_inc(s_norm_lo, 1)
                    else:
                        V.tensor_tensor(hlo[:, k, :], nht[:, k % 2, :], h, ALU.subtract).then_inc(s_norm_lo, 1)
                for k in range(KT):
                    if k > 1:
                        dve.wait_ge(s_norm_lo, norm_base(n, "lo") + k - 1)
                    V.scalar_tensor_tensor(nht[:, k % 2, :], xres[:, k, :], g(k), nrs[:, :], ALU.mult, ALU.mult)\
                        .then_inc(s_norm_ht, 1)
                    if k >= 1:
                        low(k - 1)
                low(KT - 1)

            norm_sum(0)
            norm_split(0, lambda k: vcol[:, R_NM + k:R_NM + k + 1])

            for i in range(8):
                dve.wait_ge(s_la_abs, i + 1)
                V.tensor_scalar(lt[:, 1, i % 2, :], M[i % 4][:, :], vcol[:, R_BF + i:R_BF + i + 1], 0.0,
                                ALU.add, ALU.min).then_inc(s_la_min, 1)
                dve.wait_ge(s_la_ln, i + 1)
                dve.wait_ge(s_la_min, i + 1)
                V.tensor_tensor(lt[:, 1, i % 2, :], lt[:, 1, i % 2, :], lt[:, 0, i % 2, :], ALU.subtract)\
                    .then_inc(s_la, 1)
                dve.wait_ge(s_la, i + 1)
                dve.wait_ge(s_rst, 2)
                o, a = (b_all[:, i, :], lt[:, 1, i % 2, :]) if i < 4 else (b_all[:, i, ::-1], lt[:, 1, i % 2, ::-1])
                V.tensor_tensor_scan(o, rst[:, :], a, 0.0, ALU.mult, ALU.add).then_inc(s_b_ready, 1)

            def gla_derive(h):
                dve.wait_ge(*moved(U_HEAD, 0, 8, h))
                dve.wait_ge(*moved(U_HEAD, 1, 8, h))
                dve.wait_ge(s_b_ready, 8)
                for d in range(2):
                    b = cols(b_all, h + 4 * d).rearrange("p (n c) -> p n c", c=CHUNK)
                    e = CHUNK - 1 if d == 0 else 0
                    last = b[:, :, e:e + 1].to_broadcast([P, NCH, CHUNK])
                    if later(h * 6 + 3 * d):
                        dve.wait_ge(s_der, h * 6 + 3 * d)
                    V.tensor_tensor(ex[:, 2, :].rearrange("p (n c) -> p n c", c=CHUNK), last, b, ALU.subtract)\
                        .then_inc(s_gdf, 1)
                    dve.wait_ge(s_gex, h * 6 + 3 * d + 1)
                    V.tensor_tensor(qe[:, d, :], gq[:, :], ex[:, 0, :], ALU.mult).then_inc(s_der, 1)
                    dve.wait_ge(s_gex, h * 6 + 3 * d + 2)
                    V.tensor_tensor(ke[:, d, :], gk[:, :], ex[:, 1, :], ALU.mult).then_inc(s_der, 1)
                    dve.wait_ge(s_gex, h * 6 + 3 * d + 3)
                    V.tensor_tensor(kd[:, d, :], gk[:, :], ex[:, 2, :], ALU.mult).then_inc(s_der, 1)

            def head_r(h):
                for c in range(2):
                    b, _, _ = TL(U_HEAD, 6 + c, 8, h)
                    dve.wait_ge(s_r_sig, h * 2 + c + 1)
                    V.tensor_tensor(gr[:, c, :], gr[:, c, :], acc[b][:, :], ALU.mult).then_inc(s_acc_free[b], 1)

            def gla_mask(g):
                V.memset(ga_sc[:, :, :], 0.0).then_inc(s_gmask, 1)
                for d in range(2):
                    dve.wait_ge(s_gsc, g * 2 + d + 1)
                    dve.wait_ge(s_gmask, g * 3 + d + 1)
                    dve.wait_ge(s_masks, 1)
                    hold()
                    m = masks[:, d:d + 1, :].to_broadcast([P, TT, P])
                    V.copy_predicated(ga_sc[:, :, :], m, M[2 + d][:, :].rearrange("p (t c) -> p t c", c=P))\
                        .then_inc(s_gmask, 1)

            def gla_states(g):
                for s in range(NCH - 1):
                    for d in range(2):
                        kv = M[2 * d + s % 2][:, 0:DV]
                        dve.wait_ge(s_kv, g * 14 + 2 * s + d + 1)
                        if s == 0:
                            V.tensor_copy(st[:, d, 0, :], kv).then_inc(s_gst, 1)
                        else:
                            n = s if d == 0 else NCH - 1 - s
                            dve.wait_ge(s_gst, g * 14 + 2 * s + d - 1)
                            dve.wait_ge(s_gdec, g * 2 + d + 1)
                            V.scalar_tensor_tensor(st[:, d, s, :], st[:, d, s - 1, :], dec[:, d, n:n + 1], kv,
                                                   ALU.mult, ALU.add).then_inc(s_gst, 1)

            def gla_final(g):
                dve.wait_ge(s_grs, g + 1)
                for j in range(2):
                    V.scalar_tensor_tensor(ex[:, j, :], M[j][:, :], col(vcol, g * 2 + (R_GN + j)), ex[:, 2, :],
                                           ALU.mult, ALU.mult).then_inc(s_gt, 1)
                for j in range(2):
                    b, _, free = TL(U_HEAD, 6 + j, 8, g)
                    dve.wait_ge(s_gt, g * 2 + j + 1)
                    dve.wait_ge(s_acc_free[b], free + 1)
                    V.tensor_tensor(cols(o_all, g * 2 + j), ex[:, j, :], gr[:, j, :], ALU.mult)\
                        .then_inc(s_gfin, 1)

            head_r(0)
            gla_derive(0)
            with dve.Fori(1, GLA_HEADS) as h:
                gla_mask(h - 1)
                gla_states(h - 1)
                gla_final(h - 1)
                head_r(h)
                gla_derive(h)
            g = GLA_HEADS - 1
            V.memset(upad[:, :, :], 0.0).then_inc(s_upad_zero, 1)
            gla_mask(g)
            gla_states(g)
            gla_final(g)

            n_adds = 0
            for g, w in enumerate(POOL_WINDOWS):
                dve.wait_ge(*moved(U_C, g))
                dve.wait_ge(s_gfin, 2 * GLA_HEADS + 1)
                if g > 0:
                    dve.wait_ge(s_pool_mid, g)
                if g > 0:
                    dve.wait_ge(s_pool_side, g)
                if g > 0:
                    dve.wait_ge(s_pooled, g)
                src, n, step, flip = upad[:, g, :], L + 2 * PAD, 1, 0
                while step < w:
                    n -= step
                    dst = (ptmp, ptmp2)[flip][:, 0:n]
                    V.tensor_tensor(dst, src[:, 0:n], src[:, step:step + n], ALU.add).then_inc(s_pool_add, 1)
                    n_adds += 1
                    dve.wait_ge(s_pool_add, n_adds)
                    src, flip, step = dst, 1 - flip, step * 2
                sums = src[:, PAD - w // 2:PAD - w // 2 + L]
                edges = (ptmp, ptmp2)[flip]
                dve.wait_ge(s_edge_in, 16)
                for side, c0 in ((0, 0), (1, L - PAD)):
                    V.tensor_tensor(edges[:, side * PAD:(side + 1) * PAD], sums[:, c0:c0 + PAD],
                                    edge[:, g, side * PAD:(side + 1) * PAD], ALU.mult).then_inc(s_pool_edge, 1)
                u = upad[:, g, PAD:PAD + L]
                V.scalar_tensor_tensor(u[:, PAD:L - PAD], sums[:, PAD:L - PAD], 1.0 / w, u[:, PAD:L - PAD],
                                       ALU.mult, ALU.subtract).then_inc(s_pool_mid, 1)
                dve.wait_ge(s_pool_edge, 2 * g + 2)
                for side, c0 in ((0, 0), (1, L - PAD)):
                    V.tensor_tensor(u[:, c0:c0 + PAD], edges[:, side * PAD:(side + 1) * PAD], u[:, c0:c0 + PAD],
                                    ALU.subtract).then_inc(s_pool_side if side == 0 else s_pooled, 1)
            for g in range(NG):
                dve.wait_ge(s_p_hi, g + 1)
                dve.wait_ge(s_pool_mid, g + 1)
                dve.wait_ge(s_pool_side, g + 1)
                dve.wait_ge(s_pooled, g + 1)
                V.tensor_tensor(plo[:, g, :], upad[:, g, PAD:PAD + L], phi[:, g, :].bitcast(f32), ALU.subtract)\
                    .then_inc(s_p_lo, 1)
            for k in range(KT):
                dve.wait_ge(s_o_hi, k + 1)
                V.tensor_tensor(hlo[:, k, :], o_all[:, k, :], hhi[:, k, :].bitcast(f32), ALU.subtract)\
                    .then_inc(s_o_lo, 1)
            for k in range(KT):
                b, full, free = TL(U_POOL, k)
                dve.wait_ge(s_acc_full, full)
                dve.wait_ge(*moved(U_C, 4 + k))
                V.scalar_tensor_tensor(gbm[:, k, :], acc[b][:, :], vcol[:, R_PS + k:R_PS + k + 1], gbm[:, k, :],
                                       ALU.mult, ALU.mult).then_inc(s_acc_free[b], 1)
            for k in range(KT):
                b, full, free = TL(U_BR, k)
                dve.wait_ge(s_acc_full, full)
                V.tensor_tensor(sig_ga[:, k, :], sig_ga[:, k, :], acc[b][:, :], ALU.mult)\
                    .then_inc(s_acc_free[b], 1)
                dve.wait_ge(s_acc_free[b], free + 1)
                V.tensor_tensor(sig_ga[:, k, :], sig_ga[:, k, :], gbm[:, k, :], ALU.add).then_inc(s_merged, 1)
                dve.wait_ge(s_merge_hi, k + 1)
                V.tensor_tensor(mlo[:, k, :], sig_ga[:, k, :], mhi[:, k, :].bitcast(f32), ALU.subtract)\
                    .then_inc(s_merge_lo, 1)
            dve.wait_ge(s_x_back, 16)
            for k in range(KT):
                b, full, free = TL(U_OUT, k)
                dve.wait_ge(s_acc_full, full)
                V.tensor_tensor(xres[:, k, :], xres[:, k, :], acc[b][:, :], ALU.add).then_inc(s_acc_free[b], 1)

            norm_sum(1)
            norm_split(1, lambda k: vcol[:, R_NF + k:R_NF + k + 1])
            with dve.Fori(0, FT // 2) as i:
                for j in range(2):
                    bg, _, gfree = TL(U_FIN, 2 * j, 4, i)
                    bu, full, ufree = TL(U_FIN, 2 * j + 1, 4, i)
                    dve.wait_ge(s_f_sig, i * 2 + j + 1)
                    V.tensor_tensor(fsg[:, j, :], fsg[:, j, :], acc[bg][:, :], ALU.mult)\
                        .then_inc(s_acc_free[bg], 1)
                    dve.wait_ge(s_acc_full, full)
                    dve.wait_ge(s_acc_free[bg], gfree + 1)
                    V.tensor_tensor(faa[:, j, :], fsg[:, j, :], acc[bu][:, :], ALU.mult)\
                        .then_inc(s_acc_free[bu], 1)
                    dve.wait_ge(s_f_hi, i * 2 + j + 1)
                    V.tensor_tensor(cols(alo, i * 2 + j), faa[:, j, :], cols(ahi, i * 2 + j).bitcast(f32),
                                    ALU.subtract).then_inc(s_f_lo, 1)
            dve.wait_ge(s_ada_mm, 1)
            V.tensor_tensor(mod[:, :], M[2][:, 0:24], vcol[:, R_ADA:R_ADA + 24], ALU.add).then_inc(s_mod, 1)
            dve.wait_ge(s_mod, 1)
            V.scalar_tensor_tensor(g2_col, mod[:, KT:2 * KT], 1.0, vcol[:, R_NG2:R_NG2 + KT], ALU.add, ALU.mult)\
                .then_inc(s_mod, 1)
            with dve.Fori(0, 4) as i:
                for j in range(4):
                    b, full, _ = TL(U_FOUT, j, 4, i)
                    dve.wait_ge(s_acc_full, full)
                    if j:
                        dve.wait_ge(s_acc_free[(b - 1) % 4], TL(U_FOUT, j - 1, 4, i)[2] + 1)
                    x = cols(xres, i * 2 + j // 2)
                    V.tensor_tensor(x, x, acc[b][:, :], ALU.add).then_inc(s_acc_free[b], 1)

            norm_sum(2)
            for k in range(KT):
                V.scalar_tensor_tensor(xres[:, k, :], xres[:, k, :], vcol[:, R_NFIN + k:R_NFIN + k + 1], nrs[:, :],
                                       ALU.mult, ALU.mult).then_inc(s_x_mid, 1)
            norm_sum(3)
            dve.wait_ge(s_mod, 2)
            norm_split(3, lambda k: small[:, 16 + k:17 + k], shift=True)

            def att_logits(g, a):
                dve.wait_ge(s_bias_in, g * 32 + 32)
                for q in range(TT):
                    n = (q + 1) * P
                    dve.wait_ge(s_score, g * 8 + a * 4 + q + 1)
                    hold()
                    V.tensor_tensor_reduce(out=apr[:, a, q, 0:n], in0=M[q][:, 0:n], in1=abias[:, a, n - 1::-1],
                                           scale=1.0, scalar=NEG_INF, op0=ALU.add, op1=ALU.max,
                                           accum_out=amax[:, a, q:q + 1]).then_inc(s_logit, 1)
                    dve.wait_ge(s_logit, g * 8 + a * 4 + q + 1)
                    V.tensor_scalar(amax[:, a, q:q + 1], amax[:, a, q:q + 1], -1.0, None, ALU.mult)\
                        .then_inc(s_amax, 1)

            def att_normalise(g, a):
                for q in range(TT):
                    n = (q + 1) * P
                    dve.wait_ge(s_aexp, g * 8 + a * 4 + q + 1)
                    V.reciprocal(aden[:, a, q:q + 1], aden[:, a, q:q + 1]).then_inc(s_arec, 1)
                    dve.wait_ge(s_arec, g * 8 + a * 4 + q + 1)
                    V.tensor_scalar(apr[:, a, q, 0:n], apr[:, a, q, 0:n], aden[:, a, q:q + 1], None, ALU.mult)\
                        .then_inc(s_aprob, 1)

            def att_out(g):
                dve.wait_ge(s_apv, g * 2 + 3)
                b, _, free = TL(U_ATT, 3, 4, g)
                dve.wait_ge(s_acc_free[b], free + 1)
                V.tensor_tensor(cols(oa, g), az[:, :], M[3][:, :], ALU.mult).then_inc(s_a_out, 1)

            def att_z(i):
                b, _, _ = TL(U_ATT, 3, 4, i)
                dve.wait_ge(s_az_sig, i + 1)
                V.tensor_tensor(az[:, :], az[:, :], acc[b][:, :], ALU.mult).then_inc(s_acc_free[b], 1)

            def att_head_pair(g):
                att_logits(g, 0)
                att_normalise(g, 0)
                att_logits(g, 1)
                att_normalise(g, 1)
                att_out(g)

            att_z(0)
            with dve.Fori(1, A_HEADS // 2) as i:
                att_head_pair(i - 1)
                att_z(i)
            att_head_pair(A_HEADS // 2 - 1)

            V.memset(hrst[:, :], 1.0).then_inc(s_hrst, 1)
            dve.wait_ge(s_hrst, 1)
            V.memset(hrst[:, :].rearrange("p (n c) -> p n c", c=P)[:, :, 0], 0.0).then_inc(s_hrst, 1)

            def hg_gate(dst, sigmoid, c, h):
                b, _, _ = TL(U_HG, c, 4, h)
                dve.wait_ge(sigmoid, h + 1)
                V.tensor_tensor(dst[:, :], dst[:, :], acc[b][:, :], ALU.mult).then_inc(s_acc_free[b], 1)

            def hg_factors(g):
                dve.wait_ge(*moved(U_HG, 0, 4, g))
                dve.wait_ge(*moved(U_HG, 1, 4, g))
                dve.wait_ge(s_lb, 2)
                V.tensor_scalar(hf[:, :], hf[:, :], col(lbt[:, 1, :], g), col(lbt[:, 0, :], g), ALU.mult, ALU.add)\
                    .then_inc(s_h_fg, 1)
                dve.wait_ge(s_h_fg, g * 2 + 1)
                V.tensor_scalar(hk[:, :], hf[:, :], -1.0, 1.0, ALU.mult, ALU.add).then_inc(s_h_fg, 1)
                dve.wait_ge(s_h_ln, g + 1)
                dve.wait_ge(s_hrst, 2)
                V.tensor_tensor_scan(hb[:, :], hrst[:, :], hf[:, :], 0.0, ALU.mult, ALU.add).then_inc(s_h_b, 1)
                dve.wait_ge(s_h_b, g + 1)
                b = hb[:, :].rearrange("p (n c) -> p n c", c=P)
                V.tensor_tensor(hkd[:, :].rearrange("p (n c) -> p n c", c=P),
                                b[:, :, P - 1:P].to_broadcast([P, TT, P]), b, ALU.subtract).then_inc(s_h_df, 1)
                for lev in range(LEVELS):
                    half = 1 << lev
                    nb = L // (2 * half)
                    bb = hb[:, :].rearrange("p (n c) -> p n c", c=2 * half)
                    ww = hw[:, lev, :].rearrange("p (n c) -> p n c", c=2 * half)
                    mid = bb[:, :, half - 1:half].to_broadcast([P, nb, half])
                    V.tensor_tensor(ww[:, :, 0:half], mid, bb[:, :, 0:half], ALU.subtract).then_inc(s_h_dl, 1)
                    V.tensor_tensor(ww[:, :, half:], bb[:, :, half:], mid, ALU.subtract).then_inc(s_h_df, 1)
                dve.wait_ge(s_h_ex, g * 3 + 1)
                V.tensor_tensor(hqe[:, :], hqe[:, :], hq[:, :], ALU.mult).then_inc(s_h_op, 1)
                dve.wait_ge(s_h_ex, g * 3 + 3)
                dve.wait_ge(s_h_fg, g * 2 + 2)
                V.tensor_tensor(hkd[:, :], hkd[:, :], hk[:, :], ALU.mult).then_inc(s_h_op, 1)
                for lev in range(LEVELS):
                    half = 1 << lev
                    v3 = lambda t: t.rearrange("p (n c) -> p n c", c=2 * half)
                    ww = v3(hw[:, lev, :])
                    dve.wait_ge(s_h_lex, g * 7 + lev + 1)
                    V.tensor_tensor(ww[:, :, 0:half], ww[:, :, 0:half], v3(hk[:, :])[:, :, 0:half], ALU.mult)\
                        .then_inc(s_h_wl, 1)
                    V.tensor_tensor(ww[:, :, half:], ww[:, :, half:], v3(hq[:, :])[:, :, half:], ALU.mult)\
                        .then_inc(s_h_w, 1)

            def hg_mask(g):
                V.memset(hsc[:, :, :], 0.0).then_inc(s_h_mask, 1)
                for n in range(LEVELS + 1):
                    dve.wait_ge(s_h_score, g * 8 + n + 1)
                    dve.wait_ge(s_h_mask, g * 9 + n + 1)
                    dve.wait_ge(s_masks, 1)
                    hold()
                    lev = (LEVELS, *range(LEVELS))[n]
                    m = masks[:, 2 + lev:3 + lev, :].to_broadcast([P, TT, P])
                    V.copy_predicated(hsc[:, :, :], m, M[(n + 2) % 4][:, :].rearrange("p (t c) -> p t c", c=P))\
                        .then_inc(s_h_mask, 1)

            def hg_states(g):
                dve.wait_ge(s_h_kv, g + 1)
                dve.wait_ge(s_h_ex, g * 3 + 2)
                for n in range(TT - 1):
                    kv = M[3][:, n * P:(n + 1) * P]
                    if n == 0:
                        V.tensor_copy(hst[:, 0, :], kv).then_inc(s_h_st, 1)
                    else:
                        dve.wait_ge(s_h_st, g * 3 + n)
                        V.scalar_tensor_tensor(hst[:, n, :], hst[:, n - 1, :], dec[:, 0, n:n + 1], kv, ALU.mult,
                                               ALU.add).then_inc(s_h_st, 1)

            def hg_final(g):
                dve.wait_ge(s_h_rs, g + 2)
                V.scalar_tensor_tensor(hsq[:, :], M[2][:, :], vcol[:, R_ON:R_ON + 1], hrs[:, :], ALU.mult, ALU.mult)\
                    .then_inc(s_h_t, 1)
                dve.wait_ge(s_h_t, g + 1)
                b, _, free = TL(U_HG, 3, 4, g)
                dve.wait_ge(s_acc_free[b], free + 1)
                V.tensor_tensor(cols(ob, g), hsq[:, :], hz[:, :], ALU.mult).then_inc(s_h_out, 1)

            hg_gate(hq, s_hq_sig, 0, 0)
            hg_gate(hz, s_hz_sig, 3, 0)

            def hg_iteration(h, units):
                g = h - 1
                hg_factors(g)
                hg_mask(g)
                hg_states(g)
                if units:
                    hg_gate(hq, s_hq_sig, 0, h)
                hg_final(g)
                if units:
                    hg_gate(hz, s_hz_sig, 3, h)

            with dve.Fori(1, H_HEADS) as h:
                hg_iteration(h, True)
            hg_iteration(H_HEADS, False)

            for k in range(AW // P):
                dve.wait_ge(s_oa_hi, k + 1)
                V.tensor_tensor(oalo[:, k, :], oa[:, k, :], oahi[:, k, :].bitcast(f32), ALU.subtract)\
                    .then_inc(s_oa_lo, 1)
            for k in range(KT):
                dve.wait_ge(s_ob_hi, k + 1)
                V.tensor_tensor(hlo[:, k, :], ob[:, k, :], hhi[:, k, :].bitcast(f32), ALU.subtract)\
                    .then_inc(s_ob_lo, 1)
            for k in range(KT):
                b, full, _ = TL(U_BA, k)
                dve.wait_ge(s_acc_full, full)
                dve.wait_ge(*moved(U_G2, k))
                V.tensor_tensor(sga[:, k, :], sga[:, k, :], acc[b][:, :], ALU.mult).then_inc(s_acc_free[b], 1)
            for k in range(KT):
                b, full, free = TL(U_BB, k)
                dve.wait_ge(s_acc_full, full)
                dve.wait_ge(*moved(U_G2, KT + k))
                V.tensor_tensor(sgb[:, k, :], sgb[:, k, :], acc[b][:, :], ALU.mult).then_inc(s_acc_free[b], 1)
                dve.wait_ge(s_acc_free[b], free + 1)
                dve.wait_ge(*moved(U_BA, k))
                V.tensor_tensor(sgb[:, k, :], sgb[:, k, :], sga[:, k, :], ALU.add).then_inc(s_merge2, 1)
                dve.wait_ge(s_n_hi, k + 1)
                V.tensor_tensor(nlo[:, k, :], sgb[:, k, :], nhi[:, k, :].bitcast(f32), ALU.subtract)\
                    .then_inc(s_n_lo, 1)
            for k in range(KT):
                b, full, _ = TL(U_OUT2, k)
                dve.wait_ge(s_acc_full, full)
                V.scalar_tensor_tensor(xres[:, k, :], acc[b][:, :], mod[:, 2 * KT + k:2 * KT + k + 1], xres[:, k, :],
                                       ALU.mult, ALU.add).then_inc(s_acc_free[b], 1)
            norm_sum(4)
            for k in range(KT):
                V.scalar_tensor_tensor(yT[:, k, :], xres[:, k, :], vcol[:, R_FG + k:R_FG + k + 1], nrs[:, :],
                                       ALU.mult, ALU.mult).then_inc(s_yT, 1)

        @block.gpsimd
        def _(pool):
            nc.gpsimd.memset(vrow[:, :], 0.0).then_inc(s_vrow_zero, 1)
            nc.gpsimd.memset(wup[:, :, :], 0.0).then_inc(s_vrow_zero, 1)
            nc.gpsimd.memset(relb[:, :], 1.0).then_inc(s_vrow_zero, 1)
            pool.wait_ge(s_mask_src, 16)
            nc.gpsimd.tensor_copy(masks[:, :, :], mask_src[:, :, :]).then_inc(s_masks, 1)
            split_lo(pool, 0, 0, KT * P)
            with pool.Fori(0, (U_POOL - 1) // 2) as i:
                split_lo(pool, i * 2 + 1, 1)
                split_lo(pool, i * 2 + 2, 0)
            split_lo(pool, U_POOL, 1, 4 * 2 * P)
            with pool.Fori(0, (U_END - U_BR) // 2) as i:
                split_lo(pool, i * 2 + U_BR, 0)
                split_lo(pool, i * 2 + U_BR + 1, 1)

        @block.tensor
        def _(pe):
            mm = nc.tensor.matmul

            def tile(u0, c, slot, j, per=0, i=0, nk=KT, ncol=2 * P, xh=hhi, xl=hlo):
                b, _, free = TL(u0, c, per, i)
                if later(free):
                    pe.wait_ge(s_acc_free[b], free)
                pe_tile(b, slot, j, nk, ncol, xh, xl)

            def units(u0, n, xh=hhi, xl=hlo, nk=KT, ncol=2 * P, uc=None):
                per = ncol // P
                for m in range(n):
                    pe.wait_ge(s_unit_lo, u0 + m + 1)
                    for j in range(per):
                        tile(u0, per * m + j, (u0 + m) % 2, j, nk=nk, ncol=ncol, xh=xh, xl=xl)

            def norm(n):
                pe.wait_ge(s_ones, 1)
                pe.wait_ge(s_norm_acc, norm_base(n, "acc") + KT - 1)
                mm(M[3][:, :], ones[:, :], nacc[:, :], start=True, stop=True).then_inc(s_norm_sum, 1)

            pe.wait_ge(s_id_in, 16)
            pe.wait_ge(s_rows_in, 13 * 16)
            nc.tensor.transpose(M[0][:, 0:P], vrow[:, :], ident[:, :]).then_inc(s_vcol_mm, 1)
            pe.wait_ge(s_bias_src, 32)
            mm(M[1][0:A_HEADS, :], relb[0:N_BUCKETS + 1, :], hot[:, 0:L], start=True, stop=True)\
                .then_inc(s_bias_mm, 1)
            mm(M[2][0:A_HEADS, 0:BW - L], relb[0:N_BUCKETS + 1, :], hot[:, L:BW], start=True, stop=True)\
                .then_inc(s_bias_mm, 1)
            pe.wait_ge(s_x_in, 16 * TT)
            pe.wait_ge(s_vcol, 1)
            pe.wait_ge(s_bias_row, 2)
            for k in range(KT):
                if k > 3:
                    pe.wait_ge(s_xT_out, k - 3)
                for t in range(TT):
                    last = nc.tensor.transpose(M[k % 4][:, t * P:(t + 1) * P], xnat[:, t, k * P:(k + 1) * P],
                                               ident[:, :])
                last.then_inc(s_xT, 1)
            pe.wait_ge(s_xT_out, KT)
            norm(0)

            pe.wait_ge(s_unit_lo, 0 + 1)
            pe.wait_ge(s_norm_lo, norm_base(0, "lo") + KT)
            tile(U_LR, 0, 0, 0, ncol=P)
            pe.wait_ge(*moved(U_LR, 0))
            pe.wait_ge(s_wup_in, 32)
            for i in range(8):
                if i > 3:
                    pe.wait_ge(s_la, i - 3)
                mm(M[i % 4][:, :], wup[:, i // 4, (i % 4) * P:(i % 4 + 1) * P], lrT[:, :], start=True, stop=True)\
                    .then_inc(s_up_mm, 1)

            def gla_scores(g):
                for d in range(2):
                    pe.wait_ge(s_der, g * 6 + 3 * d + 3)
                    if d == 0:
                        pe.wait_ge(s_gfin, g * 2 + 1)
                        pe.wait_ge(s_la, 8)
                    for t in range(TT):
                        last = nc.tensor.transpose(M[d][:, t * P:(t + 1) * P], kd[:, d, t * P:(t + 1) * P], ident[:, :])
                    last.then_inc(s_kd_tr, 1)
                    for t in range(TT):
                        ts = slice(t * P, (t + 1) * P)
                        last = mm(M[2 + d][:, ts], ke[:, d, ts], qe[:, d, ts], start=True, stop=True)
                    last.then_inc(s_gsc, 1)

            def gla_kv(g):
                pe.wait_ge(s_kdT, g * 2 + 2)
                pe.wait_ge(s_gmask, g * 3 + 3)
                pe.wait_ge(*moved(U_HEAD, 4, 8, g))
                pe.wait_ge(*moved(U_HEAD, 5, 8, g))
                for s in range(NCH - 1):
                    for d in range(2):
                        n = s if d == 0 else NCH - 1 - s
                        rows = slice(n % 2 * CHUNK, (n % 2 + 1) * CHUNK)
                        if s >= 2:
                            pe.wait_ge(s_gst, g * 14 + 2 * (s - 2) + d + 1)
                        mm(M[2 * d + s % 2][:, 0:DV], kdT[rows, d, n // 2, :], gv[rows, n // 2, :],
                           start=True, stop=True).then_inc(s_kv, 1)

            def gla_out(g):
                pe.wait_ge(s_gst, g * 14 + 14)
                for j in range(2):
                    js = slice(j * P, (j + 1) * P)
                    for t in range(TT):
                        mm(M[j][:, t * P:(t + 1) * P], gv[:, t, js], ga_sc[:, t, :], start=(t == 0), stop=False,
                           skip_group_check=True)
                    for n in range(1, NCH):
                        mm(M[j][:, n * CHUNK:(n + 1) * CHUNK], st[:, 0, n - 1, js],
                           qe[:, 0, n * CHUNK:(n + 1) * CHUNK], start=False, stop=False, skip_group_check=True)
                    for n in range(NCH - 1):
                        last = mm(M[j][:, n * CHUNK:(n + 1) * CHUNK], st[:, 1, NCH - 2 - n, js],
                                  qe[:, 1, n * CHUNK:(n + 1) * CHUNK], start=False, stop=(n == NCH - 2),
                                  skip_group_check=True)
                    last.then_inc(s_go, 1)

            def gla_sum(g):
                pe.wait_ge(s_gsq, g * 2 + 2)
                mm(M[2][:, :], ones[:, :], ex[:, 0, :], start=True, stop=False)
                mm(M[2][:, :], ones[:, :], ex[:, 1, :], start=False, stop=True).then_inc(s_gsum, 1)

            def head_tiles(h, c, j):
                tile(U_HEAD, c, (1 + c // 2) % 2, j, 8, h)

            def head_values(h, c):
                b, _, free = TL(U_HEAD, 4 + c, 8, h)
                if later(free):
                    pe.wait_ge(s_acc_free[b], free)
                pe_values(b, 1, c, hhi, hlo)

            def head_iteration(h, gla):
                g = h - 1
                pe.wait_ge(s_unit_lo, h * 4 + U_HEAD + 1)
                head_tiles(h, 0, 0)
                head_tiles(h, 1, 1)
                if gla:
                    gla_scores(g)
                pe.wait_ge(s_unit_lo, h * 4 + U_HEAD + 2)
                head_tiles(h, 2, 0)
                head_tiles(h, 3, 1)
                if gla:
                    gla_kv(g)
                pe.wait_ge(s_unit_lo, h * 4 + U_HEAD + 3)
                head_values(h, 0)
                if gla:
                    gla_out(g)
                head_values(h, 1)
                pe.wait_ge(s_unit_lo, h * 4 + U_HEAD + 4)
                head_tiles(h, 6, 0)
                if gla:
                    gla_sum(g)
                head_tiles(h, 7, 1)

            head_iteration(0, False)
            with pe.Fori(1, GLA_HEADS) as h:
                head_iteration(h, True)
            g = GLA_HEADS - 1
            units(U_C, 1)
            gla_scores(g)
            pe.wait_ge(s_unit_lo, U_C + 1 + 1)
            for j in range(2):
                tile(U_C, 2 + j, (U_C + 1) % 2, j)
            gla_kv(g)
            for m in range(2, 6):
                pe.wait_ge(s_unit_lo, U_C + m + 1)
                tile(U_C, 2 * m, (U_C + m) % 2, 0)
                if m == 2:
                    gla_out(g)
                tile(U_C, 2 * m + 1, (U_C + m) % 2, 1)
                if m == 2:
                    gla_sum(g)

            pe.wait_ge(s_unit_lo, U_POOL + 1)
            pe.wait_ge(s_p_lo, NG)
            for gr_ in range(NG):
                for j in range(2):
                    b, _, free = TL(U_POOL, 2 * gr_ + j)
                    if later(free):
                        pe.wait_ge(s_acc_free[b], free)
                    ws = slice(gr_ * 2 * P + j * P, gr_ * 2 * P + (j + 1) * P)
                    mm(acc[b][:, :], whi[:, 1, ws], phi[:, gr_, :], start=True, stop=False)
                    mm(acc[b][:, :], whi[:, 1, ws], plo[:, gr_, :], start=False, stop=False)
                    mm(acc[b][:, :], wlo[:, 1, ws], phi[:, gr_, :], start=False, stop=True)\
                        .then_inc(s_acc_full, 1)
            pe.wait_ge(s_o_lo, KT)
            units(U_BR, 4)
            pe.wait_ge(s_merge_lo, KT)
            units(U_OUT, 4, mhi, mlo)

            def ada_tile(n, slot):
                pe.wait_ge(s_ada_in[slot], (n - slot) * 8 + 16)
                for k in range(KT):
                    last = mm(M[2][:, ds(n, 1)], ada[:, slot, k, :], silu_c[:, k:k + 1], start=(k == 0),
                              stop=(k == KT - 1), skip_group_check=True)
                last.then_inc(s_ada_used, 1)

            norm(1)
            pe.wait_ge(s_silu_c, 1)
            pe.wait_ge(s_norm_lo, norm_base(1, "lo") + KT)
            with pe.Fori(0, FT // 2) as i:
                for j in range(2):
                    pe.wait_ge(s_unit_lo, i * 2 + U_FIN + j + 1)
                    tile(U_FIN, 2 * j, j, 0, 4, i)
                    tile(U_FIN, 2 * j + 1, j, 1, 4, i)
                    ada_tile(i * 2 + j, j)
            ada_tile(FT, 0)
            pe.wait_ge(s_ada_in[1], (FT // 2 + 1) * 16)
            for k in range(KT):
                last = mm(M[2][:, FT + 1:FT + 2], ada[:, 1, k, :], silu_c[:, k:k + 1], start=(k == 0),
                          stop=(k == KT - 1), skip_group_check=True)
            last.then_inc(s_ada_mm, 1)
            pe.wait_ge(s_f_lo, FT)
            half = FT // 2
            with pe.Fori(0, 4) as i:
                for j in range(4):
                    pe.wait_ge(s_unit_lo, i * 4 + U_FOUT + j + 1)
                    ks = slice(j % 2 * half, (j % 2 + 1) * half)
                    tile(U_FOUT, j, j % 2, 0, 4, i, nk=half, ncol=P, xh=ahi[:, ks, :], xl=alo[:, ks, :])

            norm(2)
            norm(3)
            pe.wait_ge(s_norm_lo, norm_base(3, "lo") + KT)

            def att_values(g):
                pe.wait_ge(s_a_out, g + 1)
                pe.wait_ge(*moved(U_ATT, 2, 4, g))
                for t in range(TT):
                    last = nc.tensor.transpose(M[3][:, t * P:(t + 1) * P], av[:, t * P:(t + 1) * P], ident[:, :])
                last.then_inc(s_av_tr, 1)

            def att_scores(g, a):
                pe.wait_ge(*moved(U_ATT, 0, 4, g))
                pe.wait_ge(*moved(U_ATT, 1, 4, g))
                r = slice(a * AE, (a + 1) * AE)
                for q in range(TT):
                    if a == 0 and q == 3:
                        pe.wait_ge(s_avt, g + 1)
                    if a == 1 and q < 3:
                        pe.wait_ge(s_apt, g * 8 + (4, 2, 3)[q])
                    mm(M[q][:, 0:(q + 1) * P], aq[r, q * P:(q + 1) * P], ak[r, 0:(q + 1) * P], start=True, stop=True)\
                        .then_inc(s_score, 1)

            def att_transposes(g, a):
                for q in range(TT):
                    pe.wait_ge(s_aprob, g * 8 + a * 4 + q + 1)
                    if q == 3:
                        pe.wait_ge(s_apt, g * 8 + a * 4 + 1)
                    for j in range(q + 1):
                        last = nc.tensor.transpose(M[q % 3][:, j * P:(j + 1) * P], apr[:, a, q, j * P:(j + 1) * P],
                                                   ident[:, :])
                    last.then_inc(s_a_tr, 1)

            def att_pv(g, a):
                pe.wait_ge(s_apt, g * 8 + a * 4 + 4)
                pe.wait_ge(s_logit, g * 8 + 8)
                r = slice(a * AE, (a + 1) * AE)
                for j in range(TT):
                    last = mm(M[3][r, j * P:L], avt[:, j, r], apt[:, j, j * P:L], start=(j == 0), stop=(j == TT - 1))
                last.then_inc(s_apv, 1)

            def att_iteration(i, with_units, attend):
                g = i - 1
                if with_units:
                    pe.wait_ge(s_unit_lo, i * 2 + U_ATT + 1)
                    tile(U_ATT, 0, 0, 0, 4, i)
                if attend:
                    att_values(g)
                    att_scores(g, 0)
                if with_units:
                    tile(U_ATT, 1, 0, 1, 4, i)
                if attend:
                    att_transposes(g, 0)
                    att_scores(g, 1)
                if with_units:
                    pe.wait_ge(s_unit_lo, i * 2 + U_ATT + 1 + 1)
                    tile(U_ATT, 2, 1, 0, 4, i)
                if attend:
                    att_pv(g, 0)
                    att_transposes(g, 1)
                if with_units:
                    tile(U_ATT, 3, 1, 1, 4, i)
                if attend:
                    att_pv(g, 1)

            att_iteration(0, True, False)
            with pe.Fori(1, A_HEADS // 2) as i:
                att_iteration(i, True, True)
            att_iteration(A_HEADS // 2, False, True)

            def hg_scores(g):
                if isinstance(g, int) and g == 0:
                    pe.wait_ge(s_a_out, A_HEADS // 2 + 1)
                pe.wait_ge(s_h_out, g + 1)
                pe.wait_ge(s_h_rs, g + 1)
                pe.wait_ge(*moved(U_HG, 2, 4, g))
                for t in range(TT):
                    last = nc.tensor.transpose(M[0][:, t * P:(t + 1) * P], hi_[:, t * P:(t + 1) * P], ident[:, :])
                last.then_inc(s_h_itr, 1)
                pe.wait_ge(s_h_op, g * 2 + 2)
                for t in range(TT):
                    last = nc.tensor.transpose(M[1][:, t * P:(t + 1) * P], hkd[:, t * P:(t + 1) * P], ident[:, :])
                last.then_inc(s_h_ktr, 1)
                for n in range(LEVELS + 1):
                    if n == 0:
                        pe.wait_ge(*moved(U_HG, 0, 4, g))
                    pe.wait_ge(s_h_w, g * 7 + max(n, 1))
                    if n == 2:
                        pe.wait_ge(s_h_cp, g * 2 + 1)
                    if n == 3:
                        pe.wait_ge(s_h_cp, g * 2 + 2)
                    if n >= 4:
                        pe.wait_ge(s_h_mask, g * 9 + n - 2)
                    for t in range(TT):
                        ts = slice(t * P, (t + 1) * P)
                        left, right = (hk[:, ts], hq[:, ts]) if n == 0 else (hw[:, n - 1, ts], hw[:, n - 1, ts])
                        last = mm(M[(n + 2) % 4][:, ts], left, right, start=True, stop=True)
                    last.then_inc(s_h_score, 1)
                pe.wait_ge(s_h_mask, g * 9 + 7)
                for n in range(TT - 1):
                    last = mm(M[3][:, n * P:(n + 1) * P], hkT[:, n, :], hit[:, n, :], start=True, stop=True)
                last.then_inc(s_h_kv, 1)

            def hg_out(g):
                pe.wait_ge(s_h_mask, g * 9 + 9)
                pe.wait_ge(s_h_st, g * 3 + 3)
                for t in range(TT):
                    mm(M[2][:, t * P:(t + 1) * P], hit[:, t, :], hsc[:, t, :], start=(t == 0), stop=False,
                       skip_group_check=True)
                for t in range(1, TT):
                    last = mm(M[2][:, t * P:(t + 1) * P], hst[:, t - 1, :], hqe[:, t * P:(t + 1) * P], start=False,
                              stop=(t == TT - 1), skip_group_check=True)
                last.then_inc(s_h_o, 1)

            def hg_sum(g):
                pe.wait_ge(s_h_sq, g + 1)
                mm(M[3][:, :], ones[:, :], hsq[:, :], start=True, stop=True).then_inc(s_h_sum, 1)

            def hg_iteration(h, with_units, recur):
                g = h - 1
                if with_units:
                    pe.wait_ge(s_unit_lo, h * 2 + U_HG + 1)
                    tile(U_HG, 0, 0, 0, 4, h)
                    tile(U_HG, 1, 0, 1, 4, h)
                if recur:
                    hg_scores(g)
                if with_units:
                    pe.wait_ge(s_unit_lo, h * 2 + U_HG + 1 + 1)
                    tile(U_HG, 2, 1, 0, 4, h)
                if recur:
                    hg_out(g)
                if with_units:
                    tile(U_HG, 3, 1, 1, 4, h)
                if recur:
                    hg_sum(g)

            hg_iteration(0, True, False)
            with pe.Fori(1, H_HEADS) as h:
                hg_iteration(h, True, True)
            hg_iteration(H_HEADS, False, True)

            units(U_G2, 8)
            pe.wait_ge(s_oa_lo, AW // P)
            units(U_BA, 2, oahi, oalo, nk=AW // P, ncol=L)
            pe.wait_ge(s_ob_lo, KT)
            units(U_BB, 4)
            pe.wait_ge(s_n_lo, KT)
            units(U_OUT2, 4, nhi, nlo)
            norm(4)
            for t in range(TT):
                for c in range(2):
                    m = 2 * t + c
                    if m == 3:
                        pe.wait_ge(s_norm_rs, norm_base(4, "rs") + 1)
                    if m > 3:
                        pe.wait_ge(s_y_nat, m - 3)
                    pe.wait_ge(s_yT, 4 * c + 4)
                    for k in range(4):
                        last = nc.tensor.transpose(M[m % 4][:, k * P:(k + 1) * P],
                                                   yT[:, 4 * c + k, t * P:(t + 1) * P], ident[:, :])
                    last.then_inc(s_y_tr, 1)


_INS = ["x", "norm_mix", "w_in", "w_decay_up_fwd", "b_decay_fwd", "w_decay_up_bwd", "b_decay_bwd", "gla_norm",
        "w_branch_gla", "w_pool_group", "pool_scale", "w_out", "norm_ffn", "w_ffn_in", "w_ffn_out", "norm_final",
        "c_2", "w_ada_2", "b_ada_2", "norm_g_2", "w_in_2", "hgrn_onorm_g_2", "w_branch_a_2", "w_branch_b_2",
        "w_out_2", "rel_bias_2", "hgrn_lb_2", "final_g_2"]


def kernel(**inputs):
    import numpy as _np
    import concourse.bacc as _bacc
    from concourse import mybir as _mybir
    from concourse.bass_utils import run_bass_kernel_spmd as _run

    nc = _bacc.Bacc("TRN2", target_bir_lowering=False, num_devices=1)
    arrays, aps = {}, {}
    for name, a in [(n, inputs[n]) for n in _INS] + list(shape_constants().items()):
        a = _np.ascontiguousarray(a)
        arrays[f"in_{name}_dram"] = a
        aps[name] = nc.dram_tensor(f"in_{name}_dram", a.shape, _mybir.dt.from_np(a.dtype), kind="ExternalInput").ap()
    y = nc.dram_tensor("out_0_dram", (1, L, DM), _mybir.dt.float32, kind="ExternalOutput").ap()
    build(nc, aps, y)
    r = _run(nc, [arrays], core_ids=[0])
    return r.results[0]["out_0_dram"]
```

```python
import concourse.bass as bass
from concourse import mybir
from contextlib import ExitStack
import numpy as np

P = 128
DM = 1024
L = 512
KT = DM // P
TT = L // P
GLA_HEADS, DK, DV, CHUNK = 4, 128, 256, 64
NCH = L // CHUNK
RANK = 16
POOL_WINDOWS = (2, 4, 8, 16)
NG = len(POOL_WINDOWS)
PAD = 8
D_FF = 2816
FT = D_FF // P
A_HEADS, AE = 8, 64
AW = A_HEADS * AE
H_HEADS = 8
N_BUCKETS, MAX_DISTANCE = 32, 2048
PATTERNS = ((128, 1), (512, 4), (2048, 16))
NEG_INF = -1e30
EPS = 1e-6
LEVELS = 7
BW = 640

C_Q, C_K, C_V, C_R = 0, 512, 1024, 2048
C_LR = 3072
C_U = C_LR + 2 * RANK
C_GA = C_U + 512
C_GB = C_GA + DM
D_QA, D_KA, D_VA, D_ZA = 0, 512, 1024, 1536
D_QB, D_FB, D_IB, D_ZB = 2048, 3072, 4096, 5120
D_GA, D_GB = 6144, 7168

R_NM, R_GN, R_PS, R_NF, R_BF, R_BB, R_NG2, R_ADA = 0, 8, 16, 24, 32, 36, 40, 48
R_LB0, R_LB1, R_NFIN, R_C, R_ON, R_FG = 72, 80, 88, 96, 104, 105

U_LR, U_HEAD, U_C, U_POOL, U_BR, U_OUT = 0, 1, 17, 23, 24, 28
U_FIN, U_FOUT, U_ATT, U_HG, U_G2 = 32, 54, 70, 78, 94
U_BA, U_BB, U_OUT2, U_END = 102, 104, 108, 112


def first_tile(u):
    if u == 0:
        return 0
    if u <= U_POOL:
        return 2 * u - 1
    if u <= U_FOUT:
        return 53 + 2 * (u - U_BR)
    if u <= U_ATT:
        return 113 + (u - U_FOUT)
    if u <= U_BA:
        return 129 + 2 * (u - U_ATT)
    if u == U_BA + 1:
        return 197
    return 201 + 2 * (u - U_BB)


def shape_constants():
    f = np.float32
    ident = np.eye(P, dtype=f)
    s, t = np.arange(P)[:, None], np.arange(P)[None, :]
    masks = [(s // CHUNK == t // CHUNK) & (s <= t), (s // CHUNK == t // CHUNK) & (s > t)]
    for lev in range(LEVELS):
        half = 1 << lev
        masks.append((s // (2 * half) == t // (2 * half)) & (s % (2 * half) < half) & (t % (2 * half) >= half))
    masks.append(s == t)
    masks = np.ascontiguousarray(np.stack(masks, 1).astype(f))
    edge = np.zeros((NG, 2 * PAD), f)
    for g, w in enumerate(POOL_WINDOWS):
        for c in range(PAD):
            for side, pos in ((0, c), (1, L - PAD + c)):
                lo, hi = max(pos - w // 2, 0), min(pos + w - w // 2, L)
                edge[g, side * PAD + c] = 1.0 / (hi - lo)
    dist = np.arange(BW) - (P - 1)
    n = np.maximum(dist, 0).astype(f)
    exact = N_BUCKETS // 2
    large = exact + (np.log(np.maximum(n, f(1)) / f(exact)) / f(np.log(MAX_DISTANCE / exact))
                     * f(N_BUCKETS - exact)).astype(np.int32)
    bucket = np.where(dist < exact, np.maximum(dist, 0), np.minimum(large, N_BUCKETS - 1))
    count = np.zeros(BW, np.int64)
    for window, dil in PATTERNS:
        count += (dist >= 0) & (dist <= window) & (dist % dil == 0)
    hot = np.zeros((N_BUCKETS + 1, BW), f)
    hot[bucket, np.arange(BW)] = count > 0
    hot[N_BUCKETS] = np.where(count > 0, np.log(np.maximum(count, 1)), NEG_INF)
    return {"ident": ident, "masks": masks, "edge": edge, "hot": hot}


def build(nc, inp, out):
    f32, f32r, u8 = mybir.dt.float32, mybir.dt.float32r, mybir.dt.uint8
    ALU, ACT = mybir.AluOpType, mybir.ActivationFunctionType
    ds = bass.ds
    KB = 1024
    BASE = (nc.sbuf_base + 31) // 32 * 32

    def at(name, kb, shape, dt=f32):
        return nc.alloc_sbuf_tensor_at(name, shape, dt, offset=BASE + int(kb * KB))

    raw = at("raw", 0, [P, 2, 16 * P])
    whi = at("whi", 16, [P, 2, 16 * P], f32r)
    wlo = at("wlo", 32, [P, 2, 16 * P], f32r)
    hhi = at("hhi", 48, [P, KT, L], f32r)
    hlo = at("hlo", 64, [P, KT, L], f32r)
    xres = at("xres", 80, [P, KT, L])
    sig_ga = at("sig_ga", 80, [P, KT, L])
    S0 = 96
    ident = at("ident", S0, [P, P])
    mean_dm = at("mean_dm", S0 + .5, [P, P])
    mean_dv = at("mean_dv", S0 + 4.5, [P, P])
    mean_p = at("mean_p", S0 + 5, [P, P])
    vcol = at("vcol", S0 + 1, [P, P])
    masks = at("masks", S0 + 1.5, [P, LEVELS + 3, P], u8)
    mod = at("mod", S0 + 2.75, [P, 24])
    lbt = at("lbt", S0 + 3, [P, 6, 8])
    small = at("small", S0 + 3.25, [P, 32])
    eps_col = at("eps", S0 + 3.375, [P, 1])
    one_col = at("one_col", S0 + 3.40625, [P, 1])
    edge = at("edge", S0 + 3.5, [P, NG, 2 * PAD])
    amax = at("amax", S0 + 3.75, [P, 2, TT])
    aden = at("aden", S0 + 4, [P, 2, TT])
    dec = at("dec", S0 + 4.25, [P, 2, NCH])
    relb = at("relb", S0 + 4.375, [P, A_HEADS])
    tick = at("tick", S0 + 3.4375, [1, 8])
    A0 = 101.5
    mid_col = small[:, 0:8]
    silu_c = small[:, 8:16]
    g2_col = small[:, 16:24]

    xnat = at("xnat", A0 + 16, [P, TT, DM])
    vrow = at("vrow", A0 + 32, [P, P])
    hot = at("hot", A0 + 34, [N_BUCKETS + 1, BW])
    brow = at("brow", A0 + 37, [A_HEADS, BW])
    mask_src = at("mask_src", A0 + 88, [P, LEVELS + 3, P])
    wup = at("wup", A0 + 40, [2 * RANK, 2, L])
    nsq = at("nsq", A0, [P, 2, L])
    nacc = at("nacc", A0 + 4, [P, L])
    nrs = at("nrs", A0 + 6, [P, L])
    nht = at("nht", A0 + 8, [P, 2, L])
    b_all = at("b_all", A0, [P, 8, L])
    o_all = at("o_all", A0 + 16, [P, KT, L])
    lrT = at("lrT", A0 + 44, [2 * RANK, L])
    gq, gk = at("gq", A0 + 32, [P, L]), at("gk", A0 + 34, [P, L])
    lt = at("lt", A0 + 46, [P, 2, 2, L])
    gv = at("gv", A0 + 36, [P, TT, DV])
    gr = at("gr", A0 + 54, [P, 2, L])
    qe, ke = at("qe", A0 + 58, [P, 2, L]), at("ke", A0 + 62, [P, 2, L])
    kd = at("kd", A0 + 66, [P, 2, L])
    ex = at("ex", A0 + 70, [P, 3, L])
    kdT = at("kdT", A0 + 76, [P, 2, TT, P])
    ga_sc = at("ga_sc", A0 + 80, [P, TT, P])
    st = at("st", A0 + 82, [P, 2, NCH - 1, DV])
    rst = at("rst", A0 + 96, [P, L])
    gbm = at("gbm", A0, [P, KT, L])
    phi = at("phi", A0 + 64, [P, NG, L], f32r)
    plo = at("plo", A0 + 72, [P, NG, L], f32r)
    ptmp = at("ptmp", A0 + 58, [P, L + 2 * PAD])
    ptmp2 = at("ptmp2", A0 + 60.5, [P, L + 2 * PAD])
    upad = at("upad", A0 + 40, [P, NG, L + 2 * PAD])
    mhi = at("mhi", A0 + 32, [P, KT, L], f32r)
    mlo = at("mlo", A0 + 80, [P, KT, L], f32r)
    ahi = at("ahi", A0, [P, FT, L], f32r)
    alo = at("alo", A0 + 44, [P, FT, L], f32r)
    fsg = at("fsg", A0 + 88, [P, 2, L])
    faa = at("faa", A0 + 92, [P, 2, L])
    ada = at("ada", A0 + 96, [P, 2, KT, P])
    oa = at("oa", A0, [P, AW // P, L])
    ob = at("ob", A0 + 8, [P, KT, L])
    sga = at("sga", A0 + 24, [P, KT, L])
    sgb = at("sgb", A0 + 40, [P, KT, L])
    aq, ak = at("aq", A0 + 56, [P, L]), at("ak", A0 + 58, [P, L])
    av, az = at("av", A0 + 60, [P, L]), at("az", A0 + 62, [P, L])
    avt = at("avt", A0 + 64, [P, TT, P])
    abias = at("abias", A0 + 66, [P, 2, L])
    apr = at("apr", A0 + 70, [P, 2, TT, L])
    apt = at("apt", A0 + 86, [P, TT, L])
    hq, hf = at("hq", A0 + 56, [P, L]), at("hf", A0 + 58, [P, L])
    hi_, hz = at("hi_", A0 + 60, [P, L]), at("hz", A0 + 62, [P, L])
    hk, hb = at("hk", A0 + 64, [P, L]), at("hb", A0 + 66, [P, L])
    hw = at("hw", A0 + 68, [P, LEVELS, L])
    hqe, hkd = at("hqe", A0 + 82, [P, L]), at("hkd", A0 + 84, [P, L])
    hkT = at("hkT", A0 + 86, [P, TT, P])
    hit = at("hit", A0 + 88, [P, TT, P])
    hsc = at("hsc", A0 + 90, [P, TT, P])
    hst = at("hst", A0 + 92, [P, TT - 1, P])
    hsq, hrs = at("hsq", A0 + 94, [P, L]), at("hrs", A0 + 96, [P, L])
    hrst = at("hrst", A0 + 98, [P, L])
    oahi = at("oahi", A0 + 88, [P, AW // P, L], f32r)
    oalo = at("oalo", A0 + 96, [P, AW // P, L], f32r)
    nhi = at("nhi", A0 + 56, [P, KT, L], f32r)
    nlo = at("nlo", A0 + 72, [P, KT, L], f32r)
    yT = at("yT", A0 + 16, [P, KT, L])
    ynat = at("ynat", A0 + 32, [P, TT, DM])

    x_dram = nc.dram_tensor("x_scratch", (P, KT * L), f32, kind="Internal").ap()
    bias_dram = nc.dram_tensor("bias_scratch", (A_HEADS, BW), f32, kind="Internal").ap()

    ctx = ExitStack()
    with ctx:
        acc = [ctx.enter_context(nc.psum_tensor(f"acc{b}", [P, L], f32)) for b in range(4)]
        M = [ctx.enter_context(nc.psum_tensor(f"mid{b}", [P, L], f32)) for b in range(4)]
        def sem(name):
            return ctx.enter_context(nc.semaphore(name))

        s_acc_free = [sem(f"acc_free{b}") for b in range(4)]
        s_unit_in = [sem(f"unit_in{b}") for b in range(2)]
        s_ada_in = [sem(f"ada_in{b}") for b in range(2)]
        s_a_out = sem("a_out")
        s_a_tr = sem("a_tr")
        s_acc_full = sem("acc_full")
        s_ada_sum = sem("ada_sum")
        s_ada_step = sem("ada_step")
        s_mid_rs = sem("mid_rs")
        s_mid_ln = sem("mid_ln")
        s_eps = sem("eps")
        s_h_rl = sem("h_rl")
        s_gln = sem("gln")
        s_norm_ln = sem("norm_ln")
        s_x_mid = sem("x_mid")
        s_mid_step = sem("mid_step")
        s_mid_sum = sem("mid_sum")
        s_mid_acc = sem("mid_acc")
        s_mid_sq = sem("mid_sq")
        s_norm_zero = sem("norm_zero")
        s_means = sem("means")
        s_ada_used = sem("ada_used")
        s_aexp = sem("aexp")
        s_amax = sem("amax")
        s_aprob = sem("aprob")
        s_apt = sem("apt")
        s_apv = sem("apv")
        s_arec = sem("arec")
        s_av_tr = sem("av_tr")
        s_avt = sem("avt")
        s_az_sig = sem("az_sig")
        s_b_ready = sem("b_ready")
        s_bias_in = sem("bias_in")
        s_bias_mm = sem("bias_mm")
        s_bias_out = sem("bias_out")
        s_bias_row = sem("bias_row")
        s_bias_src = sem("bias_src")
        s_csig = sem("csig")
        s_der = sem("der")
        s_edge_in = sem("edge_in")
        s_f_hi = sem("f_hi")
        s_f_lo = sem("f_lo")
        s_f_sig = sem("f_sig")
        s_gdec = sem("gdec")
        s_gdf = sem("gdf")
        s_gex = sem("gex")
        s_gfin = sem("gfin")
        s_gmask = sem("gmask")
        s_go = sem("go")
        s_grs = sem("grs")
        s_gsc = sem("gsc")
        s_gsq = sem("gsq")
        s_gst = sem("gst")
        s_gsum = sem("gsum")
        s_gt = sem("gt")
        s_h_b = sem("h_b")
        s_h_cp = sem("h_cp")
        s_h_df = sem("h_df")
        s_h_dl = sem("h_dl")
        s_h_ex = sem("h_ex")
        s_h_fg = sem("h_fg")
        s_h_itr = sem("h_itr")
        s_h_ktr = sem("h_ktr")
        s_h_kv = sem("h_kv")
        s_h_lex = sem("h_lex")
        s_h_ln = sem("h_ln")
        s_h_mask = sem("h_mask")
        s_h_o = sem("h_o")
        s_h_op = sem("h_op")
        s_h_out = sem("h_out")
        s_h_rs = sem("h_rs")
        s_h_score = sem("h_score")
        s_h_sq = sem("h_sq")
        s_h_st = sem("h_st")
        s_h_sum = sem("h_sum")
        s_h_t = sem("h_t")
        s_h_w = sem("h_w")
        s_h_wl = sem("h_wl")
        s_hq_sig = sem("hq_sig")
        s_hrst = sem("hrst")
        s_hz_sig = sem("hz_sig")
        s_id_in = sem("id_in")
        s_kdT = sem("kdT")
        s_kd_tr = sem("kd_tr")
        s_kv = sem("kv")
        s_la = sem("la")
        s_la_abs = sem("la_abs")
        s_la_exp = sem("la_exp")
        s_la_ln = sem("la_ln")
        s_la_min = sem("la_min")
        s_lb = sem("lb")
        s_lb_d = sem("lb_d")
        s_lb_e = sem("lb_e")
        s_lb_m = sem("lb_m")
        s_lb_s = sem("lb_s")
        s_logit = sem("logit")
        s_mask_src = sem("mask_src")
        s_masks = sem("masks")
        s_merge2 = sem("merge2")
        s_merge_hi = sem("merge_hi")
        s_merge_lo = sem("merge_lo")
        s_merged = sem("merged")
        s_mod = sem("mod")
        s_n_hi = sem("n_hi")
        s_n_lo = sem("n_lo")
        s_norm_acc = sem("norm_acc")
        s_norm_hi = sem("norm_hi")
        s_norm_ht = sem("norm_ht")
        s_norm_lo = sem("norm_lo")
        s_norm_rs = sem("norm_rs")
        s_norm_sq = sem("norm_sq")
        s_norm_sum = sem("norm_sum")
        s_o_hi = sem("o_hi")
        s_o_lo = sem("o_lo")
        s_oa_hi = sem("oa_hi")
        s_oa_lo = sem("oa_lo")
        s_ob_hi = sem("ob_hi")
        s_ob_lo = sem("ob_lo")
        s_p_hi = sem("p_hi")
        s_p_lo = sem("p_lo")
        s_pool_add = sem("pool_add")
        s_pool_edge = sem("pool_edge")
        s_pool_mid = sem("pool_mid")
        s_pool_side = sem("pool_side")
        s_pooled = sem("pooled")
        s_r_sig = sem("r_sig")
        s_rows_in = sem("rows_in")
        s_rst = sem("rst")
        s_score = sem("score")
        s_silu_c = sem("silu_c")
        s_unit_hi = sem("unit_hi")
        s_unit_lo = sem("unit_lo")
        s_up_mm = sem("up_mm")
        s_upad_zero = sem("upad_zero")
        s_vcol = sem("vcol")
        s_vcol_mm = sem("vcol_mm")
        s_vrow_zero = sem("vrow_zero")
        s_wup_in = sem("wup_in")
        s_xT = sem("xT")
        s_xT_out = sem("xT_out")
        s_x_back = sem("x_back")
        s_x_in = sem("x_in")
        s_x_out = sem("x_out")
        s_yT = sem("yT")
        s_y_nat = sem("y_nat")
        s_y_out = sem("y_out")
        s_y_tr = sem("y_tr")

        def later(n):
            return not isinstance(n, int) or n > 0

        def nth(n):
            return n * KT

        def cols(t, k):
            return t[:, ds(k, 1), :].rearrange("p a n -> p (a n)") if not isinstance(k, int) else t[:, k, :]

        def col(t, k):
            return t[:, ds(k, 1)] if not isinstance(k, int) else t[:, k:k + 1]

        def vtile(v):
            return v.rearrange("p (a b) -> p a b", b=P)

        def used_before(u, lin=None):
            if isinstance(u, int) and lin is None:
                return first_tile(u - 1) if u >= 2 else 0
            return lin

        def split_hi(act, u, slot, n=16 * P, lin=None):
            act.wait_ge(s_unit_in[slot], unit_count(u, slot))
            if later(used_before(u, lin)):
                act.wait_ge(s_acc_full, used_before(u, lin))
            nc.scalar.activation(whi[:, slot, 0:n], raw[:, slot, 0:n], ACT.Copy).then_inc(s_unit_hi, 1)

        def split_lo(pool, u, slot, n=16 * P):
            pool.wait_ge(s_unit_hi, u + 1)
            nc.gpsimd.tensor_tensor(wlo[:, slot, 0:n], raw[:, slot, 0:n], whi[:, slot, 0:n].bitcast(f32),
                                    ALU.subtract).then_inc(s_unit_lo, 1)

        def unit_count(u, slot):
            return 32 * (u // 2 + 1) if isinstance(u, int) else (u - slot) * 16 + 32

        def raw_free(sp, u):
            if later(u - 1):
                sp.wait_ge(s_unit_lo, u - 1)

        def pe_tile(bank, slot, j, nk, ncol, xh, xl):
            for k in range(nk):
                h = whi[:, slot, k * ncol + j * P:k * ncol + (j + 1) * P]
                lo = wlo[:, slot, k * ncol + j * P:k * ncol + (j + 1) * P]
                nc.tensor.matmul(acc[bank][:, :], h, xh[:, k, :], start=(k == 0), stop=False)
                nc.tensor.matmul(acc[bank][:, :], h, xl[:, k, :], start=False, stop=False)
                last = nc.tensor.matmul(acc[bank][:, :], lo, xh[:, k, :], start=False, stop=(k == nk - 1))
            last.then_inc(s_acc_full, 1)

        def pe_values(bank, slot, pair, xh, xl):
            for t in (2 * pair, 2 * pair + 1):
                o = acc[bank][:, (t % 2) * DV:(t % 2 + 1) * DV]
                for k in range(KT):
                    h, lo = whi[:, slot, k * DV:(k + 1) * DV], wlo[:, slot, k * DV:(k + 1) * DV]
                    xs = slice(t * P, (t + 1) * P)
                    nc.tensor.matmul(o, xh[:, k, xs], h, start=(k == 0), stop=False)
                    nc.tensor.matmul(o, xh[:, k, xs], lo, start=False, stop=False)
                    last = nc.tensor.matmul(o, xl[:, k, xs], h, start=False, stop=(k == KT - 1))
            last.then_inc(s_acc_full, 1)

        def kview(w, c0, n):
            return w.rearrange("(k p) n -> p k n", p=P)[:, :, ds(c0, n)]

        def rawk(slot, nk, ncol, j0=0, n=None):
            return raw[:, slot, 0:nk * ncol].rearrange("p (k n) -> p k n", k=nk)[:, :, j0:j0 + (n or ncol)]

        def TL(u0, c, per=0, i=0):
            t = first_tile(u0) + c
            if isinstance(i, int):
                t += per * i
                return t % 4, t + 1, t // 4
            return t % 4, t + 1 + i * per, t // 4 + i * (per // 4)

        def moved(u0, c, per=0, i=0):
            b, _, free = TL(u0, c, per, i)
            return s_acc_free[b], free + 1

        w_in, w_in2 = inp["w_in"][0], inp["w_in_2"][0]
        w_fin, w_fout = inp["w_ffn_in"][0], inp["w_ffn_out"][0]

        block = ctx.enter_context(nc.Block())

        @block.sync
        def _(sp):
            def load(u, slot, src, nk=KT, ncol=2 * P):
                raw_free(sp, u)
                sp.dma_start(rawk(slot, nk, ncol), src).then_inc(s_unit_in[slot], 32)

            def load_pair(u, slot, w, ca, cb):
                raw_free(sp, u)
                sp.dma_start(rawk(slot, KT, 2 * P, 0, P), kview(w, ca, P)).then_inc(s_unit_in[slot], 16)
                sp.dma_start(rawk(slot, KT, 2 * P, P, P), kview(w, cb, P)).then_inc(s_unit_in[slot], 16)

            xn = inp["x"][0].rearrange("(t p) d -> t p d", p=P)
            sp.dma_start(ident[:, :], inp["ident"]).then_inc(s_id_in, 16)
            for t in range(TT):
                sp.dma_start(xnat[:, t, :], xn[t]).then_inc(s_x_in, 16)
            load(0, 0, kview(w_in, C_LR, P), ncol=P)

            def head_loads(h, u):
                load_pair(u, 1, w_in, C_Q + h * DK, C_K + h * DK)
                load(u + 1, 0, kview(w_in, C_GA + h * 256, 256))
                load(u + 2, 1, kview(w_in, C_V + h * DV, 256))
                load(u + 3, 0, kview(w_in, C_R + h * DV, 256))

            sp.wait_ge(s_bias_row, 2)
            sp.dma_start(bias_dram, brow[:, :]).then_inc(s_bias_out, 16)
            head_loads(0, 1)
            sp.wait_ge(s_norm_ht, KT)
            sp.dma_start(x_dram, xres[:, :, :].rearrange("p k t -> p (k t)")).then_inc(s_x_out, 16)
            with sp.Fori(1, GLA_HEADS) as h:
                head_loads(h, h * 4 + 1)
            for j in range(2):
                load(U_C + j, (U_C + j) % 2, kview(w_in, C_U + j * 256, 256))
            for j in range(4):
                load(U_C + 2 + j, (U_C + j) % 2, kview(w_in, C_GB + j * 256, 256))
            load(U_POOL, U_POOL % 2, inp["w_pool_group"][0].rearrange("g p n -> p g n"), nk=NG)
            for j in range(4):
                load(U_BR + j, j % 2, kview(inp["w_branch_gla"][0], j * 256, 256))
            for j in range(4):
                load(U_OUT + j, j % 2, kview(inp["w_out"][0], j * 256, 256))
                if j == 1:
                    sp.wait_ge(s_merge_hi, KT)
                    sp.wait_ge(s_merge_lo, KT)
                    sp.wait_ge(s_x_out, 16)
                    sp.dma_start(xres[:, :, :].rearrange("p k t -> p (k t)"), x_dram).then_inc(s_x_back, 16)

            def ada_load(n, slot):
                if later(n - 1):
                    sp.wait_ge(s_ada_used, n - 1)
                sp.dma_start(ada[:, slot, :, :], kview(inp["w_ada_2"][0], n * P, P)).then_inc(s_ada_in[slot], 16)

            for j in range(2):
                load_pair(U_FIN + j, j, w_fin, j * P, j * P + D_FF)
            sp.wait_ge(*moved(U_OUT, KT - 1))
            for j in range(2):
                ada_load(j, j)
            with sp.Fori(1, FT // 2) as i:
                for j in range(2):
                    load_pair(U_FIN + j + i * 2, j, w_fin, i * 256 + j * P, i * 256 + j * P + D_FF)
                    ada_load(i * 2 + j, j)

            def ffn_out_load(i, j):
                u, half = U_FOUT + j + i * 4, FT // 2
                raw_free(sp, u)
                src = w_fout[(j % 2) * half * P:(j % 2 + 1) * half * P, :]
                sp.dma_start(rawk(j % 2, half, P), kview(src, i * 256 + (j // 2) * P, P))\
                    .then_inc(s_unit_in[j % 2], 32)

            ffn_out_load(0, 0)
            ffn_out_load(0, 1)
            ada_load(FT, 0)
            ada_load(FT + 1, 1)
            ffn_out_load(0, 2)
            ffn_out_load(0, 3)
            with sp.Fori(1, 4) as i:
                for j in range(4):
                    ffn_out_load(i, j)

            def bias_load(i):
                if later(i):
                    sp.wait_ge(s_logit, i * 8)
                sp.wait_ge(s_bias_out, 16)
                sp.dma_start(abias[:, :, :], bass.AP(tensor=bias_dram.tensor, offset=i * (2 * BW),
                                                     ap=[[1, P], [BW, 2], [1, L]])).then_inc(s_bias_in, 32)

            def att_loads(i):
                load_pair(U_ATT + i * 2, 0, w_in2, D_QA + i * P, D_KA + i * P)
                load_pair(U_ATT + 1 + i * 2, 1, w_in2, D_VA + i * P, D_ZA + i * P)

            att_loads(0)
            sp.wait_ge(s_norm_lo, nth(2) + KT)
            bias_load(0)
            with sp.Fori(1, A_HEADS // 2) as i:
                att_loads(i)
                bias_load(i)
            with sp.Fori(0, H_HEADS) as h:
                load_pair(U_HG + h * 2, 0, w_in2, D_QB + h * P, D_FB + h * P)
                load_pair(U_HG + 1 + h * 2, 1, w_in2, D_IB + h * P, D_ZB + h * P)
            for j in range(8):
                load(U_G2 + j, j % 2, kview(w_in2, D_GA + j * 256, 256))
            for j in range(2):
                load(U_BA + j, j % 2, kview(inp["w_branch_a_2"][0], j * L, L), nk=AW // P, ncol=L)
            for j in range(4):
                load(U_BB + j, j % 2, kview(inp["w_branch_b_2"][0], j * 256, 256))
            for j in range(4):
                load(U_OUT2 + j, j % 2, kview(inp["w_out_2"][0], j * 256, 256))
            for t in range(TT):
                sp.wait_ge(s_y_nat, 2 * (t + 1))
                sp.dma_start(out[0, t * P:(t + 1) * P, :], ynat[:, t, :]).then_inc(s_y_out, 16)
            sp.wait_ge(s_y_out, 16 * TT)

        @block.scalar
        def _(act):
            A = nc.scalar.activation
            LN_EXP = "natural_log_exp_and_others"
            act.wait_ge(s_vrow_zero, 3)
            rows = [("norm_mix", R_NM), ("gla_norm", R_GN), ("pool_scale", R_PS), ("norm_ffn", R_NF),
                    ("b_decay_fwd", R_BF), ("b_decay_bwd", R_BB), ("norm_g_2", R_NG2), ("b_ada_2", R_ADA),
                    ("norm_final", R_NFIN), ("c_2", R_C), ("hgrn_onorm_g_2", R_ON), ("final_g_2", R_FG)]
            for name, r in rows:
                v = inp[name] if len(inp[name].shape) == 1 else inp[name][0]
                n = v.shape[0] // P
                act.dma_start(vrow[r:r + n, :], v.rearrange("(r p) -> r p", p=P)).then_inc(s_rows_in, 16)
            act.dma_start(vrow[R_LB0:R_LB0 + 16, :], inp["hgrn_lb_2"].rearrange("l (r p) -> (l r) p", p=P))\
               .then_inc(s_rows_in, 16)
            act.dma_start(relb[0:N_BUCKETS, :], inp["rel_bias_2"]).then_inc(s_bias_src, 16)
            act.dma_start(hot[:, :], inp["hot"]).then_inc(s_bias_src, 16)
            act.dma_start(mask_src[:, :, :], inp["masks"]).then_inc(s_mask_src, 16)
            e = inp["edge"]
            act.dma_start(edge[:, :, :].rearrange("p g c -> p (g c)"),
                          bass.AP(tensor=e.tensor, offset=0, ap=[[0, P], [1, NG * 2 * PAD]])).then_inc(s_edge_in, 16)
            act.dma_start(wup[0:RANK, 0, :], inp["w_decay_up_fwd"][0]).then_inc(s_wup_in, 16)
            act.dma_start(wup[RANK:2 * RANK, 1, :], inp["w_decay_up_bwd"][0]).then_inc(s_wup_in, 16)

            def norm_square(n, k):
                if nth(n) + max(k - 1, 0) > 0:
                    act.wait_ge(s_norm_acc, nth(n) + max(k - 1, 0))
                A(nsq[:, k % 2, :], xres[:, k, :], ACT.Square).then_inc(s_norm_sq, 1)

            def norm_rs(n):
                nc.scalar.preload_act_table_set(LN_EXP)
                act.wait_ge(s_norm_sum, n + 1)
                A(nrs[:, :], M[3][:, :], ACT.Ln, bias=eps_col[:, :]).then_inc(s_norm_ln, 1)
                act.wait_ge(s_norm_ln, n + 1)
                A(nrs[:, :], nrs[:, :], ACT.Exp, scale=-0.5).then_inc(s_norm_rs, 1)

            def norm_hi(n, shift=False):
                for k in range(KT):
                    act.wait_ge(s_norm_ht, nth(n) + k + 1)
                    if shift:
                        A(hhi[:, k, :], nht[:, k % 2, :], ACT.Identity, bias=mod[:, k:k + 1])\
                            .then_inc(s_norm_hi, 1)
                    else:
                        A(hhi[:, k, :], nht[:, k % 2, :], ACT.Copy).then_inc(s_norm_hi, 1)

            act.wait_ge(s_vcol_mm, 1)
            A(vcol[:, :], M[0][:, 0:P], ACT.Copy).then_inc(s_vcol, 1)
            act.wait_ge(s_bias_mm, 2)
            A(brow[:, 0:L], M[1][0:A_HEADS, :], ACT.Copy).then_inc(s_bias_row, 1)
            A(brow[:, L:BW], M[2][0:A_HEADS, 0:BW - L], ACT.Copy).then_inc(s_bias_row, 1)
            act.wait_ge(s_vcol, 1)
            A(small[:, 24:32], vcol[:, R_C:R_C + KT], ACT.Sigmoid).then_inc(s_csig, 1)
            act.wait_ge(s_lb_d, 2)
            A(lbt[:, 3:5, :], lbt[:, 3:5, :], ACT.Exp).then_inc(s_lb_e, 1)

            split_hi(act, 0, 0, KT * P)
            for k in range(KT):
                act.wait_ge(s_xT, k + 1)
                A(xres[:, k, :], M[k % 4][:, :], ACT.Copy).then_inc(s_xT_out, 1)
                act.wait_ge(s_xT_out, k + 1)
                norm_square(0, k)
            act.wait_ge(s_eps, 1)
            norm_rs(0)
            norm_hi(0)

            split_hi(act, 1, 1)
            b, full, _ = TL(U_LR, 0)
            act.wait_ge(s_acc_full, full)
            A(lrT[:, :], acc[b][0:2 * RANK, :], ACT.Copy).then_inc(s_acc_free[b], 1)
            nc.scalar.preload_act_table_set(LN_EXP)
            for i in range(8):
                act.wait_ge(s_up_mm, i + 1)
                if i > 1:
                    act.wait_ge(s_la, i - 1)
                t = lt[:, 0, i % 2, :]
                A(t, M[i % 4][:, :], ACT.Abs, bias=vcol[:, R_BF + i:R_BF + i + 1]).then_inc(s_la_abs, 1)
                act.wait_ge(s_la_abs, i + 1)
                A(t, t, ACT.Exp, scale=-1.0).then_inc(s_la_exp, 1)
                act.wait_ge(s_la_exp, i + 1)
                A(t, t, ACT.Ln, bias=1.0).then_inc(s_la_ln, 1)

            def head_evict_qk(h):
                for c, dst, sc in ((0, gq, DK ** -0.5), (1, gk, 1.0)):
                    b, full, _ = TL(U_HEAD, c, 8, h)
                    act.wait_ge(s_acc_full, full)
                    if later(h):
                        act.wait_ge(s_der, h * 6)
                    A(dst[:, :], acc[b][:, :], ACT.Copy, scale=sc).then_inc(s_acc_free[b], 1)

            def head_evict_ga(h):
                for c in range(2):
                    b, full, _ = TL(U_HEAD, 2 + c, 8, h)
                    act.wait_ge(s_acc_full, full)
                    act.wait_ge(s_x_out, 16)
                    A(cols(sig_ga, h * 2 + c), acc[b][:, :], ACT.Sigmoid).then_inc(s_acc_free[b], 1)

            def head_evict_v(h):
                for c in range(2):
                    b, full, _ = TL(U_HEAD, 4 + c, 8, h)
                    act.wait_ge(s_acc_full, full)
                    A(gv[:, 2 * c:2 * c + 2, :].rearrange("p t v -> p (t v)"), acc[b][:, :], ACT.Copy)\
                        .then_inc(s_acc_free[b], 1)

            def head_evict_r(h):
                for c in range(2):
                    b, full, _ = TL(U_HEAD, 6 + c, 8, h)
                    act.wait_ge(s_acc_full, full)
                    if later(h):
                        act.wait_ge(s_gfin, h * 2 + 1)
                    A(gr[:, c, :], acc[b][:, :], ACT.Sigmoid).then_inc(s_r_sig, 1)

            def derive(h):
                for d in range(2):
                    b = cols(b_all, h + 4 * d)
                    last = b.rearrange("p (n c) -> p n c", c=CHUNK)[:, :, CHUNK - 1 if d == 0 else 0]
                    act.wait_ge(s_b_ready, 8)
                    if later(h * 6 + 3 * d):
                        act.wait_ge(s_der, h * 6 + 3 * d)
                    A(ex[:, 0, :], b, ACT.Exp, scale=1.0 / 16).then_inc(s_gex, 1)
                    A(ex[:, 1, :], b, ACT.Exp, scale=-1.0 / 16).then_inc(s_gex, 1)
                    A(dec[:, d, :], last, ACT.Exp, scale=1.0 / 16).then_inc(s_gdec, 1)
                    act.wait_ge(s_gdf, h * 2 + d + 1)
                    A(ex[:, 2, :], ex[:, 2, :], ACT.Exp, scale=1.0 / 16).then_inc(s_gex, 1)

            def gla_kdT(g):
                for d in range(2):
                    act.wait_ge(s_kd_tr, g * 2 + d + 1)
                    A(kdT[:, d, :, :].rearrange("p t k -> p (t k)"), M[d][:, :], ACT.Copy).then_inc(s_kdT, 1)

            def gla_squares(g):
                for j in range(2):
                    act.wait_ge(s_go, g * 2 + j + 1)
                    A(ex[:, j, :], M[j][:, :], ACT.Square).then_inc(s_gsq, 1)

            def gla_rs(g):
                nc.scalar.preload_act_table_set(LN_EXP)
                act.wait_ge(s_gsum, g + 1)
                A(ex[:, 2, :], M[2][:, :], ACT.Ln, bias=eps_col[:, :]).then_inc(s_gln, 1)
                act.wait_ge(s_gln, g + 1)
                A(ex[:, 2, :], ex[:, 2, :], ACT.Exp, scale=-0.5).then_inc(s_grs, 1)

            def head_split(h, j):
                v = U_HEAD + 1 + j
                split_hi(act, v + h * 4, v % 2, lin=first_tile(v - 1) + h * 8)

            head_split(0, 0)
            head_evict_qk(0)
            head_split(0, 1)
            head_evict_ga(0)
            head_split(0, 2)
            head_evict_v(0)
            head_split(0, 3)
            head_evict_r(0)
            derive(0)
            with act.Fori(1, GLA_HEADS) as h:
                g = h - 1
                head_split(h, 0)
                head_evict_qk(h)
                gla_kdT(g)
                head_split(h, 1)
                head_evict_ga(h)
                head_split(h, 2)
                gla_squares(g)
                head_evict_v(h)
                head_split(h, 3)
                gla_rs(g)
                head_evict_r(h)
                derive(h)

            g = GLA_HEADS - 1
            for j in range(2):
                split_hi(act, U_C + j + 1, (U_C + j + 1) % 2)
                for c in range(2):
                    b, full, _ = TL(U_C, 2 * j + c)
                    act.wait_ge(s_acc_full, full)
                    act.wait_ge(s_upad_zero, 1)
                    A(upad[:, 2 * j + c, PAD:PAD + L], acc[b][:, :], ACT.Copy).then_inc(s_acc_free[b], 1)
                if j == 0:
                    gla_kdT(g)
            for j in range(4):
                split_hi(act, U_C + 3 + j, (U_C + 3 + j) % 2, 4 * 2 * P if j == 3 else 16 * P)
                if j == 0:
                    gla_squares(g)
                if j == 1:
                    gla_rs(g)
                for c in range(2):
                    b, full, _ = TL(U_C, 4 + 2 * j + c)
                    act.wait_ge(s_acc_full, full)
                    act.wait_ge(s_der, 6 * GLA_HEADS)
                    A(gbm[:, 2 * j + c, :], acc[b][:, :], ACT.Sigmoid).then_inc(s_acc_free[b], 1)
            for g in range(NG):
                act.wait_ge(s_pooled, g + 1)
                A(phi[:, g, :], upad[:, g, PAD:PAD + L], ACT.Copy).then_inc(s_p_hi, 1)
            split_hi(act, U_BR, U_BR % 2)
            act.wait_ge(s_acc_full, first_tile(U_POOL))
            for k in range(KT):
                act.wait_ge(s_gfin, 2 * GLA_HEADS + 1)
                A(hhi[:, k, :], o_all[:, k, :], ACT.Copy).then_inc(s_o_hi, 1)
            for j in range(4):
                split_hi(act, U_BR + j + 1, (U_BR + j + 1) % 2)
                for c in range(2):
                    k = 2 * j + c
                    act.wait_ge(s_merged, k + 1)
                    A(mhi[:, k, :], sig_ga[:, k, :], ACT.Copy).then_inc(s_merge_hi, 1)
            for j in range(4):
                split_hi(act, U_OUT + j + 1, (U_OUT + j + 1) % 2)
                for k in (2 * j, 2 * j + 1):
                    act.wait_ge(*moved(U_OUT, k))
                    norm_square(1, k)

            norm_rs(1)
            norm_hi(1)
            with act.Fori(0, FT // 2) as i:
                for j in range(2):
                    v = U_FIN + 1 + j
                    split_hi(act, v + i * 2, v % 2, lin=first_tile(v - 1) + i * 4)
                    b, full, _ = TL(U_FIN, 2 * j, 4, i)
                    act.wait_ge(s_acc_full, full)
                    A(fsg[:, j, :], acc[b][:, :], ACT.Sigmoid).then_inc(s_f_sig, 1)
                    bu, _, free = TL(U_FIN, 2 * j + 1, 4, i)
                    act.wait_ge(s_acc_free[bu], free + 1)
                    A(cols(ahi, i * 2 + j), faa[:, j, :], ACT.Copy).then_inc(s_f_hi, 1)
            with act.Fori(0, 4) as i:
                for j in range(4):
                    v = U_FOUT + 1 + j
                    split_hi(act, v + i * 4, v % 2, FT // 2 * P if j < 3 else 16 * P, lin=first_tile(v - 1) + i * 4)
                    if j % 2:
                        k = i * 2 + j // 2
                        act.wait_ge(*moved(U_FOUT, j, 4, i))
                        act.wait_ge(s_norm_acc, k + nth(2))
                        A(fsg[:, 0, :], cols(xres, k), ACT.Square).then_inc(s_norm_sq, 1)
                        act.wait_ge(s_mid_acc, k + 1)
                        A(fsg[:, 1, :], cols(xres, k), ACT.Square, scale=col(vcol, k + R_NFIN)).then_inc(s_mid_sq, 1)

            nc.scalar.preload_act_table_set(LN_EXP)
            act.wait_ge(s_mid_step, 2)
            A(nsq[:, 1, :], nsq[:, 0, :], ACT.Ln).then_inc(s_mid_ln, 1)
            act.wait_ge(s_mid_ln, 1)
            A(nsq[:, 1, :], nsq[:, 1, :], ACT.Exp, scale=-0.5).then_inc(s_mid_rs, 1)
            norm_rs(2)
            act.wait_ge(s_mod, 3)
            norm_hi(2, shift=True)

            def att_split(i, j):
                v = U_ATT + 1 + j
                split_hi(act, v + i * 2, v % 2, lin=first_tile(v - 1) + i * 4)

            def att_copy(i, c, dst, scale=1.0):
                b, full, _ = TL(U_ATT, c, 4, i)
                act.wait_ge(s_acc_full, full)
                A(dst[:, :], acc[b][:, :], ACT.Copy, scale=scale).then_inc(s_acc_free[b], 1)

            def att_evict0(i, first=False):
                if later(i):
                    act.wait_ge(s_score, i * 8)
                att_copy(i, 0, aq, AE ** -0.5)
                att_copy(i, 1, ak)

            def att_evict1(i):
                if later(i):
                    act.wait_ge(s_av_tr, i)
                att_copy(i, 2, av)
                b, full, _ = TL(U_ATT, 3, 4, i)
                act.wait_ge(s_acc_full, full)
                if later(i):
                    act.wait_ge(s_a_out, i + 1)
                A(az[:, :], acc[b][:, :], ACT.Sigmoid).then_inc(s_az_sig, 1)

            def att_vt(g):
                act.wait_ge(s_av_tr, g + 1)
                A(avt[:, :, :].rearrange("p t v -> p (t v)"), M[3][:, :], ACT.Copy).then_inc(s_avt, 1)

            def att_exp(g, a):
                for q in range(TT):
                    n = (q + 1) * P
                    act.wait_ge(s_amax, g * 8 + a * 4 + q + 1)
                    A(apr[:, a, q, 0:n], apr[:, a, q, 0:n], ACT.Exp, bias=amax[:, a, q:q + 1],
                      accum_out=aden[:, a, q:q + 1]).then_inc(s_aexp, 1)

            def att_pt(g, a):
                act.wait_ge(s_apv, g * 2 + a + 1)
                for q in range(TT):
                    act.wait_ge(s_a_tr, g * 8 + a * 4 + q + 1)
                    A(apt[:, 0:q + 1, q * P:(q + 1) * P], M[q % 3][:, 0:(q + 1) * P].rearrange("p (j c) -> p j c", c=P),
                      ACT.Copy).then_inc(s_apt, 1)

            att_split(0, 0)
            att_evict0(0)
            att_split(0, 1)
            att_evict1(0)

            def att_iteration(i, units):
                g = i - 1
                if units:
                    att_split(i, 0)
                att_vt(g)
                att_exp(g, 0)
                att_pt(g, 0)
                if units:
                    att_evict0(i)
                    att_split(i, 1)
                att_exp(g, 1)
                att_pt(g, 1)
                if units:
                    att_evict1(i)

            with act.Fori(1, A_HEADS // 2) as i:
                att_iteration(i, True)
            att_iteration(A_HEADS // 2, False)

            def hg_split(h, j):
                v = U_HG + 1 + j
                split_hi(act, v + h * 2, v % 2, lin=first_tile(v - 1) + h * 4)

            def hg_evict_f(h):
                b, full, _ = TL(U_HG, 1, 4, h)
                act.wait_ge(s_acc_full, full)
                if later(h):
                    act.wait_ge(s_h_b, h)
                A(hf[:, :], acc[b][:, :], ACT.Sigmoid).then_inc(s_acc_free[b], 1)

            def hg_evict_q(h):
                b, full, _ = TL(U_HG, 0, 4, h)
                act.wait_ge(s_acc_full, full)
                if later(h):
                    act.wait_ge(s_h_op, h * 2)
                    act.wait_ge(s_h_w, h * 7)
                    act.wait_ge(s_h_score, h * 8 - 7)
                A(hq[:, :], acc[b][:, :], ACT.Sigmoid).then_inc(s_hq_sig, 1)

            def hg_evict_i(g):
                b, full, _ = TL(U_HG, 2, 4, g)
                act.wait_ge(s_acc_full, full)
                A(hi_[:, :], acc[b][:, :], ACT.Copy).then_inc(s_acc_free[b], 1)

            def hg_evict_z(g):
                b, full, _ = TL(U_HG, 3, 4, g)
                act.wait_ge(s_acc_full, full)
                if later(g):
                    act.wait_ge(s_h_out, g + 1)
                A(hz[:, :], acc[b][:, :], ACT.Sigmoid).then_inc(s_hz_sig, 1)

            def hg_factors(g):
                nc.scalar.preload_act_table_set(LN_EXP)
                act.wait_ge(s_h_fg, g * 2 + 2)
                A(hf[:, :], hf[:, :], ACT.Ln).then_inc(s_h_ln, 1)
                act.wait_ge(s_h_df, g * 8 + 1)
                A(hkd[:, :], hkd[:, :], ACT.Exp).then_inc(s_h_ex, 1)
                act.wait_ge(s_h_b, g + 1)
                A(dec[:, 0, 0:TT], hb[:, :].rearrange("p (n c) -> p n c", c=P)[:, :, P - 1], ACT.Exp)\
                    .then_inc(s_h_ex, 1)
                for lev in range(LEVELS):
                    act.wait_ge(s_h_df, g * 8 + 2 + lev)
                    A(hw[:, lev, :], hw[:, lev, :], ACT.Exp).then_inc(s_h_lex, 1)

            def hg_query(g):
                if later(g):
                    act.wait_ge(s_h_o, g)
                A(hqe[:, :], hb[:, :], ACT.Exp).then_inc(s_h_ex, 1)

            def hg_copies(g):
                act.wait_ge(s_h_itr, g + 1)
                A(hit[:, :, :].rearrange("p t v -> p (t v)"), M[0][:, :], ACT.Copy).then_inc(s_h_cp, 1)
                act.wait_ge(s_h_ktr, g + 1)
                A(hkT[:, :, :].rearrange("p t k -> p (t k)"), M[1][:, :], ACT.Copy).then_inc(s_h_cp, 1)

            def hg_square(g):
                act.wait_ge(s_h_o, g + 1)
                A(hsq[:, :], M[2][:, :], ACT.Square).then_inc(s_h_sq, 1)

            def hg_rs(g):
                act.wait_ge(s_h_sum, g + 1)
                A(hrs[:, :], M[3][:, :], ACT.Ln, bias=eps_col[:, :]).then_inc(s_h_rl, 1)
                act.wait_ge(s_h_rl, g + 1)
                A(hrs[:, :], hrs[:, :], ACT.Exp, scale=-0.5).then_inc(s_h_rs, 1)

            act.wait_ge(s_a_out, A_HEADS // 2 + 1)
            hg_split(0, 0)
            hg_evict_q(0)
            hg_evict_f(0)
            hg_split(0, 1)

            def gate_evict(k):
                b, full, _ = TL(U_G2, k)
                act.wait_ge(s_acc_full, full)
                A((sga if k < KT else sgb)[:, k % KT, :], acc[b][:, :], ACT.Sigmoid).then_inc(s_acc_free[b], 1)

            def hg_iteration(g, last=False):
                hg_factors(g)
                hg_evict_i(g)
                if later(g):
                    hg_square(g - 1)
                if last:
                    split_hi(act, U_G2 + 1, 1)
                else:
                    hg_split(g + 1, 0)
                if later(g):
                    hg_rs(g - 1)
                hg_query(g)
                hg_evict_z(g)
                if last:
                    split_hi(act, U_G2 + 2, 0)
                    gate_evict(0)
                    gate_evict(1)
                    hg_copies(g)
                    gate_evict(2)
                    gate_evict(3)
                else:
                    hg_split(g + 1, 1)
                    hg_evict_f(g + 1)
                    hg_copies(g)
                    hg_evict_q(g + 1)

            hg_iteration(0)
            with act.Fori(1, H_HEADS - 1) as g:
                hg_iteration(g)
            hg_iteration(H_HEADS - 1, last=True)
            hg_square(H_HEADS - 1)

            for j in range(2, 8):
                split_hi(act, U_G2 + j + 1, (j + 1) % 2)
                gate_evict(2 * j)
                if j == 2:
                    hg_rs(H_HEADS - 1)
                gate_evict(2 * j + 1)
                if j == 5:
                    act.wait_ge(s_h_out, H_HEADS + 1)
                    for k in range(AW // P):
                        A(oahi[:, k, :], oa[:, k, :], ACT.Copy).then_inc(s_oa_hi, 1)
            for k in range(KT):
                A(hhi[:, k, :], ob[:, k, :], ACT.Copy).then_inc(s_ob_hi, 1)
            for u in range(U_BA, U_OUT2):
                split_hi(act, u + 1, (u + 1) % 2)
                if u >= U_BB:
                    for c in range(2):
                        k = 2 * (u - U_BB) + c
                        act.wait_ge(s_merge2, k + 1)
                        A(nhi[:, k, :], sgb[:, k, :], ACT.Copy).then_inc(s_n_hi, 1)
            for u in range(U_OUT2, U_END - 1):
                split_hi(act, u + 1, (u + 1) % 2)
                for k in (2 * (u - U_OUT2), 2 * (u - U_OUT2) + 1):
                    act.wait_ge(*moved(U_OUT2, k))
                    norm_square(3, k)
            for k in (KT - 2, KT - 1):
                act.wait_ge(*moved(U_OUT2, k))
                norm_square(3, k)
            norm_rs(3)
            for t in range(TT):
                for c in range(2):
                    act.wait_ge(s_y_tr, 2 * t + c + 1)
                    A(ynat[:, t, c * L:(c + 1) * L], M[(2 * t + c) % 4][:, :], ACT.Copy).then_inc(s_y_nat, 1)

        @block.vector
        def _(dve):
            V = nc.vector

            def hold():
                V.memset(tick[:, 0:1], 0.0)

            for n, started in enumerate((s_gfin, s_a_out, s_apv, s_h_out, s_h_rs)):
                V.memset(tick[:, n + 1:n + 2], 0.0).then_inc(started, 1)
            V.memset(eps_col[:, :], EPS).then_inc(s_eps, 1)
            V.memset(one_col[:, :], 1.0).then_inc(s_means, 1)
            for t, width in ((mean_dm, DM), (mean_dv, DV), (mean_p, P)):
                V.memset(t[:, :], 1.0 / width).then_inc(s_means, 1)
            V.memset(rst[:, :], 1.0).then_inc(s_rst, 1)
            dve.wait_ge(s_rst, 1)
            V.memset(rst[:, :].rearrange("p (n c) -> p n c", c=CHUNK)[:, :, 0], 0.0).then_inc(s_rst, 1)

            dve.wait_ge(s_vcol, 1)
            lb0, lb1 = vcol[:, R_LB0:R_LB0 + 8], vcol[:, R_LB1:R_LB1 + 8]
            V.tensor_tensor(lbt[:, 2, :], lb0, lb1, ALU.max).then_inc(s_lb_m, 1)
            dve.wait_ge(s_lb_m, 1)
            V.tensor_tensor(lbt[:, 3, :], lb0, lbt[:, 2, :], ALU.subtract).then_inc(s_lb_d, 1)
            V.tensor_tensor(lbt[:, 4, :], lb1, lbt[:, 2, :], ALU.subtract).then_inc(s_lb_d, 1)
            dve.wait_ge(s_csig, 1)
            V.tensor_tensor(silu_c, vcol[:, R_C:R_C + KT], small[:, 24:32], ALU.mult).then_inc(s_silu_c, 1)
            dve.wait_ge(s_lb_e, 1)
            V.tensor_tensor(lbt[:, 5, :], lbt[:, 3, :], lbt[:, 4, :], ALU.add).then_inc(s_lb_s, 1)
            dve.wait_ge(s_lb_s, 1)
            V.reciprocal(lbt[:, 5, :], lbt[:, 5, :]).then_inc(s_lb_s, 1)
            dve.wait_ge(s_lb_s, 2)
            V.tensor_tensor(lbt[:, 0, :], lbt[:, 3, :], lbt[:, 5, :], ALU.mult).then_inc(s_lb, 1)
            dve.wait_ge(s_lb, 1)
            V.tensor_scalar(lbt[:, 1, :], lbt[:, 0, :], -1.0, 1.0, ALU.mult, ALU.add).then_inc(s_lb, 1)

            def norm_zero(n):
                V.memset(nacc[:, :], 0.0).then_inc(s_norm_zero, 1)

            def norm_add(n, k):
                dve.wait_ge(s_norm_sq, nth(n) + k + 1)
                if k == 0:
                    dve.wait_ge(s_norm_zero, n + 1)
                if nth(n) + k > 0:
                    dve.wait_ge(s_norm_acc, nth(n) + k)
                V.tensor_tensor(nacc[:, :], nacc[:, :], nsq[:, k % 2, :], ALU.add).then_inc(s_norm_acc, 1)

            def norm_split(n, g, rs=nrs, shift=False):
                def low(k):
                    dve.wait_ge(s_norm_hi, nth(n) + k + 1)
                    h = hhi[:, k, :].bitcast(f32)
                    if shift:
                        V.scalar_tensor_tensor(hlo[:, k, :], nht[:, k % 2, :], mod[:, k:k + 1], h, ALU.add,
                                               ALU.subtract).then_inc(s_norm_lo, 1)
                    else:
                        V.tensor_tensor(hlo[:, k, :], nht[:, k % 2, :], h, ALU.subtract).then_inc(s_norm_lo, 1)
                for k in range(KT):
                    if k > 1:
                        dve.wait_ge(s_norm_lo, nth(n) + k - 1)
                    V.scalar_tensor_tensor(nht[:, k % 2, :], xres[:, k, :], g(k), rs[:, :], ALU.mult, ALU.mult)\
                        .then_inc(s_norm_ht, 1)
                    if k >= 1:
                        low(k - 1)
                low(KT - 1)

            norm_zero(0)
            for k in range(KT):
                norm_add(0, k)
            dve.wait_ge(s_norm_rs, 1)
            norm_split(0, lambda k: vcol[:, R_NM + k:R_NM + k + 1])

            for i in range(8):
                dve.wait_ge(s_la_abs, i + 1)
                V.tensor_scalar(lt[:, 1, i % 2, :], M[i % 4][:, :], vcol[:, R_BF + i:R_BF + i + 1], 0.0,
                                ALU.add, ALU.min).then_inc(s_la_min, 1)
                dve.wait_ge(s_la_ln, i + 1)
                dve.wait_ge(s_la_min, i + 1)
                V.tensor_tensor(lt[:, 1, i % 2, :], lt[:, 1, i % 2, :], lt[:, 0, i % 2, :], ALU.subtract)\
                    .then_inc(s_la, 1)
                dve.wait_ge(s_la, i + 1)
                dve.wait_ge(s_rst, 2)
                o, a = (b_all[:, i, :], lt[:, 1, i % 2, :]) if i < 4 else (b_all[:, i, ::-1], lt[:, 1, i % 2, ::-1])
                V.tensor_tensor_scan(o, rst[:, :], a, 0.0, ALU.mult, ALU.add).then_inc(s_b_ready, 1)

            def gla_derive(h):
                dve.wait_ge(*moved(U_HEAD, 0, 8, h))
                dve.wait_ge(*moved(U_HEAD, 1, 8, h))
                dve.wait_ge(s_b_ready, 8)
                for d in range(2):
                    b = cols(b_all, h + 4 * d).rearrange("p (n c) -> p n c", c=CHUNK)
                    e = CHUNK - 1 if d == 0 else 0
                    last = b[:, :, e:e + 1].to_broadcast([P, NCH, CHUNK])
                    if later(h * 6 + 3 * d):
                        dve.wait_ge(s_der, h * 6 + 3 * d)
                    V.tensor_tensor(ex[:, 2, :].rearrange("p (n c) -> p n c", c=CHUNK), last, b, ALU.subtract)\
                        .then_inc(s_gdf, 1)
                    dve.wait_ge(s_gex, h * 6 + 3 * d + 1)
                    V.tensor_tensor(qe[:, d, :], gq[:, :], ex[:, 0, :], ALU.mult).then_inc(s_der, 1)
                    dve.wait_ge(s_gex, h * 6 + 3 * d + 2)
                    V.tensor_tensor(ke[:, d, :], gk[:, :], ex[:, 1, :], ALU.mult).then_inc(s_der, 1)
                    dve.wait_ge(s_gex, h * 6 + 3 * d + 3)
                    V.tensor_tensor(kd[:, d, :], gk[:, :], ex[:, 2, :], ALU.mult).then_inc(s_der, 1)

            def head_r(h):
                for c in range(2):
                    b, _, _ = TL(U_HEAD, 6 + c, 8, h)
                    dve.wait_ge(s_r_sig, h * 2 + c + 1)
                    V.tensor_tensor(gr[:, c, :], gr[:, c, :], acc[b][:, :], ALU.mult).then_inc(s_acc_free[b], 1)

            def gla_mask(g):
                V.memset(ga_sc[:, :, :], 0.0).then_inc(s_gmask, 1)
                for d in range(2):
                    dve.wait_ge(s_gsc, g * 2 + d + 1)
                    dve.wait_ge(s_gmask, g * 3 + d + 1)
                    dve.wait_ge(s_masks, 1)
                    hold()
                    m = masks[:, d:d + 1, :].to_broadcast([P, TT, P])
                    V.copy_predicated(ga_sc[:, :, :], m, M[2 + d][:, :].rearrange("p (t c) -> p t c", c=P))\
                        .then_inc(s_gmask, 1)

            def gla_states(g):
                for s in range(NCH - 1):
                    for d in range(2):
                        kv = M[2 * d + s % 2][:, 0:DV]
                        dve.wait_ge(s_kv, g * 14 + 2 * s + d + 1)
                        if s == 0:
                            V.tensor_copy(st[:, d, 0, :], kv).then_inc(s_gst, 1)
                        else:
                            n = s if d == 0 else NCH - 1 - s
                            dve.wait_ge(s_gst, g * 14 + 2 * s + d - 1)
                            dve.wait_ge(s_gdec, g * 2 + d + 1)
                            V.scalar_tensor_tensor(st[:, d, s, :], st[:, d, s - 1, :], dec[:, d, n:n + 1], kv,
                                                   ALU.mult, ALU.add).then_inc(s_gst, 1)

            def gla_final(g):
                dve.wait_ge(s_grs, g + 1)
                for j in range(2):
                    V.scalar_tensor_tensor(ex[:, j, :], M[j][:, :], col(vcol, g * 2 + (R_GN + j)), ex[:, 2, :],
                                           ALU.mult, ALU.mult).then_inc(s_gt, 1)
                for j in range(2):
                    b, _, free = TL(U_HEAD, 6 + j, 8, g)
                    dve.wait_ge(s_gt, g * 2 + j + 1)
                    dve.wait_ge(s_acc_free[b], free + 1)
                    V.tensor_tensor(cols(o_all, g * 2 + j), ex[:, j, :], gr[:, j, :], ALU.mult)\
                        .then_inc(s_gfin, 1)

            head_r(0)
            gla_derive(0)
            with dve.Fori(1, GLA_HEADS) as h:
                gla_mask(h - 1)
                gla_states(h - 1)
                gla_final(h - 1)
                head_r(h)
                gla_derive(h)
            g = GLA_HEADS - 1
            V.memset(upad[:, :, :], 0.0).then_inc(s_upad_zero, 1)
            gla_mask(g)
            gla_states(g)
            gla_final(g)

            n_adds = 0
            for g, w in enumerate(POOL_WINDOWS):
                dve.wait_ge(*moved(U_C, g))
                dve.wait_ge(s_gfin, 2 * GLA_HEADS + 1)
                if g > 0:
                    dve.wait_ge(s_pool_mid, g)
                if g > 0:
                    dve.wait_ge(s_pool_side, g)
                if g > 0:
                    dve.wait_ge(s_pooled, g)
                src, n, step, flip = upad[:, g, :], L + 2 * PAD, 1, 0
                while step < w:
                    n -= step
                    dst = (ptmp, ptmp2)[flip][:, 0:n]
                    V.tensor_tensor(dst, src[:, 0:n], src[:, step:step + n], ALU.add).then_inc(s_pool_add, 1)
                    n_adds += 1
                    dve.wait_ge(s_pool_add, n_adds)
                    src, flip, step = dst, 1 - flip, step * 2
                sums = src[:, PAD - w // 2:PAD - w // 2 + L]
                edges = (ptmp, ptmp2)[flip]
                dve.wait_ge(s_edge_in, 16)
                for side, c0 in ((0, 0), (1, L - PAD)):
                    V.tensor_tensor(edges[:, side * PAD:(side + 1) * PAD], sums[:, c0:c0 + PAD],
                                    edge[:, g, side * PAD:(side + 1) * PAD], ALU.mult).then_inc(s_pool_edge, 1)
                u = upad[:, g, PAD:PAD + L]
                V.scalar_tensor_tensor(u[:, PAD:L - PAD], sums[:, PAD:L - PAD], 1.0 / w, u[:, PAD:L - PAD],
                                       ALU.mult, ALU.subtract).then_inc(s_pool_mid, 1)
                dve.wait_ge(s_pool_edge, 2 * g + 2)
                for side, c0 in ((0, 0), (1, L - PAD)):
                    V.tensor_tensor(u[:, c0:c0 + PAD], edges[:, side * PAD:(side + 1) * PAD], u[:, c0:c0 + PAD],
                                    ALU.subtract).then_inc(s_pool_side if side == 0 else s_pooled, 1)
            for g in range(NG):
                dve.wait_ge(s_p_hi, g + 1)
                dve.wait_ge(s_pool_mid, g + 1)
                dve.wait_ge(s_pool_side, g + 1)
                dve.wait_ge(s_pooled, g + 1)
                V.tensor_tensor(plo[:, g, :], upad[:, g, PAD:PAD + L], phi[:, g, :].bitcast(f32), ALU.subtract)\
                    .then_inc(s_p_lo, 1)
            for k in range(KT):
                dve.wait_ge(s_o_hi, k + 1)
                V.tensor_tensor(hlo[:, k, :], o_all[:, k, :], hhi[:, k, :].bitcast(f32), ALU.subtract)\
                    .then_inc(s_o_lo, 1)
            for k in range(KT):
                b, full, free = TL(U_POOL, k)
                dve.wait_ge(s_acc_full, full)
                dve.wait_ge(*moved(U_C, 4 + k))
                V.scalar_tensor_tensor(gbm[:, k, :], acc[b][:, :], vcol[:, R_PS + k:R_PS + k + 1], gbm[:, k, :],
                                       ALU.mult, ALU.mult).then_inc(s_acc_free[b], 1)
            for k in range(KT):
                b, full, free = TL(U_BR, k)
                dve.wait_ge(s_acc_full, full)
                V.tensor_tensor(sig_ga[:, k, :], sig_ga[:, k, :], acc[b][:, :], ALU.mult)\
                    .then_inc(s_acc_free[b], 1)
                dve.wait_ge(s_acc_free[b], free + 1)
                V.tensor_tensor(sig_ga[:, k, :], sig_ga[:, k, :], gbm[:, k, :], ALU.add).then_inc(s_merged, 1)
                dve.wait_ge(s_merge_hi, k + 1)
                V.tensor_tensor(mlo[:, k, :], sig_ga[:, k, :], mhi[:, k, :].bitcast(f32), ALU.subtract)\
                    .then_inc(s_merge_lo, 1)
            norm_zero(1)
            dve.wait_ge(s_x_back, 16)
            for k in range(KT):
                b, full, free = TL(U_OUT, k)
                dve.wait_ge(s_acc_full, full)
                V.tensor_tensor(xres[:, k, :], xres[:, k, :], acc[b][:, :], ALU.add).then_inc(s_acc_free[b], 1)
                norm_add(1, k)

            dve.wait_ge(s_norm_rs, 2)
            norm_split(1, lambda k: vcol[:, R_NF + k:R_NF + k + 1])

            def ada_tile(n, slot):
                w = ada[:, slot, :, :]
                dve.wait_ge(s_ada_in[slot], (n - slot) * 8 + 16)
                V.tensor_tensor(w, w, silu_c.rearrange("p (k o) -> p k o", o=1).to_broadcast([P, KT, P]), ALU.mult)\
                    .then_inc(s_ada_step, 1)
                dve.wait_ge(s_ada_step, n * 3 + 1)
                V.tensor_tensor(w[:, 0:4, :], w[:, 0:4, :], w[:, 4:8, :], ALU.add).then_inc(s_ada_step, 1)
                dve.wait_ge(s_ada_step, n * 3 + 2)
                V.tensor_tensor(w[:, 0:2, :], w[:, 0:2, :], w[:, 2:4, :], ALU.add).then_inc(s_ada_step, 1)
                dve.wait_ge(s_ada_step, n * 3 + 3)
                V.tensor_tensor(w[:, 0, :], w[:, 0, :], w[:, 1, :], ALU.add).then_inc(s_ada_sum, 1)

            dve.wait_ge(s_silu_c, 1)
            with dve.Fori(0, FT // 2) as i:
                for j in range(2):
                    ada_tile(i * 2 + j, j)
                    bg, _, gfree = TL(U_FIN, 2 * j, 4, i)
                    bu, full, ufree = TL(U_FIN, 2 * j + 1, 4, i)
                    dve.wait_ge(s_f_sig, i * 2 + j + 1)
                    V.tensor_tensor(fsg[:, j, :], fsg[:, j, :], acc[bg][:, :], ALU.mult)\
                        .then_inc(s_acc_free[bg], 1)
                    dve.wait_ge(s_acc_full, full)
                    dve.wait_ge(s_acc_free[bg], gfree + 1)
                    V.tensor_tensor(faa[:, j, :], fsg[:, j, :], acc[bu][:, :], ALU.mult)\
                        .then_inc(s_acc_free[bu], 1)
                    dve.wait_ge(s_f_hi, i * 2 + j + 1)
                    V.tensor_tensor(cols(alo, i * 2 + j), faa[:, j, :], cols(ahi, i * 2 + j).bitcast(f32),
                                    ALU.subtract).then_inc(s_f_lo, 1)
            dve.wait_ge(s_f_lo, FT)
            V.memset(faa[:, 0, :], 0.0).then_inc(s_norm_zero, 1)
            V.memset(faa[:, 1, :], 0.0).then_inc(s_mid_acc, 1)
            dve.wait_ge(s_norm_zero, 3)

            def ffn_out(i):
                for j in range(4):
                    b, full, _ = TL(U_FOUT, j, 4, i)
                    dve.wait_ge(s_acc_full, full)
                    if j:
                        dve.wait_ge(s_acc_free[(b - 1) % 4], TL(U_FOUT, j - 1, 4, i)[2] + 1)
                    x = cols(xres, i * 2 + j // 2)
                    V.tensor_tensor(x, x, acc[b][:, :], ALU.add).then_inc(s_acc_free[b], 1)
                    if j % 2:
                        k = i * 2 + j // 2
                        dve.wait_ge(s_norm_sq, k + (nth(2) + 1))
                        dve.wait_ge(s_norm_acc, k + nth(2))
                        V.tensor_tensor(faa[:, 0, :], faa[:, 0, :], fsg[:, 0, :], ALU.add).then_inc(s_norm_acc, 1)
                        dve.wait_ge(s_mid_sq, k + 1)
                        dve.wait_ge(s_mid_acc, k + 1)
                        V.tensor_tensor(faa[:, 1, :], faa[:, 1, :], fsg[:, 1, :], ALU.add).then_inc(s_mid_acc, 1)

            ffn_out(0)
            ada_tile(FT, 0)
            ada_tile(FT + 1, 1)
            dve.wait_ge(s_ada_used, FT + 2)
            V.tensor_tensor(mod[:, :], M[2][:, 0:24], vcol[:, R_ADA:R_ADA + 24], ALU.add).then_inc(s_mod, 1)
            dve.wait_ge(s_mod, 1)
            V.scalar_tensor_tensor(g2_col, mod[:, KT:2 * KT], 1.0, vcol[:, R_NG2:R_NG2 + KT], ALU.add, ALU.mult)\
                .then_inc(s_mod, 1)
            dve.wait_ge(s_mod, 2)
            V.tensor_tensor(mid_col, g2_col, vcol[:, R_NFIN:R_NFIN + KT], ALU.mult).then_inc(s_mod, 1)
            with dve.Fori(1, 4) as i:
                ffn_out(i)

            dve.wait_ge(s_norm_sum, 3)
            dve.wait_ge(s_mid_sum, 1)
            V.tensor_scalar(nsq[:, 0, :], M[3][:, :], EPS, EPS * EPS, ALU.mult, ALU.add).then_inc(s_mid_step, 1)
            dve.wait_ge(s_mid_step, 1)
            V.tensor_tensor(nsq[:, 0, :], nsq[:, 0, :], M[1][:, :], ALU.add).then_inc(s_mid_step, 1)
            dve.wait_ge(s_mid_rs, 1)
            dve.wait_ge(s_mod, 3)
            norm_split(2, lambda k: small[:, k:k + 1], nsq[:, 1, :], shift=True)
            dve.wait_ge(s_norm_rs, 3)
            dve.wait_ge(s_norm_ht, nth(2) + KT)
            for k in range(KT):
                V.scalar_tensor_tensor(xres[:, k, :], xres[:, k, :], vcol[:, R_NFIN + k:R_NFIN + k + 1], nrs[:, :],
                                       ALU.mult, ALU.mult).then_inc(s_x_mid, 1)

            def att_logits(g, a):
                dve.wait_ge(s_bias_in, g * 32 + 32)
                for q in range(TT):
                    n = (q + 1) * P
                    dve.wait_ge(s_score, g * 8 + a * 4 + q + 1)
                    hold()
                    V.tensor_tensor_reduce(out=apr[:, a, q, 0:n], in0=M[q][:, 0:n], in1=abias[:, a, n - 1::-1],
                                           scale=1.0, scalar=NEG_INF, op0=ALU.add, op1=ALU.max,
                                           accum_out=amax[:, a, q:q + 1]).then_inc(s_logit, 1)
                    dve.wait_ge(s_logit, g * 8 + a * 4 + q + 1)
                    V.tensor_scalar(amax[:, a, q:q + 1], amax[:, a, q:q + 1], -1.0, None, ALU.mult)\
                        .then_inc(s_amax, 1)

            def att_normalise(g, a):
                for q in range(TT):
                    n = (q + 1) * P
                    dve.wait_ge(s_aexp, g * 8 + a * 4 + q + 1)
                    V.reciprocal(aden[:, a, q:q + 1], aden[:, a, q:q + 1]).then_inc(s_arec, 1)
                    dve.wait_ge(s_arec, g * 8 + a * 4 + q + 1)
                    V.tensor_scalar(apr[:, a, q, 0:n], apr[:, a, q, 0:n], aden[:, a, q:q + 1], None, ALU.mult)\
                        .then_inc(s_aprob, 1)

            def att_out(g):
                dve.wait_ge(s_apv, g * 2 + 3)
                b, _, free = TL(U_ATT, 3, 4, g)
                dve.wait_ge(s_acc_free[b], free + 1)
                V.tensor_tensor(cols(oa, g), az[:, :], M[3][:, :], ALU.mult).then_inc(s_a_out, 1)

            def att_z(i):
                b, _, _ = TL(U_ATT, 3, 4, i)
                dve.wait_ge(s_az_sig, i + 1)
                V.tensor_tensor(az[:, :], az[:, :], acc[b][:, :], ALU.mult).then_inc(s_acc_free[b], 1)

            def att_head_pair(g):
                att_logits(g, 0)
                att_normalise(g, 0)
                att_logits(g, 1)
                att_normalise(g, 1)
                att_out(g)

            att_z(0)
            with dve.Fori(1, A_HEADS // 2) as i:
                att_head_pair(i - 1)
                att_z(i)
            att_head_pair(A_HEADS // 2 - 1)

            V.memset(hrst[:, :], 1.0).then_inc(s_hrst, 1)
            dve.wait_ge(s_hrst, 1)
            V.memset(hrst[:, :].rearrange("p (n c) -> p n c", c=P)[:, :, 0], 0.0).then_inc(s_hrst, 1)

            def hg_gate(dst, sigmoid, c, h):
                b, _, _ = TL(U_HG, c, 4, h)
                dve.wait_ge(sigmoid, h + 1)
                V.tensor_tensor(dst[:, :], dst[:, :], acc[b][:, :], ALU.mult).then_inc(s_acc_free[b], 1)

            def hg_factors(g):
                dve.wait_ge(*moved(U_HG, 0, 4, g))
                dve.wait_ge(*moved(U_HG, 1, 4, g))
                dve.wait_ge(s_lb, 2)
                V.tensor_scalar(hf[:, :], hf[:, :], col(lbt[:, 1, :], g), col(lbt[:, 0, :], g), ALU.mult, ALU.add)\
                    .then_inc(s_h_fg, 1)
                dve.wait_ge(s_h_fg, g * 2 + 1)
                V.tensor_scalar(hk[:, :], hf[:, :], -1.0, 1.0, ALU.mult, ALU.add).then_inc(s_h_fg, 1)
                dve.wait_ge(s_h_ln, g + 1)
                dve.wait_ge(s_hrst, 2)
                V.tensor_tensor_scan(hb[:, :], hrst[:, :], hf[:, :], 0.0, ALU.mult, ALU.add).then_inc(s_h_b, 1)
                dve.wait_ge(s_h_b, g + 1)
                b = hb[:, :].rearrange("p (n c) -> p n c", c=P)
                V.tensor_tensor(hkd[:, :].rearrange("p (n c) -> p n c", c=P),
                                b[:, :, P - 1:P].to_broadcast([P, TT, P]), b, ALU.subtract).then_inc(s_h_df, 1)
                for lev in range(LEVELS):
                    half = 1 << lev
                    nb = L // (2 * half)
                    bb = hb[:, :].rearrange("p (n c) -> p n c", c=2 * half)
                    ww = hw[:, lev, :].rearrange("p (n c) -> p n c", c=2 * half)
                    mid = bb[:, :, half - 1:half].to_broadcast([P, nb, half])
                    V.tensor_tensor(ww[:, :, 0:half], mid, bb[:, :, 0:half], ALU.subtract).then_inc(s_h_dl, 1)
                    V.tensor_tensor(ww[:, :, half:], bb[:, :, half:], mid, ALU.subtract).then_inc(s_h_df, 1)
                dve.wait_ge(s_h_ex, g * 3 + 1)
                dve.wait_ge(s_h_fg, g * 2 + 2)
                V.tensor_tensor(hkd[:, :], hkd[:, :], hk[:, :], ALU.mult).then_inc(s_h_op, 1)
                for lev in range(LEVELS):
                    half = 1 << lev
                    v3 = lambda t: t.rearrange("p (n c) -> p n c", c=2 * half)
                    ww = v3(hw[:, lev, :])
                    dve.wait_ge(s_h_lex, g * 7 + lev + 1)
                    V.tensor_tensor(ww[:, :, 0:half], ww[:, :, 0:half], v3(hk[:, :])[:, :, 0:half], ALU.mult)\
                        .then_inc(s_h_wl, 1)
                    V.tensor_tensor(ww[:, :, half:], ww[:, :, half:], v3(hq[:, :])[:, :, half:], ALU.mult)\
                        .then_inc(s_h_w, 1)

            def hg_query(g):
                dve.wait_ge(s_h_ex, g * 3 + 3)
                V.tensor_tensor(hqe[:, :], hqe[:, :], hq[:, :], ALU.mult).then_inc(s_h_op, 1)

            def hg_mask(g):
                V.memset(hsc[:, :, :], 0.0).then_inc(s_h_mask, 1)
                for n in range(LEVELS + 1):
                    dve.wait_ge(s_h_score, g * 8 + n + 1)
                    dve.wait_ge(s_h_mask, g * 9 + n + 1)
                    dve.wait_ge(s_masks, 1)
                    hold()
                    lev = (LEVELS, *range(LEVELS))[n]
                    m = masks[:, 2 + lev:3 + lev, :].to_broadcast([P, TT, P])
                    V.copy_predicated(hsc[:, :, :], m, M[(n + 2) % 4][:, :].rearrange("p (t c) -> p t c", c=P))\
                        .then_inc(s_h_mask, 1)

            def hg_states(g):
                dve.wait_ge(s_h_kv, g + 1)
                dve.wait_ge(s_h_ex, g * 3 + 2)
                for n in range(TT - 1):
                    kv = M[3][:, n * P:(n + 1) * P]
                    if n == 0:
                        V.tensor_copy(hst[:, 0, :], kv).then_inc(s_h_st, 1)
                    else:
                        dve.wait_ge(s_h_st, g * 3 + n)
                        V.scalar_tensor_tensor(hst[:, n, :], hst[:, n - 1, :], dec[:, 0, n:n + 1], kv, ALU.mult,
                                               ALU.add).then_inc(s_h_st, 1)

            def hg_final(g):
                dve.wait_ge(s_h_rs, g + 2)
                V.scalar_tensor_tensor(hsq[:, :], M[2][:, :], vcol[:, R_ON:R_ON + 1], hrs[:, :], ALU.mult, ALU.mult)\
                    .then_inc(s_h_t, 1)
                dve.wait_ge(s_h_t, g + 1)
                b, _, free = TL(U_HG, 3, 4, g)
                dve.wait_ge(s_acc_free[b], free + 1)
                V.tensor_tensor(cols(ob, g), hsq[:, :], hz[:, :], ALU.mult).then_inc(s_h_out, 1)

            hg_gate(hq, s_hq_sig, 0, 0)

            def hg_iteration(g, last=False):
                hg_factors(g)
                if later(g):
                    hg_final(g - 1)
                hg_query(g)
                hg_gate(hz, s_hz_sig, 3, g)
                hg_mask(g)
                hg_states(g)
                if not last:
                    hg_gate(hq, s_hq_sig, 0, g + 1)

            hg_iteration(0)
            with dve.Fori(1, H_HEADS - 1) as g:
                hg_iteration(g)
            hg_iteration(H_HEADS - 1, last=True)
            hg_final(H_HEADS - 1)

            for k in range(AW // P):
                dve.wait_ge(s_oa_hi, k + 1)
                V.tensor_tensor(oalo[:, k, :], oa[:, k, :], oahi[:, k, :].bitcast(f32), ALU.subtract)\
                    .then_inc(s_oa_lo, 1)
            for k in range(KT):
                dve.wait_ge(s_ob_hi, k + 1)
                V.tensor_tensor(hlo[:, k, :], ob[:, k, :], hhi[:, k, :].bitcast(f32), ALU.subtract)\
                    .then_inc(s_ob_lo, 1)
            for k in range(KT):
                b, full, _ = TL(U_BA, k)
                dve.wait_ge(s_acc_full, full)
                dve.wait_ge(*moved(U_G2, k))
                V.tensor_tensor(sga[:, k, :], sga[:, k, :], acc[b][:, :], ALU.mult).then_inc(s_acc_free[b], 1)
            for k in range(KT):
                b, full, free = TL(U_BB, k)
                dve.wait_ge(s_acc_full, full)
                dve.wait_ge(*moved(U_G2, KT + k))
                V.tensor_tensor(sgb[:, k, :], sgb[:, k, :], acc[b][:, :], ALU.mult).then_inc(s_acc_free[b], 1)
                dve.wait_ge(s_acc_free[b], free + 1)
                dve.wait_ge(*moved(U_BA, k))
                V.tensor_tensor(sgb[:, k, :], sgb[:, k, :], sga[:, k, :], ALU.add).then_inc(s_merge2, 1)
                dve.wait_ge(s_n_hi, k + 1)
                V.tensor_tensor(nlo[:, k, :], sgb[:, k, :], nhi[:, k, :].bitcast(f32), ALU.subtract)\
                    .then_inc(s_n_lo, 1)
            norm_zero(3)
            dve.wait_ge(s_x_mid, KT)
            for k in range(KT):
                b, full, _ = TL(U_OUT2, k)
                dve.wait_ge(s_acc_full, full)
                V.scalar_tensor_tensor(xres[:, k, :], acc[b][:, :], mod[:, 2 * KT + k:2 * KT + k + 1], xres[:, k, :],
                                       ALU.mult, ALU.add).then_inc(s_acc_free[b], 1)
                norm_add(3, k)
            dve.wait_ge(s_norm_rs, 4)
            for k in range(KT):
                V.scalar_tensor_tensor(yT[:, k, :], xres[:, k, :], vcol[:, R_FG + k:R_FG + k + 1], nrs[:, :],
                                       ALU.mult, ALU.mult).then_inc(s_yT, 1)

        @block.gpsimd
        def _(pool):
            nc.gpsimd.memset(vrow[:, :], 0.0).then_inc(s_vrow_zero, 1)
            nc.gpsimd.memset(wup[:, :, :], 0.0).then_inc(s_vrow_zero, 1)
            nc.gpsimd.memset(relb[:, :], 1.0).then_inc(s_vrow_zero, 1)
            pool.wait_ge(s_mask_src, 16)
            nc.gpsimd.tensor_copy(masks[:, :, :], mask_src[:, :, :]).then_inc(s_masks, 1)
            split_lo(pool, 0, 0, KT * P)
            with pool.Fori(0, (U_POOL - 1) // 2) as i:
                split_lo(pool, i * 2 + 1, 1)
                split_lo(pool, i * 2 + 2, 0)
            split_lo(pool, U_POOL, 1, 4 * 2 * P)
            for start, end, n in ((U_BR, U_FOUT, 16 * P), (U_FOUT, U_ATT, FT // 2 * P), (U_ATT, U_END, 16 * P)):
                with pool.Fori(0, (end - start) // 2) as i:
                    split_lo(pool, i * 2 + start, 0, n)
                    split_lo(pool, i * 2 + start + 1, 1, n)

        @block.tensor
        def _(pe):
            mm = nc.tensor.matmul

            def tile(u0, c, slot, j, per=0, i=0, nk=KT, ncol=2 * P, xh=hhi, xl=hlo):
                b, _, free = TL(u0, c, per, i)
                if later(free):
                    pe.wait_ge(s_acc_free[b], free)
                pe_tile(b, slot, j, nk, ncol, xh, xl)

            def unit_as_ready(u0, slot, ready, base, per=2, xh=hhi, xl=hlo, nk=KT):
                banks = []
                for j in range(per):
                    b, _, free = TL(u0, j)
                    pe.wait_ge(s_acc_free[b], free)
                    banks.append(b)
                for k in range(nk):
                    pe.wait_ge(ready, base + k + 1)
                    for j, b in enumerate(banks):
                        o, js = acc[b][:, :], slice((k * per + j) * P, (k * per + j + 1) * P)
                        mm(o, whi[:, slot, js], xh[:, k, :], start=(k == 0), stop=False)
                        mm(o, whi[:, slot, js], xl[:, k, :], start=False, stop=False)
                        last = mm(o, wlo[:, slot, js], xh[:, k, :], start=False, stop=(k == nk - 1))
                        if k == nk - 1:
                            last.then_inc(s_acc_full, 1)

            def units(u0, n, xh=hhi, xl=hlo, nk=KT, ncol=2 * P, ready=None, base=0):
                per = ncol // P
                for m in range(n):
                    pe.wait_ge(s_unit_lo, u0 + m + 1)
                    if m == 0 and ready is not None:
                        unit_as_ready(u0, u0 % 2, ready, base, per, xh, xl, nk)
                        continue
                    for j in range(per):
                        tile(u0, per * m + j, (u0 + m) % 2, j, nk=nk, ncol=ncol, xh=xh, xl=xl)

            def norm_mean(n):
                pe.wait_ge(s_means, 4)
                pe.wait_ge(s_norm_acc, nth(n) + KT)
                if n == 2:
                    mm(M[3][:, :], mean_dm[:, :], faa[:, 0, :], start=True, stop=True).then_inc(s_norm_sum, 1)
                    pe.wait_ge(s_mid_acc, KT + 1)
                    mm(M[1][:, :], mean_dm[:, :], faa[:, 1, :], start=True, stop=True).then_inc(s_mid_sum, 1)
                else:
                    mm(M[3][:, :], mean_dm[:, :], nacc[:, :], start=True, stop=True).then_inc(s_norm_sum, 1)

            pe.wait_ge(s_id_in, 16)
            pe.wait_ge(s_rows_in, 13 * 16)
            nc.tensor.transpose(M[0][:, 0:P], vrow[:, :], ident[:, :]).then_inc(s_vcol_mm, 1)
            pe.wait_ge(s_bias_src, 32)
            mm(M[1][0:A_HEADS, :], relb[0:N_BUCKETS + 1, :], hot[:, 0:L], start=True, stop=True)\
                .then_inc(s_bias_mm, 1)
            mm(M[2][0:A_HEADS, 0:BW - L], relb[0:N_BUCKETS + 1, :], hot[:, L:BW], start=True, stop=True)\
                .then_inc(s_bias_mm, 1)
            pe.wait_ge(s_x_in, 16 * TT)
            pe.wait_ge(s_vcol, 1)
            pe.wait_ge(s_bias_row, 2)
            for k in range(KT):
                if k > 3:
                    pe.wait_ge(s_xT_out, k - 3)
                for t in range(TT):
                    last = nc.tensor.transpose(M[k % 4][:, t * P:(t + 1) * P], xnat[:, t, k * P:(k + 1) * P],
                                               ident[:, :])
                last.then_inc(s_xT, 1)
            pe.wait_ge(s_xT_out, KT)
            norm_mean(0)

            pe.wait_ge(s_unit_lo, 0 + 1)
            b, _, _ = TL(U_LR, 0)
            for k in range(KT):
                pe.wait_ge(s_norm_lo, k + 1)
                ks = slice(k * P, (k + 1) * P)
                mm(acc[b][:, :], whi[:, 0, ks], hhi[:, k, :], start=(k == 0), stop=False)
                mm(acc[b][:, :], whi[:, 0, ks], hlo[:, k, :], start=False, stop=False)
                last = mm(acc[b][:, :], wlo[:, 0, ks], hhi[:, k, :], start=False, stop=(k == KT - 1))
            last.then_inc(s_acc_full, 1)
            pe.wait_ge(*moved(U_LR, 0))
            pe.wait_ge(s_wup_in, 32)
            for i in range(8):
                if i > 3:
                    pe.wait_ge(s_la, i - 3)
                mm(M[i % 4][:, :], wup[:, i // 4, (i % 4) * P:(i % 4 + 1) * P], lrT[:, :], start=True, stop=True)\
                    .then_inc(s_up_mm, 1)

            def gla_scores(g):
                for d in range(2):
                    pe.wait_ge(s_der, g * 6 + 3 * d + 3)
                    if d == 0:
                        pe.wait_ge(s_gfin, g * 2 + 1)
                        pe.wait_ge(s_la, 8)
                    for t in range(TT):
                        last = nc.tensor.transpose(M[d][:, t * P:(t + 1) * P], kd[:, d, t * P:(t + 1) * P], ident[:, :])
                    last.then_inc(s_kd_tr, 1)
                    for t in range(TT):
                        ts = slice(t * P, (t + 1) * P)
                        last = mm(M[2 + d][:, ts], ke[:, d, ts], qe[:, d, ts], start=True, stop=True)
                    last.then_inc(s_gsc, 1)

            def gla_kv(g):
                pe.wait_ge(s_kdT, g * 2 + 2)
                pe.wait_ge(s_gmask, g * 3 + 3)
                pe.wait_ge(*moved(U_HEAD, 4, 8, g))
                pe.wait_ge(*moved(U_HEAD, 5, 8, g))
                for s in range(NCH - 1):
                    for d in range(2):
                        n = s if d == 0 else NCH - 1 - s
                        rows = slice(n % 2 * CHUNK, (n % 2 + 1) * CHUNK)
                        if s >= 2:
                            pe.wait_ge(s_gst, g * 14 + 2 * (s - 2) + d + 1)
                        mm(M[2 * d + s % 2][:, 0:DV], kdT[rows, d, n // 2, :], gv[rows, n // 2, :],
                           start=True, stop=True).then_inc(s_kv, 1)

            def gla_out(g):
                pe.wait_ge(s_gst, g * 14 + 14)
                for j in range(2):
                    js = slice(j * P, (j + 1) * P)
                    for t in range(TT):
                        mm(M[j][:, t * P:(t + 1) * P], gv[:, t, js], ga_sc[:, t, :], start=(t == 0), stop=False,
                           skip_group_check=True)
                    for n in range(1, NCH):
                        mm(M[j][:, n * CHUNK:(n + 1) * CHUNK], st[:, 0, n - 1, js],
                           qe[:, 0, n * CHUNK:(n + 1) * CHUNK], start=False, stop=False, skip_group_check=True)
                    for n in range(NCH - 1):
                        last = mm(M[j][:, n * CHUNK:(n + 1) * CHUNK], st[:, 1, NCH - 2 - n, js],
                                  qe[:, 1, n * CHUNK:(n + 1) * CHUNK], start=False, stop=(n == NCH - 2),
                                  skip_group_check=True)
                    last.then_inc(s_go, 1)

            def gla_sum(g):
                pe.wait_ge(s_gsq, g * 2 + 2)
                mm(M[2][:, :], mean_dv[:, :], ex[:, 0, :], start=True, stop=False)
                mm(M[2][:, :], mean_dv[:, :], ex[:, 1, :], start=False, stop=True).then_inc(s_gsum, 1)

            def head_tiles(h, c, j):
                tile(U_HEAD, c, (1 + c // 2) % 2, j, 8, h)

            def head_values(h, c):
                b, _, free = TL(U_HEAD, 4 + c, 8, h)
                if later(free):
                    pe.wait_ge(s_acc_free[b], free)
                pe_values(b, 1, c, hhi, hlo)

            def head_iteration(h, gla):
                g = h - 1
                pe.wait_ge(s_unit_lo, h * 4 + U_HEAD + 1)
                head_tiles(h, 0, 0)
                head_tiles(h, 1, 1)
                if gla:
                    gla_scores(g)
                pe.wait_ge(s_unit_lo, h * 4 + U_HEAD + 2)
                head_tiles(h, 2, 0)
                head_tiles(h, 3, 1)
                if gla:
                    gla_kv(g)
                pe.wait_ge(s_unit_lo, h * 4 + U_HEAD + 3)
                head_values(h, 0)
                if gla:
                    gla_out(g)
                head_values(h, 1)
                pe.wait_ge(s_unit_lo, h * 4 + U_HEAD + 4)
                head_tiles(h, 6, 0)
                if gla:
                    gla_sum(g)
                head_tiles(h, 7, 1)

            head_iteration(0, False)
            with pe.Fori(1, GLA_HEADS) as h:
                head_iteration(h, True)
            g = GLA_HEADS - 1
            units(U_C, 1)
            gla_scores(g)
            pe.wait_ge(s_unit_lo, U_C + 1 + 1)
            for j in range(2):
                tile(U_C, 2 + j, (U_C + 1) % 2, j)
            gla_kv(g)
            for m in range(2, 6):
                pe.wait_ge(s_unit_lo, U_C + m + 1)
                tile(U_C, 2 * m, (U_C + m) % 2, 0)
                if m == 2:
                    gla_out(g)
                tile(U_C, 2 * m + 1, (U_C + m) % 2, 1)
                if m == 2:
                    gla_sum(g)

            pe.wait_ge(s_unit_lo, U_POOL + 1)
            for gr_ in range(NG):
                pe.wait_ge(s_p_lo, gr_ + 1)
                for j in range(2):
                    b, _, free = TL(U_POOL, 2 * gr_ + j)
                    if later(free):
                        pe.wait_ge(s_acc_free[b], free)
                    ws = slice(gr_ * 2 * P + j * P, gr_ * 2 * P + (j + 1) * P)
                    mm(acc[b][:, :], whi[:, 1, ws], phi[:, gr_, :], start=True, stop=False)
                    mm(acc[b][:, :], whi[:, 1, ws], plo[:, gr_, :], start=False, stop=False)
                    mm(acc[b][:, :], wlo[:, 1, ws], phi[:, gr_, :], start=False, stop=True)\
                        .then_inc(s_acc_full, 1)
            units(U_BR, 4, ready=s_o_lo)
            units(U_OUT, 4, mhi, mlo, ready=s_merge_lo)

            def ada_tile(n, slot):
                pe.wait_ge(s_ada_sum, n + 1)
                mm(M[2][:, ds(n, 1)], ada[:, slot, 0, :], one_col[:, :], start=True, stop=True,
                   skip_group_check=True).then_inc(s_ada_used, 1)

            norm_mean(1)

            def gate_up(i, j):
                pe.wait_ge(s_unit_lo, i * 2 + U_FIN + j + 1)
                tile(U_FIN, 2 * j, j, 0, 4, i)
                tile(U_FIN, 2 * j + 1, j, 1, 4, i)
                ada_tile(i * 2 + j, j)

            units(U_FIN, 1, ready=s_norm_lo, base=nth(1))
            ada_tile(0, 0)
            gate_up(0, 1)
            with pe.Fori(1, FT // 2) as i:
                for j in range(2):
                    gate_up(i, j)

            def ffn_out(i, j):
                half = FT // 2
                ks = slice(j % 2 * half, (j % 2 + 1) * half)
                pe.wait_ge(s_unit_lo, i * 4 + U_FOUT + j + 1)
                if j < 2:
                    pe.wait_ge(s_f_lo, (j + 1) * half)
                tile(U_FOUT, j, j % 2, 0, 4, i, nk=half, ncol=P, xh=ahi[:, ks, :], xl=alo[:, ks, :])

            for j in range(4):
                ffn_out(0, j)
            ada_tile(FT, 0)
            ada_tile(FT + 1, 1)
            with pe.Fori(1, 4) as i:
                for j in range(4):
                    ffn_out(i, j)

            norm_mean(2)

            def att_values(g):
                pe.wait_ge(s_a_out, g + 1)
                pe.wait_ge(*moved(U_ATT, 2, 4, g))
                for t in range(TT):
                    last = nc.tensor.transpose(M[3][:, t * P:(t + 1) * P], av[:, t * P:(t + 1) * P], ident[:, :])
                last.then_inc(s_av_tr, 1)

            def att_scores(g, a):
                pe.wait_ge(*moved(U_ATT, 0, 4, g))
                pe.wait_ge(*moved(U_ATT, 1, 4, g))
                r = slice(a * AE, (a + 1) * AE)
                for q in range(TT):
                    if a == 0 and q == 3:
                        pe.wait_ge(s_avt, g + 1)
                    if a == 1 and q < 3:
                        pe.wait_ge(s_apt, g * 8 + (4, 2, 3)[q])
                    mm(M[q][:, 0:(q + 1) * P], aq[r, q * P:(q + 1) * P], ak[r, 0:(q + 1) * P], start=True, stop=True)\
                        .then_inc(s_score, 1)

            def att_transposes(g, a):
                for q in range(TT):
                    pe.wait_ge(s_aprob, g * 8 + a * 4 + q + 1)
                    if q == 3:
                        pe.wait_ge(s_apt, g * 8 + a * 4 + 1)
                    for j in range(q + 1):
                        last = nc.tensor.transpose(M[q % 3][:, j * P:(j + 1) * P], apr[:, a, q, j * P:(j + 1) * P],
                                                   ident[:, :])
                    last.then_inc(s_a_tr, 1)

            def att_pv(g, a):
                pe.wait_ge(s_apt, g * 8 + a * 4 + 4)
                pe.wait_ge(s_logit, g * 8 + 8)
                r = slice(a * AE, (a + 1) * AE)
                for j in range(TT):
                    last = mm(M[3][r, j * P:L], avt[:, j, r], apt[:, j, j * P:L], start=(j == 0), stop=(j == TT - 1))
                last.then_inc(s_apv, 1)

            def att_iteration(i, with_units, attend):
                g = i - 1
                if with_units and attend:
                    pe.wait_ge(s_unit_lo, i * 2 + U_ATT + 1)
                    tile(U_ATT, 0, 0, 0, 4, i)
                if attend:
                    att_values(g)
                    att_scores(g, 0)
                if with_units and attend:
                    tile(U_ATT, 1, 0, 1, 4, i)
                if attend:
                    att_transposes(g, 0)
                    att_scores(g, 1)
                if with_units:
                    pe.wait_ge(s_unit_lo, i * 2 + U_ATT + 1 + 1)
                    tile(U_ATT, 2, 1, 0, 4, i)
                if attend:
                    att_pv(g, 0)
                    att_transposes(g, 1)
                if with_units:
                    tile(U_ATT, 3, 1, 1, 4, i)
                if attend:
                    att_pv(g, 1)

            units(U_ATT, 1, ready=s_norm_lo, base=nth(2))
            att_iteration(0, True, False)
            with pe.Fori(1, A_HEADS // 2) as i:
                att_iteration(i, True, True)
            att_iteration(A_HEADS // 2, False, True)

            def hg_scores(g):
                if isinstance(g, int) and g == 0:
                    pe.wait_ge(s_a_out, A_HEADS // 2 + 1)
                pe.wait_ge(s_h_out, g + 1)
                pe.wait_ge(s_h_rs, g + 1)
                pe.wait_ge(*moved(U_HG, 2, 4, g))
                for t in range(TT):
                    last = nc.tensor.transpose(M[0][:, t * P:(t + 1) * P], hi_[:, t * P:(t + 1) * P], ident[:, :])
                last.then_inc(s_h_itr, 1)
                pe.wait_ge(s_h_op, g * 2 + 1)
                for t in range(TT):
                    last = nc.tensor.transpose(M[1][:, t * P:(t + 1) * P], hkd[:, t * P:(t + 1) * P], ident[:, :])
                last.then_inc(s_h_ktr, 1)
                for n in range(LEVELS + 1):
                    if n == 0:
                        pe.wait_ge(*moved(U_HG, 0, 4, g))
                    pe.wait_ge(s_h_w, g * 7 + max(n, 1))
                    if n == 2:
                        pe.wait_ge(s_h_cp, g * 2 + 1)
                    if n == 3:
                        pe.wait_ge(s_h_cp, g * 2 + 2)
                    if n >= 4:
                        pe.wait_ge(s_h_mask, g * 9 + n - 2)
                    for t in range(TT):
                        ts = slice(t * P, (t + 1) * P)
                        left, right = (hk[:, ts], hq[:, ts]) if n == 0 else (hw[:, n - 1, ts], hw[:, n - 1, ts])
                        last = mm(M[(n + 2) % 4][:, ts], left, right, start=True, stop=True)
                    last.then_inc(s_h_score, 1)
                pe.wait_ge(s_h_mask, g * 9 + 7)
                for n in range(TT - 1):
                    last = mm(M[3][:, n * P:(n + 1) * P], hkT[:, n, :], hit[:, n, :], start=True, stop=True)
                last.then_inc(s_h_kv, 1)

            def hg_out(g):
                pe.wait_ge(s_h_mask, g * 9 + 9)
                pe.wait_ge(s_h_st, g * 3 + 3)
                pe.wait_ge(s_h_op, g * 2 + 2)
                for t in range(TT):
                    mm(M[2][:, t * P:(t + 1) * P], hit[:, t, :], hsc[:, t, :], start=(t == 0), stop=False,
                       skip_group_check=True)
                for t in range(1, TT):
                    last = mm(M[2][:, t * P:(t + 1) * P], hst[:, t - 1, :], hqe[:, t * P:(t + 1) * P], start=False,
                              stop=(t == TT - 1), skip_group_check=True)
                last.then_inc(s_h_o, 1)

            def hg_sum(g):
                pe.wait_ge(s_h_sq, g + 1)
                mm(M[3][:, :], mean_p[:, :], hsq[:, :], start=True, stop=True).then_inc(s_h_sum, 1)

            def hg_iteration(g, u0=None):
                if u0 is None:
                    u, base, h = (g + 1) * 2 + U_HG, U_HG, g + 1
                else:
                    u, base, h = u0, u0, 0
                pe.wait_ge(s_unit_lo, u + 1)
                tile(base, 0, 0, 0, 4, h)
                if later(g):
                    hg_sum(g - 1)
                tile(base, 1, 0, 1, 4, h)
                pe.wait_ge(s_unit_lo, u + 2)
                tile(base, 2, 1, 0, 4, h)
                hg_scores(g)
                tile(base, 3, 1, 1, 4, h)
                hg_out(g)

            units(U_HG, 2)
            hg_iteration(0)
            with pe.Fori(1, H_HEADS - 1) as g:
                hg_iteration(g)
            hg_iteration(H_HEADS - 1, U_G2)

            pe.wait_ge(s_unit_lo, U_G2 + 3)
            tile(U_G2, 4, 0, 0)
            hg_sum(H_HEADS - 1)
            tile(U_G2, 5, 0, 1)
            units(U_G2 + 3, 5)
            units(U_BA, 2, oahi, oalo, nk=AW // P, ncol=L, ready=s_oa_lo)
            units(U_BB, 4, ready=s_ob_lo)
            units(U_OUT2, 4, nhi, nlo, ready=s_n_lo)
            norm_mean(3)
            for t in range(TT):
                for c in range(2):
                    m = 2 * t + c
                    if m == 3:
                        pe.wait_ge(s_norm_rs, 4)
                    if m > 3:
                        pe.wait_ge(s_y_nat, m - 3)
                    pe.wait_ge(s_yT, 4 * c + 4)
                    for k in range(4):
                        last = nc.tensor.transpose(M[m % 4][:, k * P:(k + 1) * P],
                                                   yT[:, 4 * c + k, t * P:(t + 1) * P], ident[:, :])
                    last.then_inc(s_y_tr, 1)


_INS = ["x", "norm_mix", "w_in", "w_decay_up_fwd", "b_decay_fwd", "w_decay_up_bwd", "b_decay_bwd", "gla_norm",
        "w_branch_gla", "w_pool_group", "pool_scale", "w_out", "norm_ffn", "w_ffn_in", "w_ffn_out", "norm_final",
        "c_2", "w_ada_2", "b_ada_2", "norm_g_2", "w_in_2", "hgrn_onorm_g_2", "w_branch_a_2", "w_branch_b_2",
        "w_out_2", "rel_bias_2", "hgrn_lb_2", "final_g_2"]


def kernel(**inputs):
    import numpy as _np
    import concourse.bacc as _bacc
    from concourse import mybir as _mybir
    from concourse.bass_utils import run_bass_kernel_spmd as _run

    nc = _bacc.Bacc("TRN2", target_bir_lowering=False, num_devices=1)
    arrays, aps = {}, {}
    for name, a in [(n, inputs[n]) for n in _INS] + list(shape_constants().items()):
        a = _np.ascontiguousarray(a)
        arrays[f"in_{name}_dram"] = a
        aps[name] = nc.dram_tensor(f"in_{name}_dram", a.shape, _mybir.dt.from_np(a.dtype), kind="ExternalInput").ap()
    y = nc.dram_tensor("out_0_dram", (1, L, DM), _mybir.dt.float32, kind="ExternalOutput").ap()
    build(nc, aps, y)
    r = _run(nc, [arrays], core_ids=[0])
    return r.results[0]["out_0_dram"]
```

```python
import concourse.bass as bass
from concourse import mybir
from contextlib import ExitStack
import numpy as np

P = 128
DM = 1024
L = 512
KT = DM // P
TT = L // P
GLA_HEADS, DK, DV, CHUNK = 4, 128, 256, 64
NCH = L // CHUNK
RANK = 16
POOL_WINDOWS = (2, 4, 8, 16)
NG = len(POOL_WINDOWS)
PAD = 8
D_FF = 2816
FT = D_FF // P
A_HEADS, AE = 8, 64
AW = A_HEADS * AE
H_HEADS = 8
N_BUCKETS, MAX_DISTANCE = 32, 2048
PATTERNS = ((128, 1), (512, 4), (2048, 16))
NEG_INF = -1e30
EPS = 1e-6
LEVELS = 7
BW = 640

C_Q, C_K, C_V, C_R = 0, 512, 1024, 2048
C_LR = 3072
C_U = C_LR + 2 * RANK
C_GA = C_U + 512
C_GB = C_GA + DM
D_QA, D_KA, D_VA, D_ZA = 0, 512, 1024, 1536
D_QB, D_FB, D_IB, D_ZB = 2048, 3072, 4096, 5120
D_GA, D_GB = 6144, 7168

R_NM, R_GN, R_PS, R_NF, R_BF, R_BB, R_NG2, R_ADA = 0, 8, 16, 24, 32, 36, 40, 48
R_LB0, R_LB1, R_NFIN, R_C, R_ON, R_FG = 72, 80, 88, 96, 104, 105

U_LR, U_HEAD, U_C, U_POOL, U_BR, U_OUT = 0, 1, 17, 23, 24, 28
U_FIN, U_FOUT, U_ATT, U_HG, U_G2 = 32, 54, 70, 78, 94
U_BA, U_BB, U_OUT2, U_END = 102, 104, 108, 112


def first_tile(u):
    if u == 0:
        return 0
    if u <= U_POOL:
        return 2 * u - 1
    if u <= U_FOUT:
        return 53 + 2 * (u - U_BR)
    if u <= U_ATT:
        return 113 + (u - U_FOUT)
    if u <= U_BA:
        return 129 + 2 * (u - U_ATT)
    if u == U_BA + 1:
        return 197
    return 201 + 2 * (u - U_BB)


def shape_constants():
    f = np.float32
    ident = np.eye(P, dtype=f)
    s, t = np.arange(P)[:, None], np.arange(P)[None, :]
    masks = [(s // CHUNK == t // CHUNK) & (s <= t), (s // CHUNK == t // CHUNK) & (s > t)]
    for lev in range(LEVELS):
        half = 1 << lev
        masks.append((s // (2 * half) == t // (2 * half)) & (s % (2 * half) < half) & (t % (2 * half) >= half))
    masks.append(s == t)
    masks = np.ascontiguousarray(np.stack(masks, 1).astype(f))
    edge = np.zeros((NG, 2 * PAD), f)
    for g, w in enumerate(POOL_WINDOWS):
        for c in range(PAD):
            for side, pos in ((0, c), (1, L - PAD + c)):
                lo, hi = max(pos - w // 2, 0), min(pos + w - w // 2, L)
                edge[g, side * PAD + c] = 1.0 / (hi - lo)
    dist = np.arange(BW) - (P - 1)
    n = np.maximum(dist, 0).astype(f)
    exact = N_BUCKETS // 2
    large = exact + (np.log(np.maximum(n, f(1)) / f(exact)) / f(np.log(MAX_DISTANCE / exact))
                     * f(N_BUCKETS - exact)).astype(np.int32)
    bucket = np.where(dist < exact, np.maximum(dist, 0), np.minimum(large, N_BUCKETS - 1))
    count = np.zeros(BW, np.int64)
    for window, dil in PATTERNS:
        count += (dist >= 0) & (dist <= window) & (dist % dil == 0)
    hot = np.zeros((N_BUCKETS + 1, BW), f)
    hot[bucket, np.arange(BW)] = count > 0
    hot[N_BUCKETS] = np.where(count > 0, np.log(np.maximum(count, 1)), NEG_INF)
    return {"ident": ident, "masks": masks, "edge": edge, "hot": hot}


def build(nc, inp, out):
    f32, f32r, u8 = mybir.dt.float32, mybir.dt.float32r, mybir.dt.uint8
    ALU, ACT = mybir.AluOpType, mybir.ActivationFunctionType
    ds = bass.ds
    KB = 1024
    BASE = (nc.sbuf_base + 31) // 32 * 32

    def at(name, kb, shape, dt=f32):
        return nc.alloc_sbuf_tensor_at(name, shape, dt, offset=BASE + int(kb * KB))

    raw = at("raw", 0, [P, 2, 16 * P])
    whi = at("whi", 16, [P, 2, 16 * P], f32r)
    wlo = at("wlo", 32, [P, 2, 16 * P], f32r)
    hhi = at("hhi", 48, [P, KT, L], f32r)
    hlo = at("hlo", 64, [P, KT, L], f32r)
    xres = at("xres", 80, [P, KT, L])
    sig_ga = at("sig_ga", 80, [P, KT, L])
    S0 = 96
    ident = at("ident", S0, [P, P])
    mean_dm = at("mean_dm", S0 + .5, [P, P])
    mean_dv = at("mean_dv", S0 + 4.5, [P, P])
    mean_p = at("mean_p", S0 + 5, [P, P])
    vcol = at("vcol", S0 + 1, [P, P])
    masks = at("masks", S0 + 1.5, [P, LEVELS + 3, P], u8)
    mod = at("mod", S0 + 2.75, [P, 24])
    lbt = at("lbt", S0 + 3, [P, 6, 8])
    small = at("small", S0 + 3.25, [P, 32])
    eps_col = at("eps", S0 + 3.375, [P, 1])
    eps2_col = at("eps2", S0 + 3.46875, [P, 1])
    one_col = at("one_col", S0 + 3.40625, [P, 1])
    edge = at("edge", S0 + 3.5, [P, NG, 2 * PAD])
    amax = at("amax", S0 + 3.75, [P, 2, TT])
    xss, xrs = amax[:, 0, :], amax[:, 1, :]
    aden = at("aden", S0 + 4, [P, 2, TT])
    dec = at("dec", S0 + 4.25, [P, 2, NCH])
    relb = at("relb", S0 + 4.375, [P, A_HEADS])
    tick = at("tick", S0 + 3.4375, [1, 8])
    A0 = 101.5
    mid_col = small[:, 0:8]
    silu_c = small[:, 8:16]
    g2_col = small[:, 16:24]

    xnat = at("xnat", A0 + 16, [P, TT, DM])
    grow = at("grow", A0 + 33, [KT, P])
    vrow = at("vrow", A0 + 32, [P, P])
    hot = at("hot", A0 + 34, [N_BUCKETS + 1, BW])
    brow = at("brow", A0 + 37, [A_HEADS, BW])
    mask_src = at("mask_src", A0 + 88, [P, LEVELS + 3, P])
    wup = at("wup", A0 + 40, [2 * RANK, 2, L])
    nsq = at("nsq", A0, [P, 2, L])
    nacc = at("nacc", A0 + 4, [P, L])
    nrs = at("nrs", A0 + 6, [P, L])
    nht = at("nht", A0 + 8, [P, 2, L])
    b_all = at("b_all", A0, [P, 8, L])
    o_all = at("o_all", A0 + 16, [P, KT, L])
    lrT = at("lrT", A0 + 44, [2 * RANK, L])
    gq, gk = at("gq", A0 + 32, [P, L]), at("gk", A0 + 34, [P, L])
    lt = at("lt", A0 + 46, [P, 2, 2, L])
    gv = at("gv", A0 + 36, [P, TT, DV])
    gr = at("gr", A0 + 54, [P, 2, L])
    qe, ke = at("qe", A0 + 58, [P, 2, L]), at("ke", A0 + 62, [P, 2, L])
    kd = at("kd", A0 + 66, [P, 2, L])
    ex = at("ex", A0 + 70, [P, 3, L])
    kdT = at("kdT", A0 + 76, [P, 2, TT, P])
    ga_sc = at("ga_sc", A0 + 80, [P, TT, P])
    st = at("st", A0 + 82, [P, 2, NCH - 1, DV])
    rst = at("rst", A0 + 96, [P, L])
    gbm = at("gbm", A0, [P, KT, L])
    phi = at("phi", A0 + 64, [P, NG, L], f32r)
    plo = at("plo", A0 + 72, [P, NG, L], f32r)
    ptmp = at("ptmp", A0 + 49, [P, L + 2 * PAD])
    ptmp2 = at("ptmp2", A0 + 51.25, [P, L + 2 * PAD])
    upad = at("upad", A0 + 40, [P, NG, L + 2 * PAD])
    mhi = at("mhi", A0 + 32, [P, KT, L], f32r)
    mlo = at("mlo", A0 + 80, [P, KT, L], f32r)
    ahi = at("ahi", A0, [P, FT, L], f32r)
    alo = at("alo", A0 + 44, [P, FT, L], f32r)
    fsg = at("fsg", A0 + 88, [P, 2, L])
    faa = at("faa", A0 + 92, [P, 2, L])
    ada = at("ada", A0 + 96, [P, 2, KT, P])
    oa = at("oa", A0, [P, AW // P, L])
    ob = at("ob", A0 + 8, [P, KT, L])
    sga = at("sga", A0 + 24, [P, KT, L])
    sgb = at("sgb", A0 + 40, [P, KT, L])
    aq, ak = at("aq", A0 + 56, [P, L]), at("ak", A0 + 58, [P, L])
    av, az = at("av", A0 + 60, [P, L]), at("az", A0 + 62, [P, L])
    avt = at("avt", A0 + 64, [P, TT, P])
    abias = at("abias", A0 + 66, [P, 2, L])
    apr = at("apr", A0 + 70, [P, 2, TT, L])
    apt = at("apt", A0 + 86, [P, TT, L])
    hq, hf = at("hq", A0 + 56, [P, L]), at("hf", A0 + 58, [P, L])
    hi_, hz = at("hi_", A0 + 60, [P, L]), at("hz", A0 + 62, [P, L])
    hk, hb = at("hk", A0 + 64, [P, L]), at("hb", A0 + 66, [P, L])
    hw = at("hw", A0 + 68, [P, LEVELS, L])
    hqe, hkd = at("hqe", A0 + 82, [P, L]), at("hkd", A0 + 84, [P, L])
    hkT = at("hkT", A0 + 86, [P, TT, P])
    hit = at("hit", A0 + 88, [P, TT, P])
    hsc = at("hsc", A0 + 90, [P, TT, P])
    hst = at("hst", A0 + 92, [P, TT - 1, P])
    hsq, hrs = at("hsq", A0 + 94, [P, L]), at("hrs", A0 + 96, [P, L])
    hrst = at("hrst", A0 + 98, [P, L])
    oahi = at("oahi", A0 + 88, [P, AW // P, L], f32r)
    oalo = at("oalo", A0 + 96, [P, AW // P, L], f32r)
    nhi = at("nhi", A0 + 56, [P, KT, L], f32r)
    nlo = at("nlo", A0 + 72, [P, KT, L], f32r)
    yT = at("yT", A0 + 16, [P, KT, L])
    ynat = at("ynat", A0 + 32, [P, TT, DM])

    bias_dram = nc.dram_tensor("bias_scratch", (A_HEADS, BW), f32, kind="Internal").ap()

    ctx = ExitStack()
    with ctx:
        acc = [ctx.enter_context(nc.psum_tensor(f"acc{b}", [P, L], f32)) for b in range(4)]
        M = [ctx.enter_context(nc.psum_tensor(f"mid{b}", [P, L], f32)) for b in range(4)]
        def sem(name):
            return ctx.enter_context(nc.semaphore(name))

        s_acc_free = [sem(f"acc_free{b}") for b in range(4)]
        s_unit_in = [sem(f"unit_in{b}") for b in range(2)]
        s_ada_in = [sem(f"ada_in{b}") for b in range(2)]
        s_a_out = sem("a_out")
        s_a_tr = sem("a_tr")
        s_acc_full = sem("acc_full")
        s_x_tr = sem("x_tr")
        s_x_res = sem("x_res")
        s_x_n = sem("x_n")
        s_x_rms = sem("x_rms")
        s_ada_sum = sem("ada_sum")
        s_ada_step = sem("ada_step")
        s_eps = sem("eps")
        s_h_rl = sem("h_rl")
        s_gln = sem("gln")
        s_norm_ln = sem("norm_ln")
        s_x_mid = sem("x_mid")
        s_mid_step = sem("mid_step")
        s_mid_sum = sem("mid_sum")
        s_mid_acc = sem("mid_acc")
        s_mid_sq = sem("mid_sq")
        s_norm_zero = sem("norm_zero")
        s_means = sem("means")
        s_ada_used = sem("ada_used")
        s_aexp = sem("aexp")
        s_amax = sem("amax")
        s_aprob = sem("aprob")
        s_apt = sem("apt")
        s_apv = sem("apv")
        s_arec = sem("arec")
        s_av_tr = sem("av_tr")
        s_avt = sem("avt")
        s_az_sig = sem("az_sig")
        s_b_ready = sem("b_ready")
        s_bias_in = sem("bias_in")
        s_bias_mm = sem("bias_mm")
        s_bias_out = sem("bias_out")
        s_bias_row = sem("bias_row")
        s_bias_src = sem("bias_src")
        s_csig = sem("csig")
        s_der = sem("der")
        s_edge_in = sem("edge_in")
        s_f_hi = sem("f_hi")
        s_f_lo = sem("f_lo")
        s_f_sig = sem("f_sig")
        s_gdec = sem("gdec")
        s_gdf = sem("gdf")
        s_gex = sem("gex")
        s_gfin = sem("gfin")
        s_gmask = sem("gmask")
        s_go = sem("go")
        s_grs = sem("grs")
        s_gsc = sem("gsc")
        s_gsq = sem("gsq")
        s_gst = sem("gst")
        s_gsum = sem("gsum")
        s_gt = sem("gt")
        s_h_b = sem("h_b")
        s_h_cp = sem("h_cp")
        s_h_df = sem("h_df")
        s_h_ex = sem("h_ex")
        s_h_fg = sem("h_fg")
        s_h_itr = sem("h_itr")
        s_h_ktr = sem("h_ktr")
        s_h_kv = sem("h_kv")
        s_h_lex = sem("h_lex")
        s_h_ln = sem("h_ln")
        s_h_mask = sem("h_mask")
        s_h_o = sem("h_o")
        s_h_op = sem("h_op")
        s_h_out = sem("h_out")
        s_h_rs = sem("h_rs")
        s_h_score = sem("h_score")
        s_h_sq = sem("h_sq")
        s_h_st = sem("h_st")
        s_h_sum = sem("h_sum")
        s_h_t = sem("h_t")
        s_h_w = sem("h_w")
        s_hq_sig = sem("hq_sig")
        s_hrst = sem("hrst")
        s_hz_sig = sem("hz_sig")
        s_id_in = sem("id_in")
        s_kdT = sem("kdT")
        s_kd_tr = sem("kd_tr")
        s_kv = sem("kv")
        s_la = sem("la")
        s_la_abs = sem("la_abs")
        s_la_exp = sem("la_exp")
        s_la_ln = sem("la_ln")
        s_la_min = sem("la_min")
        s_lb = sem("lb")
        s_logit = sem("logit")
        s_mask_src = sem("mask_src")
        s_masks = sem("masks")
        s_merge2 = sem("merge2")
        s_merge_hi = sem("merge_hi")
        s_merge_lo = sem("merge_lo")
        s_merged = sem("merged")
        s_mod = sem("mod")
        s_n_hi = sem("n_hi")
        s_n_lo = sem("n_lo")
        s_norm_acc = sem("norm_acc")
        s_norm_hi = sem("norm_hi")
        s_norm_ht = sem("norm_ht")
        s_norm_lo = sem("norm_lo")
        s_norm_rs = sem("norm_rs")
        s_norm_sq = sem("norm_sq")
        s_norm_sum = sem("norm_sum")
        s_o_hi = sem("o_hi")
        s_o_lo = sem("o_lo")
        s_oa_hi = sem("oa_hi")
        s_oa_lo = sem("oa_lo")
        s_ob_hi = sem("ob_hi")
        s_ob_lo = sem("ob_lo")
        s_p_hi = sem("p_hi")
        s_p_lo = sem("p_lo")
        s_pool_add = sem("pool_add")
        s_pool_edge = sem("pool_edge")
        s_pool_mid = sem("pool_mid")
        s_pool_side = sem("pool_side")
        s_pooled = sem("pooled")
        s_r_sig = sem("r_sig")
        s_rows_in = sem("rows_in")
        s_gain_in = sem("gain_in")
        s_gain_mm = sem("gain_mm")
        s_gain = sem("gain")
        s_rst = sem("rst")
        s_score = sem("score")
        s_silu_c = sem("silu_c")
        s_unit_hi = sem("unit_hi")
        s_unit_lo = sem("unit_lo")
        s_up_mm = sem("up_mm")
        s_upad_zero = sem("upad_zero")
        s_vcol = sem("vcol")
        s_vcol_mm = sem("vcol_mm")
        s_vrow_zero = sem("vrow_zero")
        s_wup_in = sem("wup_in")
        s_xT = sem("xT")
        s_x_back = sem("x_back")
        s_x_in = [sem(f"x_in{t}") for t in range(TT)]
        s_yT = sem("yT")
        s_y_act = sem("y_act")
        s_y_dve = sem("y_dve")
        s_gsq_sum = sem("gsq_sum")
        s_y_nat = sem("y_nat")
        s_y_out = sem("y_out")
        s_y_tr = sem("y_tr")

        def later(n):
            return not isinstance(n, int) or n > 0

        def nth(n):
            return n * KT

        def x_bank(k):
            return acc[k] if k < 4 else M[k - 4]

        def cols(t, k):
            return t[:, ds(k, 1), :].rearrange("p a n -> p (a n)") if not isinstance(k, int) else t[:, k, :]

        def col(t, k):
            return t[:, ds(k, 1)] if not isinstance(k, int) else t[:, k:k + 1]

        def vtile(v):
            return v.rearrange("p (a b) -> p a b", b=P)

        def used_before(u, lin=None):
            if isinstance(u, int) and lin is None:
                return first_tile(u - 1) if u >= 2 else 0
            return lin

        def split_hi(act, u, slot, n=16 * P, lin=None):
            act.wait_ge(s_unit_in[slot], unit_count(u, slot))
            if later(used_before(u, lin)):
                act.wait_ge(s_acc_full, used_before(u, lin))
            nc.scalar.activation(whi[:, slot, 0:n], raw[:, slot, 0:n], ACT.Copy).then_inc(s_unit_hi, 1)

        def split_lo(pool, u, slot, n=16 * P):
            pool.wait_ge(s_unit_hi, u + 1)
            nc.gpsimd.tensor_tensor(wlo[:, slot, 0:n], raw[:, slot, 0:n], whi[:, slot, 0:n].bitcast(f32),
                                    ALU.subtract).then_inc(s_unit_lo, 1)

        def unit_count(u, slot):
            return 32 * (u // 2 + 1) if isinstance(u, int) else (u - slot) * 16 + 32

        def raw_free(sp, u):
            if later(u - 1):
                sp.wait_ge(s_unit_lo, u - 1)

        def pe_tile(bank, slot, j, nk, ncol, xh, xl):
            for k in range(nk):
                h = whi[:, slot, k * ncol + j * P:k * ncol + (j + 1) * P]
                lo = wlo[:, slot, k * ncol + j * P:k * ncol + (j + 1) * P]
                nc.tensor.matmul(acc[bank][:, :], h, xh[:, k, :], start=(k == 0), stop=False)
                nc.tensor.matmul(acc[bank][:, :], h, xl[:, k, :], start=False, stop=False)
                last = nc.tensor.matmul(acc[bank][:, :], lo, xh[:, k, :], start=False, stop=(k == nk - 1))
            last.then_inc(s_acc_full, 1)

        def pe_values(bank, slot, pair, xh, xl):
            for t in (2 * pair, 2 * pair + 1):
                o = acc[bank][:, (t % 2) * DV:(t % 2 + 1) * DV]
                for k in range(KT):
                    h, lo = whi[:, slot, k * DV:(k + 1) * DV], wlo[:, slot, k * DV:(k + 1) * DV]
                    xs = slice(t * P, (t + 1) * P)
                    nc.tensor.matmul(o, xh[:, k, xs], h, start=(k == 0), stop=False)
                    nc.tensor.matmul(o, xh[:, k, xs], lo, start=False, stop=False)
                    last = nc.tensor.matmul(o, xl[:, k, xs], h, start=False, stop=(k == KT - 1))
            last.then_inc(s_acc_full, 1)

        def kview(w, c0, n):
            return w.rearrange("(k p) n -> p k n", p=P)[:, :, ds(c0, n)]

        def rawk(slot, nk, ncol, j0=0, n=None):
            return raw[:, slot, 0:nk * ncol].rearrange("p (k n) -> p k n", k=nk)[:, :, j0:j0 + (n or ncol)]

        def TL(u0, c, per=0, i=0):
            t = first_tile(u0) + c
            if isinstance(i, int):
                t += per * i
                return t % 4, t + 1, t // 4
            return t % 4, t + 1 + i * per, t // 4 + i * (per // 4)

        def moved(u0, c, per=0, i=0):
            b, _, free = TL(u0, c, per, i)
            return s_acc_free[b], free + 1

        w_in, w_in2 = inp["w_in"][0], inp["w_in_2"][0]
        w_fin, w_fout = inp["w_ffn_in"][0], inp["w_ffn_out"][0]

        def bias_load(eng, i):
            eng.dma_start(abias[:, :, :], bass.AP(tensor=bias_dram.tensor, offset=i * (2 * BW),
                                                  ap=[[1, P], [BW, 2], [1, L]])).then_inc(s_bias_in, 32)

        ROWS = [("gla_norm", R_GN), ("pool_scale", R_PS), ("norm_ffn", R_NF),
                ("b_decay_fwd", R_BF), ("b_decay_bwd", R_BB), ("norm_g_2", R_NG2), ("b_ada_2", R_ADA),
                ("norm_final", R_NFIN), ("c_2", R_C), ("hgrn_onorm_g_2", R_ON), ("final_g_2", R_FG),
                ("hgrn_lb_2", R_LB0)]

        def row_load(eng, name, r):
            v = inp[name]
            v = v.rearrange("l (r p) -> (l r) p", p=P) if name == "hgrn_lb_2" else \
                (v if len(v.shape) == 1 else v[0]).rearrange("(r p) -> r p", p=P)
            eng.dma_start(vrow[r:r + v.shape[0], :], v).then_inc(s_rows_in, 16)

        block = ctx.enter_context(nc.Block())

        @block.sync
        def _(sp):
            def load(u, slot, src, nk=KT, ncol=2 * P):
                raw_free(sp, u)
                sp.dma_start(rawk(slot, nk, ncol), src).then_inc(s_unit_in[slot], 32)

            def load_pair(u, slot, w, ca, cb):
                raw_free(sp, u)
                sp.dma_start(rawk(slot, KT, 2 * P, 0, P), kview(w, ca, P)).then_inc(s_unit_in[slot], 16)
                sp.dma_start(rawk(slot, KT, 2 * P, P, P), kview(w, cb, P)).then_inc(s_unit_in[slot], 16)

            xn = inp["x"][0].rearrange("(t p) d -> t p d", p=P)
            sp.dma_start(ident[:, :], inp["ident"]).then_inc(s_id_in, 16)
            for t in range(TT):
                sp.dma_start(xnat[:, t, :], xn[t]).then_inc(s_x_in[t], 16)
            load(0, 0, kview(w_in, C_LR, P), ncol=P)
            sp.wait_ge(s_vrow_zero, 3)
            for name, r in ROWS:
                row_load(sp, name, r)

            def head_loads(h, u):
                load_pair(u, 1, w_in, C_Q + h * DK, C_K + h * DK)
                load(u + 1, 0, kview(w_in, C_GA + h * 256, 256))
                load(u + 2, 1, kview(w_in, C_V + h * DV, 256))
                load(u + 3, 0, kview(w_in, C_R + h * DV, 256))

            head_loads(0, 1)
            with sp.Fori(1, GLA_HEADS) as h:
                head_loads(h, h * 4 + 1)
            for j in range(2):
                load(U_C + j, (U_C + j) % 2, kview(w_in, C_U + j * 256, 256))
            for j in range(4):
                load(U_C + 2 + j, (U_C + j) % 2, kview(w_in, C_GB + j * 256, 256))
            load(U_POOL, U_POOL % 2, inp["w_pool_group"][0].rearrange("g p n -> p g n"), nk=NG)
            for j in range(4):
                load(U_BR + j, j % 2, kview(inp["w_branch_gla"][0], j * 256, 256))
            sp.wait_ge(s_o_lo, KT)
            for t in range(TT):
                sp.dma_start(xnat[:, t, :], xn[t]).then_inc(s_x_back, 16)
            for j in range(4):
                load(U_OUT + j, j % 2, kview(inp["w_out"][0], j * 256, 256))
            def ada_load(n, slot):
                if later(n - 1):
                    sp.wait_ge(s_ada_used, n - 1)
                sp.dma_start(ada[:, slot, :, :], kview(inp["w_ada_2"][0], n * P, P)).then_inc(s_ada_in[slot], 16)

            for j in range(2):
                load_pair(U_FIN + j, j, w_fin, j * P, j * P + D_FF)
            sp.wait_ge(*moved(U_OUT, KT - 1))
            for j in range(2):
                ada_load(j, j)
            with sp.Fori(1, FT // 2) as i:
                for j in range(2):
                    load_pair(U_FIN + j + i * 2, j, w_fin, i * 256 + j * P, i * 256 + j * P + D_FF)
                    ada_load(i * 2 + j, j)

            def ffn_out_load(i, j):
                u, half = U_FOUT + j + i * 4, FT // 2
                raw_free(sp, u)
                src = w_fout[(j % 2) * half * P:(j % 2 + 1) * half * P, :]
                sp.dma_start(rawk(j % 2, half, P), kview(src, i * 256 + (j // 2) * P, P))\
                    .then_inc(s_unit_in[j % 2], 32)

            ffn_out_load(0, 0)
            ffn_out_load(0, 1)
            ada_load(FT, 0)
            ada_load(FT + 1, 1)
            ffn_out_load(0, 2)
            ffn_out_load(0, 3)
            with sp.Fori(1, 4) as i:
                for j in range(4):
                    ffn_out_load(i, j)

            def att_loads(i):
                load_pair(U_ATT + i * 2, 0, w_in2, D_QA + i * P, D_KA + i * P)
                load_pair(U_ATT + 1 + i * 2, 1, w_in2, D_VA + i * P, D_ZA + i * P)

            att_loads(0)
            sp.wait_ge(s_norm_lo, nth(2) + KT)
            sp.wait_ge(s_bias_out, 16)
            bias_load(sp, 0)
            with sp.Fori(1, A_HEADS // 2) as i:
                att_loads(i)
            with sp.Fori(0, H_HEADS) as h:
                load_pair(U_HG + h * 2, 0, w_in2, D_QB + h * P, D_FB + h * P)
                load_pair(U_HG + 1 + h * 2, 1, w_in2, D_IB + h * P, D_ZB + h * P)
            for j in range(8):
                load(U_G2 + j, j % 2, kview(w_in2, D_GA + j * 256, 256))
            for j in range(2):
                load(U_BA + j, j % 2, kview(inp["w_branch_a_2"][0], j * L, L), nk=AW // P, ncol=L)
            for j in range(4):
                load(U_BB + j, j % 2, kview(inp["w_branch_b_2"][0], j * 256, 256))
            for j in range(4):
                load(U_OUT2 + j, j % 2, kview(inp["w_out_2"][0], j * 256, 256))
            for t in (0, 2, 1, 3):
                if t < 2:
                    sp.wait_ge(s_y_dve, t + 1)
                else:
                    sp.wait_ge(s_y_act, t - 1)
                sp.dma_start(out[0, t * P:(t + 1) * P, :], ynat[:, t, :]).then_inc(s_y_out, 16)
            sp.wait_ge(s_y_out, 16 * TT)

        @block.scalar
        def _(act):
            A = nc.scalar.activation
            LN_EXP = "natural_log_exp_and_others"
            act.dma_start(grow[:, :], inp["norm_mix"][0].rearrange("(r p) -> r p", p=P)).then_inc(s_gain_in, 16)

            def norm_square(n, k):
                if nth(n) + max(k - 1, 0) > 0:
                    act.wait_ge(s_norm_acc, nth(n) + max(k - 1, 0))
                A(nsq[:, k % 2, :], xres[:, k, :], ACT.Square).then_inc(s_norm_sq, 1)

            def norm_rs(n):
                nc.scalar.preload_act_table_set(LN_EXP)
                act.wait_ge(s_norm_sum, n + 1)
                A(nrs[:, :], M[3][:, :], ACT.Ln, bias=eps_col[:, :]).then_inc(s_norm_ln, 1)
                act.wait_ge(s_norm_ln, n + 1)
                A(nrs[:, :], nrs[:, :], ACT.Exp, scale=-0.5).then_inc(s_norm_rs, 1)

            def norm_hi(n, split, shift=False):
                for k in range(KT):
                    if k == KT // 2:
                        split(0, 0)
                    act.wait_ge(s_norm_ht, nth(n) + k + 1)
                    if shift:
                        A(hhi[:, k, :], nht[:, k % 2, :], ACT.Identity, bias=mod[:, k:k + 1])\
                            .then_inc(s_norm_hi, 1)
                    else:
                        A(hhi[:, k, :], nht[:, k % 2, :], ACT.Copy).then_inc(s_norm_hi, 1)

            nc.scalar.preload_act_table_set(LN_EXP)
            act.wait_ge(s_eps, 1)
            for t in range(TT):
                act.wait_ge(s_x_in[t], 16)
                if t > 0:
                    act.wait_ge(s_x_rms, 3 * t - 2)
                A(nsq[:, :, :].rearrange("p a n -> p (a n)"), xnat[:, t, :], ACT.Square,
                  accum_out=xss[:, t:t + 1]).then_inc(s_x_rms, 1)
                act.wait_ge(s_x_rms, 3 * t + 1)
                A(xrs[:, t:t + 1], xss[:, t:t + 1], ACT.Ln, bias=eps_col[:, :], scale=1.0 / DM).then_inc(s_x_rms, 1)
                act.wait_ge(s_x_rms, 3 * t + 2)
                A(xrs[:, t:t + 1], xrs[:, t:t + 1], ACT.Exp, scale=-0.5).then_inc(s_x_rms, 1)
                if t == 0:
                    act.wait_ge(s_gain_mm, 1)
                    A(vcol[:, R_NM:R_NM + KT], M[0][:, 0:KT], ACT.Copy).then_inc(s_gain, 1)
            act.wait_ge(s_gain, 1)
            split_hi(act, 0, 0, KT * P)
            for k in range(KT):
                act.wait_ge(s_xT, k + 1)
                A(hhi[:, k, :], x_bank(k)[:, :], ACT.Identity, scale=vcol[:, R_NM + k:R_NM + k + 1])\
                    .then_inc(s_norm_hi, 1)

            split_hi(act, 1, 1)
            b, full, _ = TL(U_LR, 0)
            act.wait_ge(s_acc_full, full)
            A(lrT[:, :], acc[b][0:2 * RANK, :], ACT.Copy).then_inc(s_acc_free[b], 1)
            act.wait_ge(s_vcol_mm, 1)
            A(vcol[:, KT:P], M[1][:, KT:P], ACT.Copy).then_inc(s_vcol, 1)
            act.wait_ge(s_bias_mm, 2)
            A(brow[:, 0:L], M[3][0:A_HEADS, :], ACT.Copy).then_inc(s_bias_row, 1)
            A(brow[:, L:BW], M[2][0:A_HEADS, 0:BW - L], ACT.Copy).then_inc(s_bias_row, 1)
            split_hi(act, 2, 0)
            nc.scalar.preload_act_table_set(LN_EXP)
            act.wait_ge(s_vcol, 1)
            for i in range(8):
                if i == 6:
                    split_hi(act, 3, 1)
                act.wait_ge(s_up_mm, i + 1)
                if i > 1:
                    act.wait_ge(s_la, i - 1)
                t = lt[:, 0, i % 2, :]
                A(t, M[i % 4][:, :], ACT.Abs, bias=vcol[:, R_BF + i:R_BF + i + 1]).then_inc(s_la_abs, 1)
                act.wait_ge(s_la_abs, i + 1)
                A(t, t, ACT.Exp, scale=-1.0).then_inc(s_la_exp, 1)
                act.wait_ge(s_la_exp, i + 1)
                A(t, t, ACT.Ln, bias=1.0).then_inc(s_la_ln, 1)
            act.wait_ge(s_bias_row, 2)
            act.dma_start(bias_dram, brow[:, :]).then_inc(s_bias_out, 16)
            act.wait_ge(s_lb, 3)
            A(lbt[:, 3:5, :], lbt[:, 3:5, :], ACT.Exp).then_inc(s_lb, 1)
            A(small[:, 24:32], vcol[:, R_C:R_C + KT], ACT.Sigmoid).then_inc(s_csig, 1)

            def head_evict_qk(h):
                for c, dst, sc in ((0, gq, DK ** -0.5), (1, gk, 1.0)):
                    b, full, _ = TL(U_HEAD, c, 8, h)
                    act.wait_ge(s_acc_full, full)
                    if later(h):
                        act.wait_ge(s_der, h * 6)
                    A(dst[:, :], acc[b][:, :], ACT.Copy, scale=sc).then_inc(s_acc_free[b], 1)

            def head_evict_ga(h):
                for c in range(2):
                    b, full, _ = TL(U_HEAD, 2 + c, 8, h)
                    act.wait_ge(s_acc_full, full)
                    A(cols(sig_ga, h * 2 + c), acc[b][:, :], ACT.Sigmoid).then_inc(s_acc_free[b], 1)

            def head_evict_v(h):
                for c in range(2):
                    b, full, _ = TL(U_HEAD, 4 + c, 8, h)
                    act.wait_ge(s_acc_full, full)
                    act.wait_ge(s_bias_out, 16)
                    A(gv[:, 2 * c:2 * c + 2, :].rearrange("p t v -> p (t v)"), acc[b][:, :], ACT.Copy)\
                        .then_inc(s_acc_free[b], 1)

            def head_evict_r(h):
                for c in range(2):
                    b, full, _ = TL(U_HEAD, 6 + c, 8, h)
                    act.wait_ge(s_acc_full, full)
                    if later(h):
                        act.wait_ge(s_gfin, h * 2 + 1)
                    A(gr[:, c, :], acc[b][:, :], ACT.Sigmoid).then_inc(s_r_sig, 1)

            def derive(h):
                for d in range(2):
                    b = cols(b_all, h + 4 * d)
                    last = b.rearrange("p (n c) -> p n c", c=CHUNK)[:, :, CHUNK - 1 if d == 0 else 0]
                    act.wait_ge(s_b_ready, 8)
                    if later(h * 6 + 3 * d):
                        act.wait_ge(s_der, h * 6 + 3 * d)
                    A(ex[:, 0, :], b, ACT.Exp, scale=1.0 / 16).then_inc(s_gex, 1)
                    A(ex[:, 1, :], b, ACT.Exp, scale=-1.0 / 16).then_inc(s_gex, 1)
                    A(dec[:, d, :], last, ACT.Exp, scale=1.0 / 16).then_inc(s_gdec, 1)
                    act.wait_ge(s_gdf, h * 2 + d + 1)
                    A(ex[:, 2, :], ex[:, 2, :], ACT.Exp, scale=1.0 / 16).then_inc(s_gex, 1)

            def gla_kdT(g):
                for d in range(2):
                    act.wait_ge(s_kd_tr, g * 2 + d + 1)
                    A(kdT[:, d, :, :].rearrange("p t k -> p (t k)"), M[d][:, :], ACT.Copy).then_inc(s_kdT, 1)

            def gla_squares(g):
                for j in range(2):
                    act.wait_ge(s_go, g * 2 + j + 1)
                    A(ex[:, j, :], M[j][:, :], ACT.Square).then_inc(s_gsq, 1)

            def gla_rs(g):
                nc.scalar.preload_act_table_set(LN_EXP)
                act.wait_ge(s_gsum, g + 1)
                A(ex[:, 2, :], M[2][:, :], ACT.Ln, bias=eps_col[:, :]).then_inc(s_gln, 1)
                act.wait_ge(s_gln, g + 1)
                A(ex[:, 2, :], ex[:, 2, :], ACT.Exp, scale=-0.5).then_inc(s_grs, 1)

            def head_split(h, j):
                v = U_HEAD + 1 + j
                split_hi(act, v + h * 4, v % 2, lin=first_tile(v - 1) + h * 8)

            head_evict_qk(0)
            head_evict_ga(0)
            head_split(0, 2)
            head_evict_v(0)
            head_split(0, 3)
            head_evict_r(0)
            derive(0)
            with act.Fori(1, GLA_HEADS) as h:
                g = h - 1
                head_split(h, 0)
                head_evict_qk(h)
                gla_kdT(g)
                head_split(h, 1)
                head_evict_ga(h)
                head_split(h, 2)
                gla_squares(g)
                head_evict_v(h)
                head_split(h, 3)
                gla_rs(g)
                head_evict_r(h)
                derive(h)

            g = GLA_HEADS - 1
            for j in range(2):
                split_hi(act, U_C + j + 1, (U_C + j + 1) % 2)
                for c in range(2):
                    b, full, _ = TL(U_C, 2 * j + c)
                    act.wait_ge(s_acc_full, full)
                    act.wait_ge(s_upad_zero, 1)
                    A(upad[:, 2 * j + c, PAD:PAD + L], acc[b][:, :], ACT.Copy).then_inc(s_acc_free[b], 1)
                if j == 0:
                    gla_kdT(g)
            for j in range(4):
                split_hi(act, U_C + 3 + j, (U_C + 3 + j) % 2, 4 * 2 * P if j == 3 else 16 * P)
                if j == 0:
                    gla_squares(g)
                if j == 1:
                    gla_rs(g)
                if j == 2:
                    for m in range(NG):
                        act.wait_ge(s_gfin, 2 * GLA_HEADS + 1)
                        act.wait_ge(s_pooled, m + 1)
                        A(phi[:, m, :], upad[:, m, PAD:PAD + L], ACT.Copy).then_inc(s_p_hi, 1)
                for c in range(2):
                    b, full, _ = TL(U_C, 4 + 2 * j + c)
                    act.wait_ge(s_acc_full, full)
                    act.wait_ge(s_der, 6 * GLA_HEADS)
                    A(gbm[:, 2 * j + c, :], acc[b][:, :], ACT.Sigmoid).then_inc(s_acc_free[b], 1)
            split_hi(act, U_BR, U_BR % 2)
            act.wait_ge(s_acc_full, first_tile(U_POOL))
            for k in range(KT):
                act.wait_ge(s_gfin, 2 * GLA_HEADS + 1)
                A(hhi[:, k, :], o_all[:, k, :], ACT.Copy).then_inc(s_o_hi, 1)
            for j in range(4):
                split_hi(act, U_BR + j + 1, (U_BR + j + 1) % 2)
                for c in range(2):
                    k = 2 * j + c
                    act.wait_ge(s_merged, k + 1)
                    A(mhi[:, k, :], sig_ga[:, k, :], ACT.Copy).then_inc(s_merge_hi, 1)
            act.wait_ge(s_merge_lo, KT)
            for j in range(4):
                for k in (2 * j, 2 * j + 1):
                    act.wait_ge(s_x_tr, k + 1)
                    A(xres[:, k, :], M[k % 4][:, :], ACT.Copy).then_inc(s_x_res, 1)
                split_hi(act, U_OUT + j + 1, (U_OUT + j + 1) % 2)
                for k in (2 * j, 2 * j + 1):
                    act.wait_ge(*moved(U_OUT, k))
                    norm_square(0, k)

            def ffn_split(i, j):
                v = U_FIN + 1 + j
                split_hi(act, v + i * 2, v % 2, lin=first_tile(v - 1) + i * 4)

            def ffn_tile(i, j):
                b, full, _ = TL(U_FIN, 2 * j, 4, i)
                act.wait_ge(s_acc_full, full)
                A(fsg[:, j, :], acc[b][:, :], ACT.Sigmoid).then_inc(s_f_sig, 1)
                bu, _, free = TL(U_FIN, 2 * j + 1, 4, i)
                act.wait_ge(s_acc_free[bu], free + 1)
                A(cols(ahi, i * 2 + j), faa[:, j, :], ACT.Copy).then_inc(s_f_hi, 1)

            norm_rs(0)
            norm_hi(0, ffn_split)
            ffn_tile(0, 0)
            ffn_split(0, 1)
            ffn_tile(0, 1)
            with act.Fori(1, FT // 2) as i:
                for j in range(2):
                    ffn_split(i, j)
                    ffn_tile(i, j)
            with act.Fori(0, 4) as i:
                for j in range(4):
                    v = U_FOUT + 1 + j
                    split_hi(act, v + i * 4, v % 2, FT // 2 * P if j < 3 else 16 * P, lin=first_tile(v - 1) + i * 4)
                    if j % 2:
                        k = i * 2 + j // 2
                        act.wait_ge(*moved(U_FOUT, j, 4, i))
                        act.wait_ge(s_norm_acc, k + nth(1))
                        A(fsg[:, 0, :], cols(xres, k), ACT.Square).then_inc(s_norm_sq, 1)
                        act.wait_ge(s_mid_acc, k + 1)
                        A(fsg[:, 1, :], cols(xres, k), ACT.Square, scale=col(vcol, k + R_NFIN)).then_inc(s_mid_sq, 1)

            def att_split(i, j):
                v = U_ATT + 1 + j
                split_hi(act, v + i * 2, v % 2, lin=first_tile(v - 1) + i * 4)

            nc.scalar.preload_act_table_set(LN_EXP)
            act.wait_ge(s_eps, 2)
            act.wait_ge(s_mid_sum, 1)
            A(nsq[:, 1, :], M[1][:, :], ACT.Ln, bias=eps2_col[:, :]).then_inc(s_mid_step, 1)
            act.wait_ge(s_mid_step, 2)
            A(nsq[:, 1, :], nsq[:, 1, :], ACT.Exp, scale=-0.5).then_inc(s_mid_step, 1)
            norm_rs(1)
            act.wait_ge(s_mod, 3)
            norm_hi(1, att_split, shift=True)

            def att_copy(i, c, dst, scale=1.0):
                b, full, _ = TL(U_ATT, c, 4, i)
                act.wait_ge(s_acc_full, full)
                A(dst[:, :], acc[b][:, :], ACT.Copy, scale=scale).then_inc(s_acc_free[b], 1)

            def att_evict0(i, first=False):
                if later(i):
                    act.wait_ge(s_score, i * 8)
                att_copy(i, 0, aq, AE ** -0.5)
                att_copy(i, 1, ak)

            def att_evict1(i):
                if later(i):
                    act.wait_ge(s_av_tr, i)
                att_copy(i, 2, av)
                b, full, _ = TL(U_ATT, 3, 4, i)
                act.wait_ge(s_acc_full, full)
                if later(i):
                    act.wait_ge(s_a_out, i + 1)
                A(az[:, :], acc[b][:, :], ACT.Sigmoid).then_inc(s_az_sig, 1)

            def att_vt(g):
                act.wait_ge(s_av_tr, g + 1)
                A(avt[:, :, :].rearrange("p t v -> p (t v)"), M[3][:, :], ACT.Copy).then_inc(s_avt, 1)

            def att_exp(g, a):
                for q in range(TT):
                    n = (q + 1) * P
                    act.wait_ge(s_amax, g * 8 + a * 4 + q + 1)
                    A(apr[:, a, q, 0:n], apr[:, a, q, 0:n], ACT.Exp, bias=amax[:, a, q:q + 1],
                      accum_out=aden[:, a, q:q + 1]).then_inc(s_aexp, 1)

            def att_pt(g, a):
                act.wait_ge(s_apv, g * 2 + a + 1)
                for q in range(TT):
                    act.wait_ge(s_a_tr, g * 8 + a * 4 + q + 1)
                    A(apt[:, 0:q + 1, q * P:(q + 1) * P], M[q % 3][:, 0:(q + 1) * P].rearrange("p (j c) -> p j c", c=P),
                      ACT.Copy).then_inc(s_apt, 1)

            att_evict0(0)
            att_split(0, 1)
            att_evict1(0)

            def att_iteration(i, units):
                g = i - 1
                if units:
                    att_split(i, 0)
                att_vt(g)
                att_exp(g, 0)
                att_pt(g, 0)
                if units:
                    att_evict0(i)
                    att_split(i, 1)
                att_exp(g, 1)
                if units:
                    act.wait_ge(s_logit, i * 8)
                    bias_load(act, i)
                att_pt(g, 1)
                if units:
                    att_evict1(i)

            with act.Fori(1, A_HEADS // 2) as i:
                att_iteration(i, True)
            att_iteration(A_HEADS // 2, False)

            def hg_split(h, j):
                v = U_HG + 1 + j
                split_hi(act, v + h * 2, v % 2, lin=first_tile(v - 1) + h * 4)

            def hg_evict_f(h):
                b, full, _ = TL(U_HG, 1, 4, h)
                act.wait_ge(s_acc_full, full)
                if later(h):
                    act.wait_ge(s_h_b, h)
                A(hf[:, :], acc[b][:, :], ACT.Sigmoid).then_inc(s_acc_free[b], 1)

            def hg_evict_q(h):
                b, full, _ = TL(U_HG, 0, 4, h)
                act.wait_ge(s_acc_full, full)
                if later(h):
                    act.wait_ge(s_h_op, h * 2)
                    act.wait_ge(s_h_w, h * 7)
                    act.wait_ge(s_h_score, h * 8 - 7)
                A(hq[:, :], acc[b][:, :], ACT.Sigmoid).then_inc(s_hq_sig, 1)

            def hg_evict_i(g):
                b, full, _ = TL(U_HG, 2, 4, g)
                act.wait_ge(s_acc_full, full)
                A(hi_[:, :], acc[b][:, :], ACT.Copy).then_inc(s_acc_free[b], 1)

            def hg_evict_z(g):
                b, full, _ = TL(U_HG, 3, 4, g)
                act.wait_ge(s_acc_full, full)
                if later(g):
                    act.wait_ge(s_h_out, g + 1)
                A(hz[:, :], acc[b][:, :], ACT.Sigmoid).then_inc(s_hz_sig, 1)

            def hg_factors(g):
                nc.scalar.preload_act_table_set(LN_EXP)
                act.wait_ge(s_h_fg, g * 2 + 2)
                A(hf[:, :], hf[:, :], ACT.Ln).then_inc(s_h_ln, 1)
                act.wait_ge(s_h_df, g * 8 + 1)
                A(hkd[:, :], hkd[:, :], ACT.Exp).then_inc(s_h_ex, 1)
                act.wait_ge(s_h_b, g + 1)
                A(dec[:, 0, 0:TT], hb[:, :].rearrange("p (n c) -> p n c", c=P)[:, :, P - 1], ACT.Exp)\
                    .then_inc(s_h_ex, 1)
                for lev in range(LEVELS):
                    act.wait_ge(s_h_df, g * 8 + 2 + lev)
                    A(hw[:, lev, :], hw[:, lev, :], ACT.Exp).then_inc(s_h_lex, 1)

            def hg_query(g):
                if later(g):
                    act.wait_ge(s_h_o, g)
                A(hqe[:, :], hb[:, :], ACT.Exp).then_inc(s_h_ex, 1)

            def hg_copies(g):
                act.wait_ge(s_h_itr, g + 1)
                A(hit[:, :, :].rearrange("p t v -> p (t v)"), M[0][:, :], ACT.Copy).then_inc(s_h_cp, 1)
                act.wait_ge(s_h_ktr, g + 1)
                A(hkT[:, :, :].rearrange("p t k -> p (t k)"), M[1][:, :], ACT.Copy).then_inc(s_h_cp, 1)

            def hg_square(g):
                act.wait_ge(s_h_o, g + 1)
                A(hsq[:, :], M[2][:, :], ACT.Square).then_inc(s_h_sq, 1)

            def hg_rs(g):
                act.wait_ge(s_h_sum, g + 1)
                A(hrs[:, :], M[3][:, :], ACT.Ln, bias=eps_col[:, :]).then_inc(s_h_rl, 1)
                act.wait_ge(s_h_rl, g + 1)
                A(hrs[:, :], hrs[:, :], ACT.Exp, scale=-0.5).then_inc(s_h_rs, 1)

            act.wait_ge(s_a_out, A_HEADS // 2 + 1)
            hg_split(0, 0)
            hg_evict_q(0)
            hg_evict_f(0)
            hg_split(0, 1)

            def gate_evict(k):
                b, full, _ = TL(U_G2, k)
                act.wait_ge(s_acc_full, full)
                A((sga if k < KT else sgb)[:, k % KT, :], acc[b][:, :], ACT.Sigmoid).then_inc(s_acc_free[b], 1)

            def hg_iteration(g, last=False):
                hg_factors(g)
                hg_evict_i(g)
                if later(g):
                    hg_square(g - 1)
                if last:
                    split_hi(act, U_G2 + 1, 1)
                else:
                    hg_split(g + 1, 0)
                if later(g):
                    hg_rs(g - 1)
                hg_query(g)
                hg_evict_z(g)
                if last:
                    split_hi(act, U_G2 + 2, 0)
                    gate_evict(0)
                    gate_evict(1)
                    hg_copies(g)
                    gate_evict(2)
                    gate_evict(3)
                else:
                    hg_split(g + 1, 1)
                    hg_evict_f(g + 1)
                    hg_copies(g)
                    hg_evict_q(g + 1)

            hg_iteration(0)
            with act.Fori(1, H_HEADS - 1) as g:
                hg_iteration(g)
            hg_iteration(H_HEADS - 1, last=True)
            hg_square(H_HEADS - 1)

            for j in range(2, 8):
                split_hi(act, U_G2 + j + 1, (j + 1) % 2)
                gate_evict(2 * j)
                if j == 2:
                    hg_rs(H_HEADS - 1)
                gate_evict(2 * j + 1)
                if j == 5:
                    act.wait_ge(s_h_out, H_HEADS + 1)
                    for k in range(AW // P):
                        A(oahi[:, k, :], oa[:, k, :], ACT.Copy).then_inc(s_oa_hi, 1)
            for k in range(KT):
                A(hhi[:, k, :], ob[:, k, :], ACT.Copy).then_inc(s_ob_hi, 1)
            for u in range(U_BA, U_OUT2):
                split_hi(act, u + 1, (u + 1) % 2)
                if u >= U_BB:
                    for c in range(2):
                        k = 2 * (u - U_BB) + c
                        act.wait_ge(s_merge2, k + 1)
                        A(nhi[:, k, :], sgb[:, k, :], ACT.Copy).then_inc(s_n_hi, 1)

            def out_tile(k):
                act.wait_ge(*moved(U_OUT2, k))
                norm_square(2, k)
                A(yT[:, k, :], xres[:, k, :], ACT.Copy, scale=vcol[:, R_FG + k:R_FG + k + 1]).then_inc(s_yT, 1)

            for u in range(U_OUT2, U_END - 1):
                split_hi(act, u + 1, (u + 1) % 2)
                for k in (2 * (u - U_OUT2), 2 * (u - U_OUT2) + 1):
                    out_tile(k)
            for k in (KT - 2, KT - 1):
                out_tile(k)
            nc.scalar.preload_act_table_set(LN_EXP)
            act.wait_ge(s_norm_sum, 3)
            A(xss, M[3][:, 0:TT], ACT.Ln, bias=eps_col[:, :]).then_inc(s_norm_ln, 1)
            act.wait_ge(s_norm_ln, 3)
            A(xrs, xss, ACT.Exp, scale=-0.5).then_inc(s_norm_rs, 1)
            act.wait_ge(s_norm_rs, 3)
            act.wait_ge(s_y_nat, KT)
            for t in (2, 3):
                A(ynat[:, t, :], ynat[:, t, :], ACT.Copy, scale=xrs[:, t:t + 1]).then_inc(s_y_act, 1)

        @block.vector
        def _(dve):
            V = nc.vector

            def hold():
                V.memset(tick[:, 0:1], 0.0)

            for n, started in enumerate((s_gfin, s_a_out, s_apv, s_h_out, s_h_rs)):
                V.memset(tick[:, n + 1:n + 2], 0.0).then_inc(started, 1)
            V.memset(eps_col[:, :], EPS).then_inc(s_eps, 1)
            V.memset(eps2_col[:, :], EPS * EPS).then_inc(s_eps, 1)
            V.memset(one_col[:, :], 1.0).then_inc(s_means, 1)
            for t, width in ((mean_dm, DM), (mean_dv, DV), (mean_p, P)):
                V.memset(t[:, :], 1.0 / width).then_inc(s_means, 1)
            V.memset(rst[:, :], 1.0).then_inc(s_rst, 1)
            dve.wait_ge(s_rst, 1)
            V.memset(rst[:, :].rearrange("p (n c) -> p n c", c=CHUNK)[:, :, 0], 0.0).then_inc(s_rst, 1)

            def norm_zero(n):
                V.memset(nacc[:, :], 0.0).then_inc(s_norm_zero, 1)

            def norm_add(n, k):
                dve.wait_ge(s_norm_sq, nth(n) + k + 1)
                if k == 0:
                    dve.wait_ge(s_norm_zero, n + 1)
                if nth(n) + k > 0:
                    dve.wait_ge(s_norm_acc, nth(n) + k)
                V.tensor_tensor(nacc[:, :], nacc[:, :], nsq[:, k % 2, :], ALU.add).then_inc(s_norm_acc, 1)

            def norm_split(n, g, rs=nrs, shift=False):
                def low(k):
                    dve.wait_ge(s_norm_hi, nth(n + 1) + k + 1)
                    h = hhi[:, k, :].bitcast(f32)
                    if shift:
                        V.scalar_tensor_tensor(hlo[:, k, :], nht[:, k % 2, :], mod[:, k:k + 1], h, ALU.add,
                                               ALU.subtract).then_inc(s_norm_lo, 1)
                    else:
                        V.tensor_tensor(hlo[:, k, :], nht[:, k % 2, :], h, ALU.subtract).then_inc(s_norm_lo, 1)
                for k in range(KT):
                    if k > 1:
                        dve.wait_ge(s_norm_lo, nth(n + 1) + k - 1)
                    V.scalar_tensor_tensor(nht[:, k % 2, :], xres[:, k, :], g(k), rs[:, :], ALU.mult, ALU.mult)\
                        .then_inc(s_norm_ht, 1)
                    if k >= 1:
                        low(k - 1)
                low(KT - 1)

            for t in range(TT):
                dve.wait_ge(s_x_rms, 3 * t + 3)
                V.tensor_scalar(xnat[:, t, :], xnat[:, t, :], xrs[:, t:t + 1], None, ALU.mult).then_inc(s_x_n, 1)
            dve.wait_ge(s_gain, 1)
            for k in range(KT):
                dve.wait_ge(s_norm_hi, k + 1)
                V.scalar_tensor_tensor(hlo[:, k, :], x_bank(k)[:, :], vcol[:, R_NM + k:R_NM + k + 1],
                                       hhi[:, k, :].bitcast(f32), ALU.mult, ALU.subtract).then_inc(s_norm_lo, 1)

            dve.wait_ge(s_vcol, 1)
            for i in range(8):
                dve.wait_ge(s_la_abs, i + 1)
                V.tensor_scalar(lt[:, 1, i % 2, :], M[i % 4][:, :], vcol[:, R_BF + i:R_BF + i + 1], 0.0,
                                ALU.add, ALU.min).then_inc(s_la_min, 1)
                dve.wait_ge(s_la_ln, i + 1)
                dve.wait_ge(s_la_min, i + 1)
                V.tensor_tensor(lt[:, 1, i % 2, :], lt[:, 1, i % 2, :], lt[:, 0, i % 2, :], ALU.subtract)\
                    .then_inc(s_la, 1)
                dve.wait_ge(s_la, i + 1)
                dve.wait_ge(s_rst, 2)
                o, a = (b_all[:, i, :], lt[:, 1, i % 2, :]) if i < 4 else (b_all[:, i, ::-1], lt[:, 1, i % 2, ::-1])
                V.tensor_tensor_scan(o, rst[:, :], a, 0.0, ALU.mult, ALU.add).then_inc(s_b_ready, 1)

            dve.wait_ge(s_vcol, 1)
            lb0, lb1 = vcol[:, R_LB0:R_LB0 + 8], vcol[:, R_LB1:R_LB1 + 8]
            V.tensor_tensor(lbt[:, 2, :], lb0, lb1, ALU.max).then_inc(s_lb, 1)
            dve.wait_ge(s_lb, 1)
            V.tensor_tensor(lbt[:, 3, :], lb0, lbt[:, 2, :], ALU.subtract).then_inc(s_lb, 1)
            V.tensor_tensor(lbt[:, 4, :], lb1, lbt[:, 2, :], ALU.subtract).then_inc(s_lb, 1)
            dve.wait_ge(s_csig, 1)
            V.tensor_tensor(silu_c, vcol[:, R_C:R_C + KT], small[:, 24:32], ALU.mult).then_inc(s_silu_c, 1)
            dve.wait_ge(s_lb, 4)
            V.tensor_tensor(lbt[:, 5, :], lbt[:, 3, :], lbt[:, 4, :], ALU.add).then_inc(s_lb, 1)
            dve.wait_ge(s_lb, 5)
            V.reciprocal(lbt[:, 5, :], lbt[:, 5, :]).then_inc(s_lb, 1)
            dve.wait_ge(s_lb, 6)
            V.tensor_tensor(lbt[:, 0, :], lbt[:, 3, :], lbt[:, 5, :], ALU.mult).then_inc(s_lb, 1)
            dve.wait_ge(s_lb, 7)
            V.tensor_scalar(lbt[:, 1, :], lbt[:, 0, :], -1.0, 1.0, ALU.mult, ALU.add).then_inc(s_lb, 1)

            def gla_derive(h):
                dve.wait_ge(*moved(U_HEAD, 0, 8, h))
                dve.wait_ge(*moved(U_HEAD, 1, 8, h))
                dve.wait_ge(s_b_ready, 8)
                for d in range(2):
                    b = cols(b_all, h + 4 * d).rearrange("p (n c) -> p n c", c=CHUNK)
                    e = CHUNK - 1 if d == 0 else 0
                    last = b[:, :, e:e + 1].to_broadcast([P, NCH, CHUNK])
                    if later(h * 6 + 3 * d):
                        dve.wait_ge(s_der, h * 6 + 3 * d)
                    V.tensor_tensor(ex[:, 2, :].rearrange("p (n c) -> p n c", c=CHUNK), last, b, ALU.subtract)\
                        .then_inc(s_gdf, 1)
                    dve.wait_ge(s_gex, h * 6 + 3 * d + 1)
                    V.tensor_tensor(qe[:, d, :], gq[:, :], ex[:, 0, :], ALU.mult).then_inc(s_der, 1)
                    dve.wait_ge(s_gex, h * 6 + 3 * d + 2)
                    V.tensor_tensor(ke[:, d, :], gk[:, :], ex[:, 1, :], ALU.mult).then_inc(s_der, 1)
                    dve.wait_ge(s_gex, h * 6 + 3 * d + 3)
                    V.tensor_tensor(kd[:, d, :], gk[:, :], ex[:, 2, :], ALU.mult).then_inc(s_der, 1)

            def head_r(h):
                for c in range(2):
                    b, _, _ = TL(U_HEAD, 6 + c, 8, h)
                    dve.wait_ge(s_r_sig, h * 2 + c + 1)
                    V.tensor_tensor(gr[:, c, :], gr[:, c, :], acc[b][:, :], ALU.mult).then_inc(s_acc_free[b], 1)

            def gla_mask(g):
                V.memset(ga_sc[:, :, :], 0.0).then_inc(s_gmask, 1)
                for d in range(2):
                    dve.wait_ge(s_gsc, g * 2 + d + 1)
                    dve.wait_ge(s_gmask, g * 3 + d + 1)
                    dve.wait_ge(s_masks, 1)
                    hold()
                    m = masks[:, d:d + 1, :].to_broadcast([P, TT, P])
                    V.copy_predicated(ga_sc[:, :, :], m, M[2 + d][:, :].rearrange("p (t c) -> p t c", c=P))\
                        .then_inc(s_gmask, 1)

            def gla_states(g):
                for s in range(NCH - 1):
                    for d in range(2):
                        kv = M[2 * d + s % 2][:, 0:DV]
                        dve.wait_ge(s_kv, g * 14 + 2 * s + d + 1)
                        if s == 0:
                            V.tensor_copy(st[:, d, 0, :], kv).then_inc(s_gst, 1)
                        else:
                            n = s if d == 0 else NCH - 1 - s
                            dve.wait_ge(s_gst, g * 14 + 2 * s + d - 1)
                            dve.wait_ge(s_gdec, g * 2 + d + 1)
                            V.scalar_tensor_tensor(st[:, d, s, :], st[:, d, s - 1, :], dec[:, d, n:n + 1], kv,
                                                   ALU.mult, ALU.add).then_inc(s_gst, 1)

            def gla_square_sum(g):
                dve.wait_ge(s_gsq, g * 2 + 2)
                V.tensor_tensor(ex[:, 0, :], ex[:, 0, :], ex[:, 1, :], ALU.add).then_inc(s_gsq_sum, 1)

            def gla_final(g):
                dve.wait_ge(s_grs, g + 1)
                for j in range(2):
                    V.scalar_tensor_tensor(ex[:, j, :], M[j][:, :], col(vcol, g * 2 + (R_GN + j)), ex[:, 2, :],
                                           ALU.mult, ALU.mult).then_inc(s_gt, 1)
                for j in range(2):
                    b, _, free = TL(U_HEAD, 6 + j, 8, g)
                    dve.wait_ge(s_gt, g * 2 + j + 1)
                    dve.wait_ge(s_acc_free[b], free + 1)
                    V.tensor_tensor(cols(o_all, g * 2 + j), ex[:, j, :], gr[:, j, :], ALU.mult)\
                        .then_inc(s_gfin, 1)

            head_r(0)
            gla_derive(0)
            with dve.Fori(1, GLA_HEADS) as h:
                gla_mask(h - 1)
                gla_states(h - 1)
                gla_square_sum(h - 1)
                gla_final(h - 1)
                head_r(h)
                gla_derive(h)
            g = GLA_HEADS - 1
            V.memset(upad[:, :, :], 0.0).then_inc(s_upad_zero, 1)
            gla_mask(g)
            gla_states(g)

            n_adds = 0
            for m, w in enumerate(POOL_WINDOWS):
                dve.wait_ge(*moved(U_C, m))
                if m > 0:
                    dve.wait_ge(s_pool_mid, m)
                if m > 0:
                    dve.wait_ge(s_pool_side, m)
                if m > 0:
                    dve.wait_ge(s_pooled, m)
                src, n, step, flip = upad[:, m, :], L + 2 * PAD, 1, 0
                while step < w:
                    n -= step
                    dst = (ptmp, ptmp2)[flip][:, 0:n]
                    V.tensor_tensor(dst, src[:, 0:n], src[:, step:step + n], ALU.add).then_inc(s_pool_add, 1)
                    n_adds += 1
                    dve.wait_ge(s_pool_add, n_adds)
                    src, flip, step = dst, 1 - flip, step * 2
                sums = src[:, PAD - w // 2:PAD - w // 2 + L]
                edges = (ptmp, ptmp2)[flip]
                dve.wait_ge(s_edge_in, 16)
                for side, c0 in ((0, 0), (1, L - PAD)):
                    V.tensor_tensor(edges[:, side * PAD:(side + 1) * PAD], sums[:, c0:c0 + PAD],
                                    edge[:, m, side * PAD:(side + 1) * PAD], ALU.mult).then_inc(s_pool_edge, 1)
                u = upad[:, m, PAD:PAD + L]
                V.scalar_tensor_tensor(u[:, PAD:L - PAD], sums[:, PAD:L - PAD], 1.0 / w, u[:, PAD:L - PAD],
                                       ALU.mult, ALU.subtract).then_inc(s_pool_mid, 1)
                dve.wait_ge(s_pool_edge, 2 * m + 2)
                for side, c0 in ((0, 0), (1, L - PAD)):
                    V.tensor_tensor(u[:, c0:c0 + PAD], edges[:, side * PAD:(side + 1) * PAD], u[:, c0:c0 + PAD],
                                    ALU.subtract).then_inc(s_pool_side if side == 0 else s_pooled, 1)
            gla_square_sum(g)
            gla_final(g)
            dve.wait_ge(s_gfin, 2 * GLA_HEADS + 1)

            for g in range(NG):
                dve.wait_ge(s_p_hi, g + 1)
                dve.wait_ge(s_pool_mid, g + 1)
                dve.wait_ge(s_pool_side, g + 1)
                dve.wait_ge(s_pooled, g + 1)
                V.tensor_tensor(plo[:, g, :], upad[:, g, PAD:PAD + L], phi[:, g, :].bitcast(f32), ALU.subtract)\
                    .then_inc(s_p_lo, 1)
            for k in range(KT):
                b, full, free = TL(U_POOL, k)
                dve.wait_ge(s_acc_full, full)
                dve.wait_ge(*moved(U_C, 4 + k))
                V.scalar_tensor_tensor(gbm[:, k, :], acc[b][:, :], vcol[:, R_PS + k:R_PS + k + 1], gbm[:, k, :],
                                       ALU.mult, ALU.mult).then_inc(s_acc_free[b], 1)
                dve.wait_ge(s_o_hi, k + 1)
                V.tensor_tensor(hlo[:, k, :], o_all[:, k, :], hhi[:, k, :].bitcast(f32), ALU.subtract)\
                    .then_inc(s_o_lo, 1)
            for k in range(KT):
                b, full, free = TL(U_BR, k)
                dve.wait_ge(s_acc_full, full)
                V.tensor_tensor(sig_ga[:, k, :], sig_ga[:, k, :], acc[b][:, :], ALU.mult)\
                    .then_inc(s_acc_free[b], 1)
                dve.wait_ge(s_acc_free[b], free + 1)
                V.tensor_tensor(sig_ga[:, k, :], sig_ga[:, k, :], gbm[:, k, :], ALU.add).then_inc(s_merged, 1)
                dve.wait_ge(s_merge_hi, k + 1)
                V.tensor_tensor(mlo[:, k, :], sig_ga[:, k, :], mhi[:, k, :].bitcast(f32), ALU.subtract)\
                    .then_inc(s_merge_lo, 1)
            norm_zero(0)
            for k in range(KT):
                b, full, free = TL(U_OUT, k)
                dve.wait_ge(s_acc_full, full)
                dve.wait_ge(s_x_res, k + 1)
                V.tensor_tensor(xres[:, k, :], xres[:, k, :], acc[b][:, :], ALU.add).then_inc(s_acc_free[b], 1)
                norm_add(0, k)

            dve.wait_ge(s_norm_rs, 1)
            norm_split(0, lambda k: vcol[:, R_NF + k:R_NF + k + 1])

            def ada_tile(n, slot):
                w = ada[:, slot, :, :]
                dve.wait_ge(s_ada_in[slot], (n - slot) * 8 + 16)
                V.tensor_tensor(w, w, silu_c.rearrange("p (k o) -> p k o", o=1).to_broadcast([P, KT, P]), ALU.mult)\
                    .then_inc(s_ada_step, 1)
                dve.wait_ge(s_ada_step, n * 3 + 1)
                V.tensor_tensor(w[:, 0:4, :], w[:, 0:4, :], w[:, 4:8, :], ALU.add).then_inc(s_ada_step, 1)
                dve.wait_ge(s_ada_step, n * 3 + 2)
                V.tensor_tensor(w[:, 0:2, :], w[:, 0:2, :], w[:, 2:4, :], ALU.add).then_inc(s_ada_step, 1)
                dve.wait_ge(s_ada_step, n * 3 + 3)
                V.tensor_tensor(w[:, 0, :], w[:, 0, :], w[:, 1, :], ALU.add).then_inc(s_ada_sum, 1)

            dve.wait_ge(s_silu_c, 1)
            with dve.Fori(0, FT // 2) as i:
                for j in range(2):
                    ada_tile(i * 2 + j, j)
                    bg, _, gfree = TL(U_FIN, 2 * j, 4, i)
                    bu, full, ufree = TL(U_FIN, 2 * j + 1, 4, i)
                    dve.wait_ge(s_f_sig, i * 2 + j + 1)
                    V.tensor_tensor(fsg[:, j, :], fsg[:, j, :], acc[bg][:, :], ALU.mult)\
                        .then_inc(s_acc_free[bg], 1)
                    dve.wait_ge(s_acc_full, full)
                    dve.wait_ge(s_acc_free[bg], gfree + 1)
                    V.tensor_tensor(faa[:, j, :], fsg[:, j, :], acc[bu][:, :], ALU.mult)\
                        .then_inc(s_acc_free[bu], 1)
                    dve.wait_ge(s_f_hi, i * 2 + j + 1)
                    V.tensor_tensor(cols(alo, i * 2 + j), faa[:, j, :], cols(ahi, i * 2 + j).bitcast(f32),
                                    ALU.subtract).then_inc(s_f_lo, 1)
            dve.wait_ge(s_f_lo, FT)
            V.memset(faa[:, 0, :], 0.0).then_inc(s_norm_zero, 1)
            V.memset(faa[:, 1, :], 0.0).then_inc(s_mid_acc, 1)
            dve.wait_ge(s_norm_zero, 2)

            def ffn_out(i):
                for j in range(4):
                    b, full, _ = TL(U_FOUT, j, 4, i)
                    dve.wait_ge(s_acc_full, full)
                    if j:
                        dve.wait_ge(s_acc_free[(b - 1) % 4], TL(U_FOUT, j - 1, 4, i)[2] + 1)
                    x = cols(xres, i * 2 + j // 2)
                    V.tensor_tensor(x, x, acc[b][:, :], ALU.add).then_inc(s_acc_free[b], 1)
                    if j % 2:
                        k = i * 2 + j // 2
                        dve.wait_ge(s_norm_sq, k + (nth(1) + 1))
                        dve.wait_ge(s_norm_acc, k + nth(1))
                        V.tensor_tensor(faa[:, 0, :], faa[:, 0, :], fsg[:, 0, :], ALU.add).then_inc(s_norm_acc, 1)
                        dve.wait_ge(s_mid_sq, k + 1)
                        dve.wait_ge(s_mid_acc, k + 1)
                        V.tensor_tensor(faa[:, 1, :], faa[:, 1, :], fsg[:, 1, :], ALU.add).then_inc(s_mid_acc, 1)

            ada_tile(FT, 0)
            ada_tile(FT + 1, 1)
            ffn_out(0)
            dve.wait_ge(s_ada_used, FT + 2)
            V.tensor_tensor(mod[:, :], M[2][:, 0:24], vcol[:, R_ADA:R_ADA + 24], ALU.add).then_inc(s_mod, 1)
            dve.wait_ge(s_mod, 1)
            V.scalar_tensor_tensor(g2_col, mod[:, KT:2 * KT], 1.0, vcol[:, R_NG2:R_NG2 + KT], ALU.add, ALU.mult)\
                .then_inc(s_mod, 1)
            dve.wait_ge(s_mod, 2)
            V.tensor_tensor(mid_col, g2_col, vcol[:, R_NFIN:R_NFIN + KT], ALU.mult).then_inc(s_mod, 1)
            with dve.Fori(1, 4) as i:
                ffn_out(i)

            dve.wait_ge(s_norm_acc, nth(1) + KT)
            dve.wait_ge(s_mid_acc, KT + 1)
            V.scalar_tensor_tensor(fsg[:, 0, :], faa[:, 0, :], EPS, faa[:, 1, :], ALU.mult, ALU.add)\
                .then_inc(s_mid_step, 1)
            dve.wait_ge(s_mid_step, 3)
            dve.wait_ge(s_mod, 3)
            norm_split(1, lambda k: small[:, k:k + 1], nsq[:, 1, :], shift=True)
            dve.wait_ge(s_norm_rs, 2)
            dve.wait_ge(s_norm_ht, nth(1) + KT)
            for k in range(KT):
                V.scalar_tensor_tensor(xres[:, k, :], xres[:, k, :], vcol[:, R_NFIN + k:R_NFIN + k + 1], nrs[:, :],
                                       ALU.mult, ALU.mult).then_inc(s_x_mid, 1)

            def att_logits(g, a):
                dve.wait_ge(s_bias_in, g * 32 + 32)
                for q in range(TT):
                    n = (q + 1) * P
                    dve.wait_ge(s_score, g * 8 + a * 4 + q + 1)
                    hold()
                    V.tensor_tensor_reduce(out=apr[:, a, q, 0:n], in0=M[q][:, 0:n], in1=abias[:, a, n - 1::-1],
                                           scale=1.0, scalar=NEG_INF, op0=ALU.add, op1=ALU.max,
                                           accum_out=amax[:, a, q:q + 1]).then_inc(s_logit, 1)
                    dve.wait_ge(s_logit, g * 8 + a * 4 + q + 1)
                    V.tensor_scalar(amax[:, a, q:q + 1], amax[:, a, q:q + 1], -1.0, None, ALU.mult)\
                        .then_inc(s_amax, 1)

            def att_normalise(g, a):
                for q in range(TT):
                    n = (q + 1) * P
                    dve.wait_ge(s_aexp, g * 8 + a * 4 + q + 1)
                    V.reciprocal(aden[:, a, q:q + 1], aden[:, a, q:q + 1]).then_inc(s_arec, 1)
                    dve.wait_ge(s_arec, g * 8 + a * 4 + q + 1)
                    V.tensor_scalar(apr[:, a, q, 0:n], apr[:, a, q, 0:n], aden[:, a, q:q + 1], None, ALU.mult)\
                        .then_inc(s_aprob, 1)

            def att_out(g):
                dve.wait_ge(s_apv, g * 2 + 3)
                b, _, free = TL(U_ATT, 3, 4, g)
                dve.wait_ge(s_acc_free[b], free + 1)
                V.tensor_tensor(cols(oa, g), az[:, :], M[3][:, :], ALU.mult).then_inc(s_a_out, 1)

            def att_z(i):
                b, _, _ = TL(U_ATT, 3, 4, i)
                dve.wait_ge(s_az_sig, i + 1)
                V.tensor_tensor(az[:, :], az[:, :], acc[b][:, :], ALU.mult).then_inc(s_acc_free[b], 1)

            def att_head_pair(g):
                att_logits(g, 0)
                att_normalise(g, 0)
                att_logits(g, 1)
                att_normalise(g, 1)
                att_out(g)

            att_z(0)
            with dve.Fori(1, A_HEADS // 2) as i:
                att_head_pair(i - 1)
                att_z(i)
            att_head_pair(A_HEADS // 2 - 1)

            V.memset(hrst[:, :], 1.0).then_inc(s_hrst, 1)
            dve.wait_ge(s_hrst, 1)
            V.memset(hrst[:, :].rearrange("p (n c) -> p n c", c=P)[:, :, 0], 0.0).then_inc(s_hrst, 1)

            def hg_gate(dst, sigmoid, c, h):
                b, _, _ = TL(U_HG, c, 4, h)
                dve.wait_ge(sigmoid, h + 1)
                V.tensor_tensor(dst[:, :], dst[:, :], acc[b][:, :], ALU.mult).then_inc(s_acc_free[b], 1)

            def hg_factors(g):
                dve.wait_ge(*moved(U_HG, 0, 4, g))
                dve.wait_ge(*moved(U_HG, 1, 4, g))
                dve.wait_ge(s_lb, 8)
                V.tensor_scalar(hf[:, :], hf[:, :], col(lbt[:, 1, :], g), col(lbt[:, 0, :], g), ALU.mult, ALU.add)\
                    .then_inc(s_h_fg, 1)
                dve.wait_ge(s_h_fg, g * 2 + 1)
                V.tensor_scalar(hk[:, :], hf[:, :], -1.0, 1.0, ALU.mult, ALU.add).then_inc(s_h_fg, 1)
                dve.wait_ge(s_h_ln, g + 1)
                dve.wait_ge(s_hrst, 2)
                V.tensor_tensor_scan(hb[:, :], hrst[:, :], hf[:, :], 0.0, ALU.mult, ALU.add).then_inc(s_h_b, 1)
                dve.wait_ge(s_h_b, g + 1)
                b = hb[:, :].rearrange("p (n c) -> p n c", c=P)
                V.tensor_tensor(hkd[:, :].rearrange("p (n c) -> p n c", c=P),
                                b[:, :, P - 1:P].to_broadcast([P, TT, P]), b, ALU.subtract).then_inc(s_h_df, 1)
                for lev in range(LEVELS):
                    half = 1 << lev
                    nb = L // (2 * half)
                    bb = hb[:, :].rearrange("p (n c) -> p n c", c=2 * half)
                    ww = hw[:, lev, :].rearrange("p (n c) -> p n c", c=2 * half)
                    mid = bb[:, :, half - 1:half].to_broadcast([P, nb, half])
                    V.tensor_tensor(ww[:, :, 0:half], mid, bb[:, :, 0:half], ALU.subtract)
                    V.tensor_tensor(ww[:, :, half:], bb[:, :, half:], mid, ALU.subtract).then_inc(s_h_df, 1)
                dve.wait_ge(s_h_ex, g * 3 + 1)
                dve.wait_ge(s_h_fg, g * 2 + 2)
                V.tensor_tensor(hkd[:, :], hkd[:, :], hk[:, :], ALU.mult).then_inc(s_h_op, 1)
                for lev in range(LEVELS):
                    half = 1 << lev
                    v3 = lambda t: t.rearrange("p (n c) -> p n c", c=2 * half)
                    ww = v3(hw[:, lev, :])
                    dve.wait_ge(s_h_lex, g * 7 + lev + 1)
                    V.tensor_tensor(ww[:, :, 0:half], ww[:, :, 0:half], v3(hk[:, :])[:, :, 0:half], ALU.mult)
                    V.tensor_tensor(ww[:, :, half:], ww[:, :, half:], v3(hq[:, :])[:, :, half:], ALU.mult)\
                        .then_inc(s_h_w, 1)

            def hg_query(g):
                dve.wait_ge(s_h_ex, g * 3 + 3)
                V.tensor_tensor(hqe[:, :], hqe[:, :], hq[:, :], ALU.mult).then_inc(s_h_op, 1)

            def hg_mask(g):
                V.memset(hsc[:, :, :], 0.0).then_inc(s_h_mask, 1)
                for n in range(LEVELS + 1):
                    dve.wait_ge(s_h_score, g * 8 + n + 1)
                    dve.wait_ge(s_h_mask, g * 9 + n + 1)
                    dve.wait_ge(s_masks, 1)
                    hold()
                    scores = M[(n + 2) % 4][:, :]
                    if n == 0:
                        m = masks[:, 2 + LEVELS:3 + LEVELS, :].to_broadcast([P, TT, P])
                        V.copy_predicated(hsc[:, :, :], m, scores.rearrange("p (t c) -> p t c", c=P))\
                            .then_inc(s_h_mask, 1)
                    else:
                        half = 1 << (n - 1)
                        nb = P // (2 * half)
                        m = masks[:, n + 1, :].rearrange("p (o n c) -> p o n c", o=1, c=2 * half)[:, :, :, half:]
                        V.copy_predicated(hsc[:, :, :].rearrange("p t (n c) -> p t n c", c=2 * half)[:, :, :, half:],
                                          m.to_broadcast([P, TT, nb, half]),
                                          scores.rearrange("p (t n c) -> p t n c", t=TT, c=2 * half)[:, :, :, half:])\
                            .then_inc(s_h_mask, 1)

            def hg_states(g):
                dve.wait_ge(s_h_kv, g + 1)
                dve.wait_ge(s_h_ex, g * 3 + 2)
                for n in range(TT - 1):
                    kv = M[3][:, n * P:(n + 1) * P]
                    if n == 0:
                        V.tensor_copy(hst[:, 0, :], kv).then_inc(s_h_st, 1)
                    else:
                        dve.wait_ge(s_h_st, g * 3 + n)
                        V.scalar_tensor_tensor(hst[:, n, :], hst[:, n - 1, :], dec[:, 0, n:n + 1], kv, ALU.mult,
                                               ALU.add).then_inc(s_h_st, 1)

            def hg_final(g):
                dve.wait_ge(s_h_rs, g + 2)
                V.scalar_tensor_tensor(hsq[:, :], M[2][:, :], vcol[:, R_ON:R_ON + 1], hrs[:, :], ALU.mult, ALU.mult)\
                    .then_inc(s_h_t, 1)
                dve.wait_ge(s_h_t, g + 1)
                b, _, free = TL(U_HG, 3, 4, g)
                dve.wait_ge(s_acc_free[b], free + 1)
                V.tensor_tensor(cols(ob, g), hsq[:, :], hz[:, :], ALU.mult).then_inc(s_h_out, 1)

            hg_gate(hq, s_hq_sig, 0, 0)

            def hg_iteration(g, last=False):
                hg_factors(g)
                if later(g):
                    hg_final(g - 1)
                hg_query(g)
                hg_gate(hz, s_hz_sig, 3, g)
                hg_mask(g)
                hg_states(g)
                if not last:
                    hg_gate(hq, s_hq_sig, 0, g + 1)

            hg_iteration(0)
            with dve.Fori(1, H_HEADS - 1) as g:
                hg_iteration(g)
            hg_iteration(H_HEADS - 1, last=True)
            hg_final(H_HEADS - 1)

            for k in range(AW // P):
                dve.wait_ge(s_oa_hi, k + 1)
                V.tensor_tensor(oalo[:, k, :], oa[:, k, :], oahi[:, k, :].bitcast(f32), ALU.subtract)\
                    .then_inc(s_oa_lo, 1)
            for k in range(KT):
                dve.wait_ge(s_ob_hi, k + 1)
                V.tensor_tensor(hlo[:, k, :], ob[:, k, :], hhi[:, k, :].bitcast(f32), ALU.subtract)\
                    .then_inc(s_ob_lo, 1)
            for k in range(KT):
                b, full, _ = TL(U_BA, k)
                dve.wait_ge(s_acc_full, full)
                dve.wait_ge(*moved(U_G2, k))
                V.tensor_tensor(sga[:, k, :], sga[:, k, :], acc[b][:, :], ALU.mult).then_inc(s_acc_free[b], 1)
            for k in range(KT):
                b, full, free = TL(U_BB, k)
                dve.wait_ge(s_acc_full, full)
                dve.wait_ge(*moved(U_G2, KT + k))
                V.tensor_tensor(sgb[:, k, :], sgb[:, k, :], acc[b][:, :], ALU.mult).then_inc(s_acc_free[b], 1)
                dve.wait_ge(s_acc_free[b], free + 1)
                dve.wait_ge(*moved(U_BA, k))
                V.tensor_tensor(sgb[:, k, :], sgb[:, k, :], sga[:, k, :], ALU.add).then_inc(s_merge2, 1)
                dve.wait_ge(s_n_hi, k + 1)
                V.tensor_tensor(nlo[:, k, :], sgb[:, k, :], nhi[:, k, :].bitcast(f32), ALU.subtract)\
                    .then_inc(s_n_lo, 1)
            norm_zero(2)
            dve.wait_ge(s_x_mid, KT)

            def y_evict(k):
                dve.wait_ge(s_y_tr, k + 1)
                V.tensor_copy(ynat[:, :, k * P:(k + 1) * P], M[k % 3][:, :].rearrange("p (t c) -> p t c", c=P))\
                    .then_inc(s_y_nat, 1)

            for k in range(KT):
                for m in {4: (0, 1), 5: (2,), 6: (3,), 7: (4, 5)}.get(k, ()):
                    y_evict(m)
                b, full, _ = TL(U_OUT2, k)
                dve.wait_ge(s_acc_full, full)
                V.scalar_tensor_tensor(xres[:, k, :], acc[b][:, :], mod[:, 2 * KT + k:2 * KT + k + 1], xres[:, k, :],
                                       ALU.mult, ALU.add).then_inc(s_acc_free[b], 1)
                norm_add(2, k)
            y_evict(6)
            y_evict(7)
            dve.wait_ge(s_norm_rs, 3)
            dve.wait_ge(s_y_nat, KT)
            for t in (0, 1):
                V.tensor_scalar(ynat[:, t, :], ynat[:, t, :], xrs[:, t:t + 1], None, ALU.mult).then_inc(s_y_dve, 1)


        @block.gpsimd
        def _(pool):
            nc.gpsimd.memset(vrow[:, :], 0.0).then_inc(s_vrow_zero, 1)
            nc.gpsimd.memset(wup[:, :, :], 0.0).then_inc(s_vrow_zero, 1)
            nc.gpsimd.memset(relb[:, :], 1.0).then_inc(s_vrow_zero, 1)
            pool.wait_ge(s_vrow_zero, 3)
            pool.dma_start(relb[0:N_BUCKETS, :], inp["rel_bias_2"]).then_inc(s_bias_src, 16)
            pool.dma_start(hot[:, :], inp["hot"]).then_inc(s_bias_src, 16)
            pool.dma_start(mask_src[:, :, :], inp["masks"]).then_inc(s_mask_src, 16)
            e = inp["edge"]
            pool.dma_start(edge[:, :, :].rearrange("p g c -> p (g c)"),
                          bass.AP(tensor=e.tensor, offset=0, ap=[[0, P], [1, NG * 2 * PAD]])).then_inc(s_edge_in, 16)
            pool.dma_start(wup[0:RANK, 0, :], inp["w_decay_up_fwd"][0]).then_inc(s_wup_in, 16)
            pool.dma_start(wup[RANK:2 * RANK, 1, :], inp["w_decay_up_bwd"][0]).then_inc(s_wup_in, 16)
            split_lo(pool, 0, 0, KT * P)
            split_lo(pool, 1, 1)
            split_lo(pool, 2, 0)
            pool.wait_ge(s_mask_src, 16)
            nc.gpsimd.tensor_copy(masks[:, :, :], mask_src[:, :, :]).then_inc(s_masks, 1)
            with pool.Fori(1, (U_POOL - 1) // 2) as i:
                split_lo(pool, i * 2 + 1, 1)
                split_lo(pool, i * 2 + 2, 0)
            split_lo(pool, U_POOL, 1, 4 * 2 * P)
            for start, end, n in ((U_BR, U_FOUT, 16 * P), (U_FOUT, U_ATT, FT // 2 * P), (U_ATT, U_END, 16 * P)):
                with pool.Fori(0, (end - start) // 2) as i:
                    split_lo(pool, i * 2 + start, 0, n)
                    split_lo(pool, i * 2 + start + 1, 1, n)

        @block.tensor
        def _(pe):
            mm = nc.tensor.matmul

            def tile(u0, c, slot, j, per=0, i=0, nk=KT, ncol=2 * P, xh=hhi, xl=hlo):
                b, _, free = TL(u0, c, per, i)
                if later(free):
                    pe.wait_ge(s_acc_free[b], free)
                pe_tile(b, slot, j, nk, ncol, xh, xl)

            def unit_as_ready(u0, slot, ready, base, per=2, xh=hhi, xl=hlo, nk=KT):
                banks = []
                for j in range(per):
                    b, _, free = TL(u0, j)
                    pe.wait_ge(s_acc_free[b], free)
                    banks.append(b)
                for k in range(nk):
                    pe.wait_ge(ready, base + k + 1)
                    for j, b in enumerate(banks):
                        o, js = acc[b][:, :], slice((k * per + j) * P, (k * per + j + 1) * P)
                        mm(o, whi[:, slot, js], xh[:, k, :], start=(k == 0), stop=False)
                        mm(o, whi[:, slot, js], xl[:, k, :], start=False, stop=False)
                        last = mm(o, wlo[:, slot, js], xh[:, k, :], start=False, stop=(k == nk - 1))
                        if k == nk - 1:
                            last.then_inc(s_acc_full, 1)

            def units(u0, n, xh=hhi, xl=hlo, nk=KT, ncol=2 * P, ready=None, base=0):
                per = ncol // P
                for m in range(n):
                    pe.wait_ge(s_unit_lo, u0 + m + 1)
                    if m == 0 and ready is not None:
                        unit_as_ready(u0, u0 % 2, ready, base, per, xh, xl, nk)
                        continue
                    for j in range(per):
                        tile(u0, per * m + j, (u0 + m) % 2, j, nk=nk, ncol=ncol, xh=xh, xl=xl)

            def norm_mean(n):
                pe.wait_ge(s_means, 4)
                pe.wait_ge(s_norm_acc, nth(n) + KT)
                if n == 1:
                    pe.wait_ge(s_mid_step, 1)
                    mm(M[1][:, :], mean_dm[:, :], fsg[:, 0, :], start=True, stop=True).then_inc(s_mid_sum, 1)
                    mm(M[3][:, :], mean_dm[:, :], faa[:, 0, :], start=True, stop=True).then_inc(s_norm_sum, 1)
                else:
                    mm(M[3][:, :], mean_dm[:, :], nacc[:, :], start=True, stop=True).then_inc(s_norm_sum, 1)

            pe.wait_ge(s_id_in, 16)
            pe.wait_ge(s_gain_in, 16)
            nc.tensor.transpose(M[0][:, 0:KT], grow[:, :], ident[0:KT, 0:KT]).then_inc(s_gain_mm, 1)
            for t in range(TT):
                pe.wait_ge(s_x_n, t + 1)
                for k in range(KT):
                    if t == 0 and k == 4:
                        pe.wait_ge(s_gain, 1)
                    last = nc.tensor.transpose(x_bank(k)[:, t * P:(t + 1) * P], xnat[:, t, k * P:(k + 1) * P],
                                               ident[:, :])
                    if t == TT - 1:
                        last.then_inc(s_xT, 1)

            pe.wait_ge(s_unit_lo, 0 + 1)
            b, _, _ = TL(U_LR, 0)
            for k in range(KT):
                pe.wait_ge(s_norm_lo, k + 1)
                ks = slice(k * P, (k + 1) * P)
                mm(acc[b][:, :], whi[:, 0, ks], hhi[:, k, :], start=(k == 0), stop=False)
                mm(acc[b][:, :], whi[:, 0, ks], hlo[:, k, :], start=False, stop=False)
                last = mm(acc[b][:, :], wlo[:, 0, ks], hhi[:, k, :], start=False, stop=(k == KT - 1))
            last.then_inc(s_acc_full, 1)
            pe.wait_ge(s_rows_in, 12 * 16)
            nc.tensor.transpose(M[1][:, 0:P], vrow[:, :], ident[:, :]).then_inc(s_vcol_mm, 1)
            pe.wait_ge(s_bias_src, 32)
            mm(M[3][0:A_HEADS, :], relb[0:N_BUCKETS + 1, :], hot[:, 0:L], start=True, stop=True)\
                .then_inc(s_bias_mm, 1)
            mm(M[2][0:A_HEADS, 0:BW - L], relb[0:N_BUCKETS + 1, :], hot[:, L:BW], start=True, stop=True)\
                .then_inc(s_bias_mm, 1)
            pe.wait_ge(*moved(U_LR, 0))
            pe.wait_ge(s_wup_in, 32)
            def head_tiles(h, c, j):
                tile(U_HEAD, c, (1 + c // 2) % 2, j, 8, h)

            for i in range(8):
                if i == 4:
                    pe.wait_ge(s_unit_lo, U_HEAD + 1)
                    head_tiles(0, 0, 0)
                    head_tiles(0, 1, 1)
                if i == 1:
                    pe.wait_ge(s_vcol, 1)
                if i == 2:
                    pe.wait_ge(s_bias_row, 2)
                if i > 3:
                    pe.wait_ge(s_la, i - 3)
                mm(M[i % 4][:, :], wup[:, i // 4, (i % 4) * P:(i % 4 + 1) * P], lrT[:, :], start=True, stop=True)\
                    .then_inc(s_up_mm, 1)

            def gla_scores(g):
                for d in range(2):
                    pe.wait_ge(s_der, g * 6 + 3 * d + 3)
                    if d == 0:
                        pe.wait_ge(s_gfin, g * 2 + 1)
                        pe.wait_ge(s_la, 8)
                    for t in range(TT):
                        last = nc.tensor.transpose(M[d][:, t * P:(t + 1) * P], kd[:, d, t * P:(t + 1) * P], ident[:, :])
                    last.then_inc(s_kd_tr, 1)
                    for t in range(TT):
                        ts = slice(t * P, (t + 1) * P)
                        last = mm(M[2 + d][:, ts], ke[:, d, ts], qe[:, d, ts], start=True, stop=True)
                    last.then_inc(s_gsc, 1)

            def gla_kv(g):
                pe.wait_ge(s_kdT, g * 2 + 2)
                pe.wait_ge(s_gmask, g * 3 + 3)
                pe.wait_ge(*moved(U_HEAD, 4, 8, g))
                pe.wait_ge(*moved(U_HEAD, 5, 8, g))
                for s in range(NCH - 1):
                    for d in range(2):
                        n = s if d == 0 else NCH - 1 - s
                        rows = slice(n % 2 * CHUNK, (n % 2 + 1) * CHUNK)
                        if s >= 2:
                            pe.wait_ge(s_gst, g * 14 + 2 * (s - 2) + d + 1)
                        mm(M[2 * d + s % 2][:, 0:DV], kdT[rows, d, n // 2, :], gv[rows, n // 2, :],
                           start=True, stop=True).then_inc(s_kv, 1)

            def gla_out(g):
                pe.wait_ge(s_gst, g * 14 + 14)
                for j in range(2):
                    js = slice(j * P, (j + 1) * P)
                    for t in range(TT):
                        mm(M[j][:, t * P:(t + 1) * P], gv[:, t, js], ga_sc[:, t, :], start=(t == 0), stop=False,
                           skip_group_check=True)
                    for n in range(1, NCH):
                        mm(M[j][:, n * CHUNK:(n + 1) * CHUNK], st[:, 0, n - 1, js],
                           qe[:, 0, n * CHUNK:(n + 1) * CHUNK], start=False, stop=False, skip_group_check=True)
                    for n in range(NCH - 1):
                        last = mm(M[j][:, n * CHUNK:(n + 1) * CHUNK], st[:, 1, NCH - 2 - n, js],
                                  qe[:, 1, n * CHUNK:(n + 1) * CHUNK], start=False, stop=(n == NCH - 2),
                                  skip_group_check=True)
                    last.then_inc(s_go, 1)

            def gla_sum(g):
                pe.wait_ge(s_gsq_sum, g + 1)
                mm(M[2][:, :], mean_dv[:, :], ex[:, 0, :], start=True, stop=True).then_inc(s_gsum, 1)

            def head_values(h, c):
                b, _, free = TL(U_HEAD, 4 + c, 8, h)
                if later(free):
                    pe.wait_ge(s_acc_free[b], free)
                pe_values(b, 1, c, hhi, hlo)

            def head_iteration(h, gla):
                g = h - 1
                if gla:
                    pe.wait_ge(s_unit_lo, h * 4 + U_HEAD + 1)
                    head_tiles(h, 0, 0)
                    head_tiles(h, 1, 1)
                    gla_scores(g)
                pe.wait_ge(s_unit_lo, h * 4 + U_HEAD + 2)
                head_tiles(h, 2, 0)
                head_tiles(h, 3, 1)
                if gla:
                    gla_kv(g)
                pe.wait_ge(s_unit_lo, h * 4 + U_HEAD + 3)
                head_values(h, 0)
                if gla:
                    gla_out(g)
                head_values(h, 1)
                pe.wait_ge(s_unit_lo, h * 4 + U_HEAD + 4)
                head_tiles(h, 6, 0)
                if gla:
                    gla_sum(g)
                head_tiles(h, 7, 1)

            head_iteration(0, False)
            with pe.Fori(1, GLA_HEADS) as h:
                head_iteration(h, True)
            g = GLA_HEADS - 1
            units(U_C, 1)
            gla_scores(g)
            pe.wait_ge(s_unit_lo, U_C + 1 + 1)
            for j in range(2):
                tile(U_C, 2 + j, (U_C + 1) % 2, j)
            gla_kv(g)
            for m in range(2, 6):
                pe.wait_ge(s_unit_lo, U_C + m + 1)
                tile(U_C, 2 * m, (U_C + m) % 2, 0)
                if m == 2:
                    gla_out(g)
                tile(U_C, 2 * m + 1, (U_C + m) % 2, 1)
                if m == 2:
                    gla_sum(g)

            pe.wait_ge(s_unit_lo, U_POOL + 1)
            for gr_ in range(NG):
                pe.wait_ge(s_p_lo, gr_ + 1)
                for j in range(2):
                    b, _, free = TL(U_POOL, 2 * gr_ + j)
                    if later(free):
                        pe.wait_ge(s_acc_free[b], free)
                    ws = slice(gr_ * 2 * P + j * P, gr_ * 2 * P + (j + 1) * P)
                    mm(acc[b][:, :], whi[:, 1, ws], phi[:, gr_, :], start=True, stop=False)
                    mm(acc[b][:, :], whi[:, 1, ws], plo[:, gr_, :], start=False, stop=False)
                    mm(acc[b][:, :], wlo[:, 1, ws], phi[:, gr_, :], start=False, stop=True)\
                        .then_inc(s_acc_full, 1)
            units(U_BR, 4, ready=s_o_lo)
            pe.wait_ge(s_x_back, 16 * TT)
            pe.wait_ge(s_gfin, 2 * GLA_HEADS + 1)
            for m in range(4):
                for k in (2 * m, 2 * m + 1):
                    if k >= 4:
                        pe.wait_ge(s_x_res, k - 3)
                    for t in range(TT):
                        last = nc.tensor.transpose(M[k % 4][:, t * P:(t + 1) * P], xnat[:, t, k * P:(k + 1) * P],
                                                   ident[:, :])
                    last.then_inc(s_x_tr, 1)
                units(U_OUT + m, 1, mhi, mlo, ready=s_merge_lo if m == 0 else None)

            def ada_tile(n, slot):
                pe.wait_ge(s_ada_sum, n + 1)
                mm(M[2][:, ds(n, 1)], ada[:, slot, 0, :], one_col[:, :], start=True, stop=True,
                   skip_group_check=True).then_inc(s_ada_used, 1)

            norm_mean(0)

            def gate_up(i, j):
                pe.wait_ge(s_unit_lo, i * 2 + U_FIN + j + 1)
                tile(U_FIN, 2 * j, j, 0, 4, i)
                tile(U_FIN, 2 * j + 1, j, 1, 4, i)
                ada_tile(i * 2 + j, j)

            units(U_FIN, 1, ready=s_norm_lo, base=nth(1))
            ada_tile(0, 0)
            gate_up(0, 1)
            with pe.Fori(1, FT // 2) as i:
                for j in range(2):
                    gate_up(i, j)

            def ffn_out(i, j):
                half = FT // 2
                ks = slice(j % 2 * half, (j % 2 + 1) * half)
                pe.wait_ge(s_unit_lo, i * 4 + U_FOUT + j + 1)
                if j < 2:
                    pe.wait_ge(s_f_lo, (j + 1) * half)
                tile(U_FOUT, j, j % 2, 0, 4, i, nk=half, ncol=P, xh=ahi[:, ks, :], xl=alo[:, ks, :])

            for j in range(4):
                ffn_out(0, j)
            ada_tile(FT, 0)
            ada_tile(FT + 1, 1)
            with pe.Fori(1, 4) as i:
                for j in range(4):
                    ffn_out(i, j)

            norm_mean(1)

            def att_values(g):
                pe.wait_ge(s_a_out, g + 1)
                pe.wait_ge(*moved(U_ATT, 2, 4, g))
                for t in range(TT):
                    last = nc.tensor.transpose(M[3][:, t * P:(t + 1) * P], av[:, t * P:(t + 1) * P], ident[:, :])
                last.then_inc(s_av_tr, 1)

            def att_scores(g, a):
                pe.wait_ge(*moved(U_ATT, 0, 4, g))
                pe.wait_ge(*moved(U_ATT, 1, 4, g))
                r = slice(a * AE, (a + 1) * AE)
                for q in range(TT):
                    if a == 0 and q == 3:
                        pe.wait_ge(s_avt, g + 1)
                    if a == 1 and q < 3:
                        pe.wait_ge(s_apt, g * 8 + (4, 2, 3)[q])
                    mm(M[q][:, 0:(q + 1) * P], aq[r, q * P:(q + 1) * P], ak[r, 0:(q + 1) * P], start=True, stop=True)\
                        .then_inc(s_score, 1)

            def att_transposes(g, a):
                for q in range(TT):
                    pe.wait_ge(s_aprob, g * 8 + a * 4 + q + 1)
                    if q == 3:
                        pe.wait_ge(s_apt, g * 8 + a * 4 + 1)
                    for j in range(q + 1):
                        last = nc.tensor.transpose(M[q % 3][:, j * P:(j + 1) * P], apr[:, a, q, j * P:(j + 1) * P],
                                                   ident[:, :])
                    last.then_inc(s_a_tr, 1)

            def att_pv(g, a):
                pe.wait_ge(s_apt, g * 8 + a * 4 + 4)
                pe.wait_ge(s_logit, g * 8 + 8)
                r = slice(a * AE, (a + 1) * AE)
                for j in range(TT):
                    last = mm(M[3][r, j * P:L], avt[:, j, r], apt[:, j, j * P:L], start=(j == 0), stop=(j == TT - 1))
                last.then_inc(s_apv, 1)

            def att_iteration(i, with_units, attend):
                g = i - 1
                if with_units and attend:
                    pe.wait_ge(s_unit_lo, i * 2 + U_ATT + 1)
                    tile(U_ATT, 0, 0, 0, 4, i)
                if attend:
                    att_values(g)
                    att_scores(g, 0)
                if with_units and attend:
                    tile(U_ATT, 1, 0, 1, 4, i)
                if attend:
                    att_transposes(g, 0)
                    att_scores(g, 1)
                if with_units:
                    pe.wait_ge(s_unit_lo, i * 2 + U_ATT + 1 + 1)
                    tile(U_ATT, 2, 1, 0, 4, i)
                if attend:
                    att_pv(g, 0)
                    att_transposes(g, 1)
                if with_units:
                    tile(U_ATT, 3, 1, 1, 4, i)
                if attend:
                    att_pv(g, 1)

            units(U_ATT, 1, ready=s_norm_lo, base=nth(2))
            att_iteration(0, True, False)
            with pe.Fori(1, A_HEADS // 2) as i:
                att_iteration(i, True, True)
            att_iteration(A_HEADS // 2, False, True)

            def right_halves(t, lev):
                half = 1 << lev
                return t.rearrange("p (n c) -> p n c", c=2 * half)[:, :, half:]

            def hg_scores(g):
                if isinstance(g, int) and g == 0:
                    pe.wait_ge(s_a_out, A_HEADS // 2 + 1)
                pe.wait_ge(s_h_out, g + 1)
                pe.wait_ge(s_h_rs, g + 1)
                pe.wait_ge(*moved(U_HG, 2, 4, g))
                for t in range(TT):
                    last = nc.tensor.transpose(M[0][:, t * P:(t + 1) * P], hi_[:, t * P:(t + 1) * P], ident[:, :])
                last.then_inc(s_h_itr, 1)
                pe.wait_ge(s_h_op, g * 2 + 1)
                for t in range(TT):
                    last = nc.tensor.transpose(M[1][:, t * P:(t + 1) * P], hkd[:, t * P:(t + 1) * P], ident[:, :])
                last.then_inc(s_h_ktr, 1)
                for n in range(LEVELS + 1):
                    if n == 0:
                        pe.wait_ge(*moved(U_HG, 0, 4, g))
                    pe.wait_ge(s_h_w, g * 7 + max(n, 1))
                    if n == 2:
                        pe.wait_ge(s_h_cp, g * 2 + 1)
                    if n == 3:
                        pe.wait_ge(s_h_cp, g * 2 + 2)
                    if n >= 4:
                        pe.wait_ge(s_h_mask, g * 9 + n - 2)
                    for t in range(TT):
                        ts = slice(t * P, (t + 1) * P)
                        if n == 0:
                            last = mm(M[2][:, ts], hk[:, ts], hq[:, ts], start=True, stop=True)
                        else:
                            last = mm(right_halves(M[(n + 2) % 4][:, ts], n - 1), hw[:, n - 1, ts],
                                      right_halves(hw[:, n - 1, ts], n - 1), start=True, stop=True)
                    last.then_inc(s_h_score, 1)
                pe.wait_ge(s_h_mask, g * 9 + 7)
                for n in range(TT - 1):
                    last = mm(M[3][:, n * P:(n + 1) * P], hkT[:, n, :], hit[:, n, :], start=True, stop=True)
                last.then_inc(s_h_kv, 1)

            def hg_out(g):
                pe.wait_ge(s_h_mask, g * 9 + 9)
                pe.wait_ge(s_h_st, g * 3 + 3)
                pe.wait_ge(s_h_op, g * 2 + 2)
                for t in range(TT):
                    mm(M[2][:, t * P:(t + 1) * P], hit[:, t, :], hsc[:, t, :], start=(t == 0), stop=False,
                       skip_group_check=True)
                for t in range(1, TT):
                    last = mm(M[2][:, t * P:(t + 1) * P], hst[:, t - 1, :], hqe[:, t * P:(t + 1) * P], start=False,
                              stop=(t == TT - 1), skip_group_check=True)
                last.then_inc(s_h_o, 1)

            def hg_sum(g):
                pe.wait_ge(s_h_sq, g + 1)
                mm(M[3][:, :], mean_p[:, :], hsq[:, :], start=True, stop=True).then_inc(s_h_sum, 1)

            def hg_iteration(g, u0=None):
                if u0 is None:
                    u, base, h = (g + 1) * 2 + U_HG, U_HG, g + 1
                else:
                    u, base, h = u0, u0, 0
                pe.wait_ge(s_unit_lo, u + 1)
                tile(base, 0, 0, 0, 4, h)
                if later(g):
                    hg_sum(g - 1)
                tile(base, 1, 0, 1, 4, h)
                pe.wait_ge(s_unit_lo, u + 2)
                tile(base, 2, 1, 0, 4, h)
                hg_scores(g)
                tile(base, 3, 1, 1, 4, h)
                hg_out(g)

            units(U_HG, 2)
            hg_iteration(0)
            with pe.Fori(1, H_HEADS - 1) as g:
                hg_iteration(g)
            hg_iteration(H_HEADS - 1, U_G2)

            pe.wait_ge(s_unit_lo, U_G2 + 3)
            tile(U_G2, 4, 0, 0)
            hg_sum(H_HEADS - 1)
            tile(U_G2, 5, 0, 1)
            units(U_G2 + 3, 5)
            units(U_BA, 2, oahi, oalo, nk=AW // P, ncol=L, ready=s_oa_lo)
            units(U_BB, 4, ready=s_ob_lo)

            def y_transpose(k):
                pe.wait_ge(s_yT, k + 1)
                if k >= 3:
                    pe.wait_ge(s_y_nat, k - 2)
                for t in range(TT):
                    last = nc.tensor.transpose(M[k % 3][:, t * P:(t + 1) * P], yT[:, k, t * P:(t + 1) * P], ident[:, :])
                last.then_inc(s_y_tr, 1)

            units(U_OUT2, 2, nhi, nlo, ready=s_n_lo)
            pe.wait_ge(s_h_out, H_HEADS + 1)
            y_transpose(0)
            y_transpose(1)
            pe.wait_ge(s_unit_lo, U_OUT2 + 3)
            tile(U_OUT2, 4, 0, 0, xh=nhi, xl=nlo)
            y_transpose(2)
            tile(U_OUT2, 5, 0, 1, xh=nhi, xl=nlo)
            y_transpose(3)
            pe.wait_ge(s_unit_lo, U_OUT2 + 4)
            tile(U_OUT2, 6, 1, 0, xh=nhi, xl=nlo)
            y_transpose(4)
            y_transpose(5)
            tile(U_OUT2, 7, 1, 1, xh=nhi, xl=nlo)
            y_transpose(6)
            y_transpose(7)
            pe.wait_ge(s_norm_acc, nth(2) + KT)
            for t in range(TT):
                last = mm(M[3][:, t:t + 1], nacc[:, t * P:(t + 1) * P], mean_dm[:, 0:1], start=True, stop=True,
                          skip_group_check=True)
            last.then_inc(s_norm_sum, 1)


_INS = ["x", "norm_mix", "w_in", "w_decay_up_fwd", "b_decay_fwd", "w_decay_up_bwd", "b_decay_bwd", "gla_norm",
        "w_branch_gla", "w_pool_group", "pool_scale", "w_out", "norm_ffn", "w_ffn_in", "w_ffn_out", "norm_final",
        "c_2", "w_ada_2", "b_ada_2", "norm_g_2", "w_in_2", "hgrn_onorm_g_2", "w_branch_a_2", "w_branch_b_2",
        "w_out_2", "rel_bias_2", "hgrn_lb_2", "final_g_2"]


def kernel(**inputs):
    import numpy as _np
    import concourse.bacc as _bacc
    from concourse import mybir as _mybir
    from concourse.bass_utils import run_bass_kernel_spmd as _run

    nc = _bacc.Bacc("TRN2", target_bir_lowering=False, num_devices=1)
    arrays, aps = {}, {}
    for name, a in [(n, inputs[n]) for n in _INS] + list(shape_constants().items()):
        a = _np.ascontiguousarray(a)
        arrays[f"in_{name}_dram"] = a
        aps[name] = nc.dram_tensor(f"in_{name}_dram", a.shape, _mybir.dt.from_np(a.dtype), kind="ExternalInput").ap()
    y = nc.dram_tensor("out_0_dram", (1, L, DM), _mybir.dt.float32, kind="ExternalOutput").ap()
    build(nc, aps, y)
    r = _run(nc, [arrays], core_ids=[0])
    return r.results[0]["out_0_dram"]
```
